# Optimizing a Trainium2 kernel written in Bass

```python
import jax, jax.numpy as jnp
from jax import lax
import numpy as np
import math

D_MODEL = 1024
BATCH = 1
SEQ = 512
DEPTH = 2

CHUNK = 64
EPS = 1e-6
HEAD_DIM = 64
H_A = D_MODEL // (2 * HEAD_DIM)
A_PREV_CHUNKS = 8
MAX_REL_DIST = 256
H_B = D_MODEL // (2 * HEAD_DIM)
H_B_KV = H_B // 4
B_WINDOW = 128
B_PREV_CHUNKS = B_WINDOW // CHUNK
ATTN_PROJ = 3 * H_A * HEAD_DIM + H_B * HEAD_DIM + 2 * H_B_KV * HEAD_DIM
D_INNER = 2 * D_MODEL
SSM_HEAD_DIM = 64
SSM_HEADS = D_INNER // SSM_HEAD_DIM
SSM_GROUPS = 4
SSM_STATE = 128
SSM_CONV = 4
SSD_CHUNK = 64
SSM_CONV_CH = D_INNER + 2 * SSM_GROUPS * SSM_STATE
SSM_PROJ = D_INNER + SSM_CONV_CH + SSM_HEADS
D_FF = ((8 * D_MODEL // 3 + 127) // 128) * 128
FFN_CONV = 3


def rmsnorm(x, g):
    xf = x.astype(jnp.float32)
    y = xf * lax.rsqrt(jnp.mean(xf * xf, axis=-1, keepdims=True) + EPS)
    return (y * g.astype(jnp.float32)).astype(x.dtype)

def causal_dwconv(x, w, b):
    k = w.shape[0]
    y = lax.conv_general_dilated(
        x, w[:, None, :].astype(x.dtype), window_strides=(1,), padding=[(k - 1, 0)],
        dimension_numbers=("NWC", "WIO", "NWC"), feature_group_count=x.shape[-1])
    return y + b.astype(x.dtype)

def band_offsets(n_prev):
    band = (n_prev + 1) * CHUNK
    q_off = jnp.arange(CHUNK, dtype=jnp.int32)
    k_off = jnp.arange(band, dtype=jnp.int32) - n_prev * CHUNK
    return q_off[:, None] - k_off[None, :], k_off

def band_attention(q, k, v, n_prev, bias, sinks):
    b, s, hq, d = q.shape
    hkv = k.shape[2]
    grp = hq // hkv
    nc = s // CHUNK
    band = (n_prev + 1) * CHUNK
    pad = n_prev * CHUNK
    kp = jnp.pad(k, ((0, 0), (pad, 0), (0, 0), (0, 0)))
    vp = jnp.pad(v, ((0, 0), (pad, 0), (0, 0), (0, 0)))
    qc = jnp.moveaxis(q.reshape(b, nc, CHUNK, hkv, grp, d), 1, 0)
    _, k_off = band_offsets(n_prev)
    scale = d ** -0.5

    def one_chunk(args):
        c, qb = args
        start = c * CHUNK
        kb = lax.dynamic_slice_in_dim(kp, start, band, axis=1)
        vb = lax.dynamic_slice_in_dim(vp, start, band, axis=1)
        sc = jnp.einsum("bqkgd,bskd->bkgqs", qb, kb).astype(jnp.float32) * scale + bias
        valid = (start + k_off) >= 0
        sc = jnp.where(valid, sc, -jnp.inf)
        if sinks is None:
            p = jax.nn.softmax(sc, axis=-1)
        else:
            snk = sinks.astype(jnp.float32)[None, :, :, None, None]
            m = jnp.maximum(jnp.max(sc, axis=-1, keepdims=True), snk)
            e = jnp.exp(sc - m)
            p = e / (jnp.sum(e, axis=-1, keepdims=True) + jnp.exp(snk - m))
        return jnp.einsum("bkgqs,bskd->bqkgd", p.astype(vb.dtype), vb)

    out = lax.map(one_chunk, (jnp.arange(nc, dtype=jnp.int32), qc))
    return jnp.moveaxis(out, 0, 1).reshape(b, s, hq * d)

def attn_layer(h, w_in, w_out, relpos_table, q_norm_a, k_norm_a, q_norm_b, k_norm_b, sinks):
    b, s, _ = h.shape
    da, db, dkv = H_A * HEAD_DIM, H_B * HEAD_DIM, H_B_KV * HEAD_DIM
    cuts = [da, 2 * da, 3 * da, 3 * da + db, 3 * da + db + dkv]
    qa, ka, va, qb, kb, vb = jnp.split(h @ w_in, cuts, axis=-1)
    heads = lambda t, n: t.reshape(b, s, n, HEAD_DIM)
    qa = rmsnorm(heads(qa, H_A), q_norm_a)
    ka = rmsnorm(heads(ka, H_A), k_norm_a)
    rel_a, _ = band_offsets(A_PREV_CHUNKS)
    idx = jnp.clip(rel_a, -MAX_REL_DIST, MAX_REL_DIST) + MAX_REL_DIST
    bias_a = relpos_table.astype(jnp.float32)[:, idx][:, None]
    oa = band_attention(qa, ka, heads(va, H_A), A_PREV_CHUNKS, bias_a, None)
    qb = rmsnorm(heads(qb, H_B), q_norm_b)
    kb = rmsnorm(heads(kb, H_B_KV), k_norm_b)
    rel_b, _ = band_offsets(B_PREV_CHUNKS)
    slopes = 2.0 ** (-8.0 * jnp.arange(1, H_B + 1, dtype=jnp.float32) / H_B)
    bias_b = (-slopes[:, None, None] * jnp.abs(rel_b).astype(jnp.float32)).reshape(
        H_B_KV, H_B // H_B_KV, CHUNK, (B_PREV_CHUNKS + 1) * CHUNK)
    ob = band_attention(qb, kb, heads(vb, H_B_KV), B_PREV_CHUNKS, bias_b,
                        sinks.reshape(H_B_KV, H_B // H_B_KV))
    return jnp.concatenate([oa, ob], axis=-1) @ w_out

def ssd_scan(x, dt, a, bm, cm):
    b, s, h, p = x.shape
    g, n = bm.shape[2], bm.shape[3]
    r = h // g
    L = SSD_CHUNK
    nc = s // L

    def to_chunks(t):
        return jnp.moveaxis(t.reshape((b, nc, L) + t.shape[2:]), 1, 0)

    xc = to_chunks(x.reshape(b, s, g, r, p))
    dtc = to_chunks(dt.reshape(b, s, g, r))
    bc, cc = to_chunks(bm), to_chunks(cm)
    a = a.reshape(g, r)
    causal = jnp.tril(jnp.ones((L, L), dtype=bool))[None, :, :, None, None]

    def step(state, inp):
        xk, dtk, bk, ck = inp
        acs = jnp.cumsum(dtk * a, axis=1)
        seg = acs[:, :, None] - acs[:, None, :]
        decay = jnp.exp(jnp.where(causal, seg, -jnp.inf))
        cb = jnp.einsum("blgn,bsgn->bgls", ck, bk)
        y_intra = jnp.einsum("bgls,blsgr,bsgrp->blgrp", cb, decay, xk * dtk[..., None])
        y_state = jnp.einsum("blgn,bgrpn->blgrp", ck, state) * jnp.exp(acs)[..., None]
        last = acs[:, -1]
        w_in = jnp.exp(last[:, None] - acs) * dtk
        new_state = state * jnp.exp(last)[..., None, None] + jnp.einsum(
            "bsgn,bsgr,bsgrp->bgrpn", bk, w_in, xk)
        return new_state, y_intra + y_state

    state0 = jnp.zeros((b, g, r, p, n), jnp.float32)
    _, ys = lax.scan(step, state0, (xc, dtc, bc, cc))
    return jnp.moveaxis(ys, 0, 1).reshape(b, s, h, p)

def ssm_layer(h, w_in, conv_w, conv_b, dt_bias, a_log, d_skip, norm_w, w_out):
    b, s, _ = h.shape
    z, xbc, dt = jnp.split(h @ w_in, [D_INNER, D_INNER + SSM_CONV_CH], axis=-1)
    xbc = jax.nn.silu(causal_dwconv(xbc, conv_w, conv_b))
    xs, bm, cm = jnp.split(xbc, [D_INNER, D_INNER + SSM_GROUPS * SSM_STATE], axis=-1)
    xs = xs.reshape(b, s, SSM_HEADS, SSM_HEAD_DIM).astype(jnp.float32)
    bm = bm.reshape(b, s, SSM_GROUPS, SSM_STATE).astype(jnp.float32)
    cm = cm.reshape(b, s, SSM_GROUPS, SSM_STATE).astype(jnp.float32)
    dt = jax.nn.softplus(dt.astype(jnp.float32) + dt_bias.astype(jnp.float32))
    a = -jnp.exp(a_log.astype(jnp.float32))
    y = ssd_scan(xs, dt, a, bm, cm) + d_skip.astype(jnp.float32)[:, None] * xs
    y = y.reshape(b, s, D_INNER) * jax.nn.silu(z.astype(jnp.float32))
    yg = y.reshape(b, s, SSM_GROUPS, D_INNER // SSM_GROUPS)
    yg = yg * lax.rsqrt(jnp.mean(yg * yg, axis=-1, keepdims=True) + EPS)
    y = (yg.reshape(b, s, D_INNER) * norm_w.astype(jnp.float32)).astype(h.dtype)
    return y @ w_out

def conv_ffn(h, w_in, conv_w, conv_b, w_out):
    gate, up = jnp.split(h @ w_in, [D_FF], axis=-1)
    gate = causal_dwconv(gate, conv_w, conv_b)
    return (jax.nn.silu(gate) * up) @ w_out

def first_inputs(seed: int = 0) -> dict:
    key = jax.random.key(seed)
    ks = jax.random.split(key, 24)
    n_even, n_odd = (DEPTH + 1) // 2, DEPTH // 2
    nrm = lambda k, shape, scale: jax.random.normal(k, shape, jnp.float32) * scale
    dt0 = jnp.exp(jax.random.uniform(ks[15], (n_odd, SSM_HEADS), jnp.float32,
                                     np.log(1e-3), np.log(1e-1)))
    return {
        "x": nrm(ks[0], (BATCH, SEQ, D_MODEL), 1.0),
        "norm_mix": 1.0 + nrm(ks[1], (DEPTH, D_MODEL), 0.05),
        "norm_ffn": 1.0 + nrm(ks[2], (DEPTH, D_MODEL), 0.05),
        "attn_w_in": nrm(ks[3], (n_even, D_MODEL, ATTN_PROJ), D_MODEL ** -0.5),
        "attn_w_out": nrm(ks[4], (n_even, (H_A + H_B) * HEAD_DIM, D_MODEL), ((H_A + H_B) * HEAD_DIM) ** -0.5),
        "relpos_table": nrm(ks[5], (n_even, H_A, 2 * MAX_REL_DIST + 1), 0.2),
        "q_norm_a": 1.0 + nrm(ks[6], (n_even, HEAD_DIM), 0.05),
        "k_norm_a": 1.0 + nrm(ks[7], (n_even, HEAD_DIM), 0.05),
        "q_norm_b": 1.0 + nrm(ks[8], (n_even, HEAD_DIM), 0.05),
        "k_norm_b": 1.0 + nrm(ks[9], (n_even, HEAD_DIM), 0.05),
        "sinks": nrm(ks[10], (n_even, H_B), 0.5),
        "ssm_w_in": nrm(ks[11], (n_odd, D_MODEL, SSM_PROJ), D_MODEL ** -0.5),
        "ssm_conv_w": nrm(ks[12], (n_odd, SSM_CONV, SSM_CONV_CH), SSM_CONV ** -0.5),
        "ssm_conv_b": nrm(ks[13], (n_odd, SSM_CONV_CH), 0.02),
        "ssm_dt_bias": dt0 + jnp.log(-jnp.expm1(-dt0)),
        "ssm_a_log": jnp.log(jax.random.uniform(ks[14], (n_odd, SSM_HEADS), jnp.float32, 1.0, 16.0)),
        "ssm_d": 1.0 + nrm(ks[16], (n_odd, SSM_HEADS), 0.1),
        "ssm_norm": 1.0 + nrm(ks[17], (n_odd, D_INNER), 0.05),
        "ssm_w_out": nrm(ks[18], (n_odd, D_INNER, D_MODEL), D_INNER ** -0.5),
        "ffn_w_in": nrm(ks[19], (DEPTH, D_MODEL, 2 * D_FF), D_MODEL ** -0.5),
        "ffn_conv_w": nrm(ks[20], (DEPTH, FFN_CONV, D_FF), FFN_CONV ** -0.5),
        "ffn_conv_b": nrm(ks[21], (DEPTH, D_FF), 0.02),
        "ffn_w_out": nrm(ks[22], (DEPTH, D_FF, D_MODEL), D_FF ** -0.5),
    }

def first_block(x, norm_mix, norm_ffn, attn_w_in, attn_w_out, relpos_table, q_norm_a, k_norm_a,
              q_norm_b, k_norm_b, sinks, ssm_w_in, ssm_conv_w, ssm_conv_b, ssm_dt_bias, ssm_a_log,
              ssm_d, ssm_norm, ssm_w_out, ffn_w_in, ffn_conv_w, ffn_conv_b, ffn_w_out):
    for layer in range(DEPTH):
        i = layer // 2
        h = rmsnorm(x, norm_mix[layer])
        if layer % 2 == 0:
            mix = attn_layer(h, attn_w_in[i], attn_w_out[i], relpos_table[i], q_norm_a[i],
                             k_norm_a[i], q_norm_b[i], k_norm_b[i], sinks[i])
        else:
            mix = ssm_layer(h, ssm_w_in[i], ssm_conv_w[i], ssm_conv_b[i], ssm_dt_bias[i],
                            ssm_a_log[i], ssm_d[i], ssm_norm[i], ssm_w_out[i])
        x = x + mix
        h = rmsnorm(x, norm_ffn[layer])
        x = x + conv_ffn(h, ffn_w_in[layer], ffn_conv_w[layer], ffn_conv_b[layer], ffn_w_out[layer])
    return x


N_A_LAYERS = DEPTH // 2
N_B_LAYERS = DEPTH - N_A_LAYERS
CONV_WIDTH = 31
DIFF_HEADS = 8
DIFF_HEAD_DIM = 64
DIFF_V_DIM = 2 * DIFF_HEAD_DIM
ROT_DIM = DIFF_HEAD_DIM // 4
ROPE_THETA = 500000.0
Q_BLOCK = 128
MEM_TOKENS = 256
MEM_HEADS = 4
MEM_HEAD_DIM = D_MODEL // MEM_HEADS
FFN_HIDDEN = -(-(8 * D_MODEL) // (3 * 256)) * 256
RMS_EPS = 1e-6
LN_EPS = 1e-5
SUBLN_EPS = 1e-5


def rms_norm(x, g, eps=RMS_EPS):
    xf = x.astype(jnp.float32)
    y = xf * lax.rsqrt(jnp.mean(xf * xf, axis=-1, keepdims=True) + eps)
    return (y * g.astype(jnp.float32)).astype(x.dtype)

def layer_norm(x, g, b, eps=LN_EPS):
    xf = x.astype(jnp.float32)
    mu = jnp.mean(xf, axis=-1, keepdims=True)
    xc = xf - mu
    y = xc * lax.rsqrt(jnp.mean(xc * xc, axis=-1, keepdims=True) + eps)
    return (y * g.astype(jnp.float32) + b.astype(jnp.float32)).astype(x.dtype)

def rope_tables(positions):
    inv_freq = ROPE_THETA ** (-jnp.arange(0, ROT_DIM, 2, dtype=jnp.float32) / ROT_DIM)
    ang = positions.astype(jnp.float32)[..., None] * inv_freq
    return jnp.cos(ang), jnp.sin(ang)

def apply_partial_rope(t, cos, sin):
    half = ROT_DIM // 2
    tf = t.astype(jnp.float32)
    r1 = tf[..., :half]
    r2 = tf[..., half:ROT_DIM]
    c = cos[:, :, None, None, :]
    s = sin[:, :, None, None, :]
    out = jnp.concatenate([r1 * c - r2 * s, r1 * s + r2 * c, tf[..., ROT_DIM:]], axis=-1)
    return out.astype(t.dtype)

def conformer_conv(h, w_pw1, b_pw1, w_dw, b_dw, ln_g, ln_b, w_pw2, b_pw2):
    u = h @ w_pw1 + b_pw1
    a, gate = jnp.split(u, 2, axis=-1)
    u = a * jax.nn.sigmoid(gate)
    u = lax.conv_general_dilated(
        u, w_dw[:, None, :].astype(u.dtype), window_strides=(1,),
        padding=((CONV_WIDTH - 1, 0),),
        dimension_numbers=("NWC", "WIO", "NWC"),
        feature_group_count=D_MODEL) + b_dw
    u = jax.nn.silu(layer_norm(u, ln_g, ln_b))
    return u @ w_pw2 + b_pw2

def shared_kv(x, kv_norm, w_k, w_v, cos, sin):
    B, S, _ = x.shape
    h = rms_norm(x, kv_norm)
    k = apply_partial_rope((h @ w_k).reshape(B, S, DIFF_HEADS, 2, DIFF_HEAD_DIM), cos, sin)
    v = (h @ w_v).reshape(B, S, DIFF_HEADS, DIFF_V_DIM)
    return k, v

def diff_attention(h, k, v, cos, sin, w_q, lq1, lk1, lq2, lk2, subln_g, w_o, lambda_init):
    B, S, _ = h.shape
    q = apply_partial_rope((h @ w_q).reshape(B, S, DIFF_HEADS, 2, DIFF_HEAD_DIM), cos, sin)
    lam = (jnp.exp(jnp.sum(lq1.astype(jnp.float32) * lk1.astype(jnp.float32)))
           - jnp.exp(jnp.sum(lq2.astype(jnp.float32) * lk2.astype(jnp.float32)))
           + lambda_init)
    n_blocks = S // Q_BLOCK
    q_blocks = q.reshape(B, n_blocks, Q_BLOCK, DIFF_HEADS, 2, DIFF_HEAD_DIM).swapaxes(0, 1)
    k_pos = jnp.arange(S)
    scale = DIFF_HEAD_DIM ** -0.5

    def one_block(args):
        blk, qb = args
        q_pos = blk * Q_BLOCK + jnp.arange(Q_BLOCK)
        s = jnp.einsum('bqhcd,bkhcd->bhcqk', qb, k,
                       preferred_element_type=jnp.float32) * scale
        mask = k_pos[None, :] <= q_pos[:, None]
        p = jax.nn.softmax(jnp.where(mask, s, -jnp.inf), axis=-1)
        a = p[:, :, 0] - lam * p[:, :, 1]
        return jnp.einsum('bhqk,bkhe->bqhe', a.astype(v.dtype), v)

    o = lax.map(one_block, (jnp.arange(n_blocks), q_blocks))
    o = o.swapaxes(0, 1).reshape(B, S, DIFF_HEADS, DIFF_V_DIM)
    o = rms_norm(o, subln_g, SUBLN_EPS) * (1.0 - lambda_init)
    return o.reshape(B, S, DIFF_HEADS * DIFF_V_DIM) @ w_o

def memory_cross_attention(h, mem, w_q, w_k, w_v, w_o):
    B, S, _ = h.shape
    M = mem.shape[1]
    q = (h @ w_q).reshape(B, S, MEM_HEADS, MEM_HEAD_DIM)
    k = (mem @ w_k).reshape(B, M, MEM_HEADS, MEM_HEAD_DIM)
    v = (mem @ w_v).reshape(B, M, MEM_HEADS, MEM_HEAD_DIM)
    s = jnp.einsum('bshd,bmhd->bhsm', q, k, preferred_element_type=jnp.float32) * MEM_HEAD_DIM ** -0.5
    p = jax.nn.softmax(s, axis=-1)
    o = jnp.einsum('bhsm,bmhd->bshd', p.astype(v.dtype), v).reshape(B, S, D_MODEL)
    return o @ w_o

def swiglu(h, w_gate, w_up, w_down):
    return (jax.nn.silu(h @ w_gate) * (h @ w_up)) @ w_down

def second_inputs(seed: int = 0) -> dict:
    key = jax.random.key(seed)
    ks = iter(jax.random.split(key, 40))
    f32 = jnp.float32

    def w(shape, fan_in):
        return jax.random.normal(next(ks), shape, f32) * (fan_in ** -0.5)

    def gain(shape):
        return 1.0 + 0.02 * jax.random.normal(next(ks), shape, f32)

    def small(shape, scale=0.01):
        return scale * jax.random.normal(next(ks), shape, f32)

    D, F, A, Bn = D_MODEL, FFN_HIDDEN, N_A_LAYERS, N_B_LAYERS
    QK = DIFF_HEADS * 2 * DIFF_HEAD_DIM
    VW = DIFF_HEADS * DIFF_V_DIM
    x = jax.random.normal(next(ks), (BATCH, SEQ, D), f32)
    mem = jax.random.normal(next(ks), (BATCH, MEM_TOKENS, D), f32)
    offset = jax.random.randint(next(ks), (BATCH, 1), 0, 1024, dtype=jnp.int32)
    positions = (offset + jnp.arange(SEQ, dtype=jnp.int32)[None, :]).astype(jnp.int32)
    return {
        "x": x, "mem": mem, "positions": positions,
        "norm_mix": gain((DEPTH, D)), "norm_mem": gain((DEPTH, D)),
        "norm_ffn": gain((DEPTH, D)), "norm_final": gain((D,)),
        "conv_w_pw1": w((A, D, 2 * D), D), "conv_b_pw1": small((A, 2 * D)),
        "conv_w_dw": w((A, CONV_WIDTH, D), CONV_WIDTH), "conv_b_dw": small((A, D)),
        "conv_ln_g": gain((A, D)), "conv_ln_b": small((A, D)),
        "conv_w_pw2": w((A, D, D), D), "conv_b_pw2": small((A, D)),
        "kv_norm": gain((D,)), "w_k_shared": w((D, QK), D), "w_v_shared": w((D, VW), D),
        "diff_w_q": w((Bn, D, QK), D),
        "diff_lambda_q1": small((Bn, DIFF_HEAD_DIM), 0.1), "diff_lambda_k1": small((Bn, DIFF_HEAD_DIM), 0.1),
        "diff_lambda_q2": small((Bn, DIFF_HEAD_DIM), 0.1), "diff_lambda_k2": small((Bn, DIFF_HEAD_DIM), 0.1),
        "diff_subln_g": gain((Bn, DIFF_V_DIM)), "diff_w_o": w((Bn, VW, D), VW),
        "mem_w_q": w((DEPTH, D, D), D), "mem_w_k": w((DEPTH, D, D), D),
        "mem_w_v": w((DEPTH, D, D), D), "mem_w_o": w((DEPTH, D, D), D),
        "ffn_w_gate": w((DEPTH, D, F), D), "ffn_w_up": w((DEPTH, D, F), D),
        "ffn_w_down": w((DEPTH, F, D), F),
    }

def second_block(x, mem, positions, norm_mix, norm_mem, norm_ffn, norm_final,
              conv_w_pw1, conv_b_pw1, conv_w_dw, conv_b_dw, conv_ln_g, conv_ln_b,
              conv_w_pw2, conv_b_pw2, kv_norm, w_k_shared, w_v_shared,
              diff_w_q, diff_lambda_q1, diff_lambda_k1, diff_lambda_q2, diff_lambda_k2,
              diff_subln_g, diff_w_o, mem_w_q, mem_w_k, mem_w_v, mem_w_o,
              ffn_w_gate, ffn_w_up, ffn_w_down):
    cos, sin = rope_tables(positions)
    k_sh = None
    v_sh = None
    for i in range(DEPTH):
        if i < N_A_LAYERS:
            a = i
            h = rms_norm(x, norm_mix[i])
            x = x + conformer_conv(h, conv_w_pw1[a], conv_b_pw1[a], conv_w_dw[a], conv_b_dw[a],
                                   conv_ln_g[a], conv_ln_b[a], conv_w_pw2[a], conv_b_pw2[a])
        else:
            b = i - N_A_LAYERS
            if b == 0:
                k_sh, v_sh = shared_kv(x, kv_norm, w_k_shared, w_v_shared, cos, sin)
            lambda_init = 0.8 - 0.6 * math.exp(-0.3 * i)
            h = rms_norm(x, norm_mix[i])
            x = x + diff_attention(h, k_sh, v_sh, cos, sin, diff_w_q[b],
                                   diff_lambda_q1[b], diff_lambda_k1[b],
                                   diff_lambda_q2[b], diff_lambda_k2[b],
                                   diff_subln_g[b], diff_w_o[b], lambda_init)
        x = x + memory_cross_attention(rms_norm(x, norm_mem[i]), mem,
                                       mem_w_q[i], mem_w_k[i], mem_w_v[i], mem_w_o[i])
        x = x + swiglu(rms_norm(x, norm_ffn[i]), ffn_w_gate[i], ffn_w_up[i], ffn_w_down[i])
    return rms_norm(x, norm_final)


def setup_inputs(seed=0):
    out = dict(first_inputs(seed))
    for name, value in second_inputs(seed + 1).items():
        if name != "x":
            out[name + "_2"] = value
    return out


def reference(
    x, norm_mix, norm_ffn, attn_w_in, attn_w_out, relpos_table, q_norm_a, k_norm_a, q_norm_b,
    k_norm_b, sinks, ssm_w_in, ssm_conv_w, ssm_conv_b, ssm_dt_bias, ssm_a_log, ssm_d, ssm_norm,
    ssm_w_out, ffn_w_in, ffn_conv_w, ffn_conv_b, ffn_w_out, mem_2, positions_2, norm_mix_2,
    norm_mem_2, norm_ffn_2, norm_final_2, conv_w_pw1_2, conv_b_pw1_2, conv_w_dw_2, conv_b_dw_2,
    conv_ln_g_2, conv_ln_b_2, conv_w_pw2_2, conv_b_pw2_2, kv_norm_2, w_k_shared_2, w_v_shared_2,
    diff_w_q_2, diff_lambda_q1_2, diff_lambda_k1_2, diff_lambda_q2_2, diff_lambda_k2_2,
    diff_subln_g_2, diff_w_o_2, mem_w_q_2, mem_w_k_2, mem_w_v_2, mem_w_o_2, ffn_w_gate_2,
    ffn_w_up_2, ffn_w_down_2,
):
    x = first_block(
        x, norm_mix, norm_ffn, attn_w_in, attn_w_out, relpos_table, q_norm_a, k_norm_a,
        q_norm_b, k_norm_b, sinks, ssm_w_in, ssm_conv_w, ssm_conv_b, ssm_dt_bias, ssm_a_log,
        ssm_d, ssm_norm, ssm_w_out, ffn_w_in, ffn_conv_w, ffn_conv_b, ffn_w_out,
    )
    return second_block(
        x, mem_2, positions_2, norm_mix_2, norm_mem_2, norm_ffn_2, norm_final_2, conv_w_pw1_2,
        conv_b_pw1_2, conv_w_dw_2, conv_b_dw_2, conv_ln_g_2, conv_ln_b_2, conv_w_pw2_2,
        conv_b_pw2_2, kv_norm_2, w_k_shared_2, w_v_shared_2, diff_w_q_2, diff_lambda_q1_2,
        diff_lambda_k1_2, diff_lambda_q2_2, diff_lambda_k2_2, diff_subln_g_2, diff_w_o_2,
        mem_w_q_2, mem_w_k_2, mem_w_v_2, mem_w_o_2, ffn_w_gate_2, ffn_w_up_2, ffn_w_down_2,
    )


_drawn_inputs = setup_inputs


def setup_inputs(seed=0):
    import zlib

    import numpy as np

    out = dict(_drawn_inputs(seed))
    spreads = {}
    factors = {'q_norm_a': 7.153,
     'k_norm_a': 7.672,
     'q_norm_b': 5.0,
     'k_norm_b': 4.255,
     'ffn_conv_b': 3.245,
     'norm_mix_2': 5.823,
     'norm_mem_2': 8.0,
     'norm_ffn_2': 4.509,
     'norm_final_2': 25.63,
     'conv_b_pw1_2': 8.0,
     'conv_b_dw_2': 4.812,
     'conv_ln_g_2': 4.957,
     'conv_ln_b_2': 8.0,
     'conv_b_pw2_2': 5.491,
     'kv_norm_2': 6.828,
     'diff_lambda_q1_2': 3.634,
     'diff_lambda_k1_2': 7.067,
     'diff_lambda_k2_2': 7.846,
     'diff_subln_g_2': 170.124,
     'sinks': 64.0}
    for name, (base, spread) in spreads.items():
        noise = np.random.default_rng([zlib.crc32(name.encode()), seed]).standard_normal(out[name].shape)
        drawn = base * np.exp(spread * noise) if base else spread * noise
        out[name] = __import__('jax').numpy.asarray(drawn.astype(out[name].dtype))
    for name, factor in factors.items():
        out[name] = (out[name] * factor).astype(out[name].dtype)
    return out
```

```python
import math
from contextlib import ExitStack

import numpy as np

import concourse.bass as bass
from concourse import mybir

F32 = mybir.dt.float32
F32R = mybir.dt.float32r
BF16 = mybir.dt.bfloat16
I32 = mybir.dt.int32
ALU = mybir.AluOpType
ACT = mybir.ActivationFunctionType
AX_X = mybir.AxisListType.X
ds = bass.ds

P = 128
S = 512
D = 1024
KD = D // P
NT = S // P
DFF = 2816
KF = DFF // P
DIN = 2048
KI = DIN // P
NGRP = 4
NSTATE = 128
SSMH = 32
M = 256
CONVW = 31
RMS_EPS = 1e-6
LN_EPS = 1e-5
MASKED = -1e30
LAMBDA_INIT = 0.8 - 0.6 * math.exp(-0.3 * 1)

BANKS = 4
SLOTS = 4
SLAB = 8

STREAMS = [
    ("attn_in", 18, KD), ("attn_out", KD, KD),
    ("ffn_in0", 2 * KF, KD), ("ffn_out0", KD, KF),
    ("ssm_in", 41, KD), ("ssm_out", KD, KI),
    ("ffn_in1", 2 * KF, KD), ("ffn_out1", KD, KF),
    ("pw1", 2 * KD, KD), ("pw2", KD, KD),
    ("mem_kv0", 2 * KD, KD), ("mem_q0", KD, KD), ("mem_out0", KD, KD),
    ("glu_in0", 2 * KF, KD), ("glu_out0", KD, KF),
    ("diff_kv", 2 * KD, KD), ("diff_q", KD, KD), ("diff_out", KD, KD),
    ("mem_kv1", 2 * KD, KD), ("mem_q1", KD, KD), ("mem_out1", KD, KD),
    ("glu_in1", 2 * KF, KD), ("glu_out1", KD, KF),
]

COLUMNS = [
    ("norm_mix0", KD), ("norm_mix1", KD), ("norm_ffn0", KD), ("norm_ffn1", KD),
    ("g_qk", 13),
    ("ffn_w0", 3 * KF), ("ffn_w1", 3 * KF), ("ffn_b0", KF), ("ffn_b1", KF),
    ("ssm_cw", 4 * 24), ("ssm_cb", 24), ("ssm_d", KI), ("ssm_norm", KI), ("ssm_dtb", 1), ("ssm_alog", 1),
    ("norm_mix2_0", KD), ("norm_mix2_1", KD), ("norm_mem2_0", KD), ("norm_mem2_1", KD),
    ("norm_ffn2_0", KD), ("norm_ffn2_1", KD), ("norm_final", KD), ("kv_norm", KD),
    ("pw1_b", 2 * KD), ("dw_w", CONVW * KD), ("dw_b", KD), ("ln_g", KD), ("ln_b", KD), ("pw2_b", KD),
    ("subln", 1),
]
CONSTS = [("masks", 3 * P), ("head_ones", P), ("alibi", 8 * 256)]
NCST = sum(n for _, n in CONSTS)
COL = {}
NCOL = 0
for _name, _n in COLUMNS:
    COL[_name] = NCOL
    NCOL += _n


class Stream:

    def __init__(self, name, chunks, kc, slab0, chunk0):
        self.name, self.chunks, self.kc = name, chunks, kc
        self.slab0, self.chunk0 = slab0, chunk0
        self.slabs = [min(SLAB, kc - k) for k in range(0, kc, SLAB)]
        self.per = len(self.slabs)


def plan(names):
    out, slab, chunk = {}, 0, 0
    for name, chunks, kc in STREAMS:
        if name not in names:
            continue
        st = Stream(name, chunks, kc, slab, chunk)
        out[name] = st
        slab += chunks * st.per
        chunk += chunks
    return out


def each(eng, n, body, peel=0, tail=0, start=0):
    first = start + peel
    turns = max(n - tail - first, 0) // 4
    for c in range(start, min(first, n)):
        body(c, c % 4, c // 4)
    if turns > 1:
        with eng.Fori(0, turns) as i:
            for j in range(4):
                body(first + 4 * i + j, j, i + first // 4)
    for c in range(first + (4 * turns if turns > 1 else 0), n):
        body(c, c % 4, c // 4)


def lagged(fin, last):
    def after(c, j):
        if j >= 1:
            fin(c - 1, j - 1)
        if j == 3 or (isinstance(c, int) and c == last):
            fin(c, j)
    return after


class Unit:

    def __init__(self, scores, nk, scale, sink=None, rel=None):
        self.scores, self.nk, self.scale, self.sink, self.rel = scores, nk, scale, sink, rel


ALL = ("attn", "ffn0", "ssm", "ffn1", "conf", "mem0", "glu0", "diff", "mem1", "glu1", "final")
OF = {"attn": ("attn_in", "attn_out"), "ffn0": ("ffn_in0", "ffn_out0"), "ssm": ("ssm_in", "ssm_out"),
      "ffn1": ("ffn_in1", "ffn_out1"), "conf": ("pw1", "pw2"), "mem0": ("mem_kv0", "mem_q0", "mem_out0"),
      "glu0": ("glu_in0", "glu_out0"), "diff": ("diff_kv", "diff_q", "diff_out"),
      "mem1": ("mem_kv1", "mem_q1", "mem_out1"), "glu1": ("glu_in1", "glu_out1"), "final": ()}
GAIN = {"attn": "norm_mix0", "ffn0": "norm_ffn0", "ssm": "norm_mix1", "ffn1": "norm_ffn1", "conf": "norm_mix2_0",
        "mem0": "norm_mem2_0", "glu0": "norm_ffn2_0", "diff": "kv_norm", "mem1": "norm_mem2_1",
        "glu1": "norm_ffn2_1", "final": "norm_final"}


def build(nc, A, out, stages=ALL):
    ST = plan([n for s in stages for n in OF[s]])
    SLABS = sum(st.chunks * st.per for st in ST.values())
    nxt = {s: stages[i + 1] if i + 1 < len(stages) else None for i, s in enumerate(stages)}

    with ExitStack() as ctx:
        sems = {}

        def sem(name):
            if name not in sems:
                sems[name] = ctx.enter_context(nc.semaphore(name))
            return sems[name]

        base = (nc.sbuf_base + 63) // 64 * 64
        cursor = [base]
        high = [base]

        def sb(name, shape, dt=F32):
            t = nc.alloc_sbuf_tensor_at(name, [shape[0] if shape[0] > 1 else 1] + list(shape[1:]), dt, offset=cursor[0])
            n = int(np.prod(shape[1:])) * (2 if dt == BF16 else 4)
            cursor[0] += (n + 31) // 32 * 32
            high[0] = max(high[0], cursor[0])
            assert cursor[0] <= nc.sbuf_usable_end, (name, cursor[0] - nc.sbuf_usable_end)
            return t

        xt = sb("xt", [P, KD, S])
        w_raw = sb("w_raw", [P, SLOTS, SLAB * P])
        w_hi = sb("w_hi", [P, SLOTS, SLAB * P], F32R)
        w_lo = sb("w_lo", [P, SLOTS, SLAB * P], F32R)
        cols = sb("cols", [P, NCOL])
        ident = sb("ident", [P, P])
        ones = sb("ones", [P, P])
        ident_b = sb("ident_b", [P, P], BF16)
        masks_b = sb("masks_b", [P, 3, P], BF16)
        eps = sb("eps", [P, 2])
        rstd = sb("rstd", [P, S])
        acc = sb("acc", [P, S])
        sq = sb("sq", [P, 2, S])
        root = sq[:, 0, :]
        x_start = cursor[0]
        xh = sb("xh", [P, KD, S], F32R)
        xl = sb("xl", [P, KD, S], F32R)
        arena = cursor[0]

        hh = sb("hh", [P, KF, S], F32R)
        hl = sb("hl", [P, KF, S], F32R)
        f_g = sb("f_g", [P, S + 2])
        f_y = sb("f_y", [P, S])
        f_u = sb("f_u", [P, S])
        f_h = sb("f_h", [P, S])

        cursor[0] = arena
        oh = sb("oh", [P, KD, S], F32R)
        ol = sb("ol", [P, KD, S], F32R)
        a_prob_t = sb("a_prob_t", [P, 4, S])
        a_pt_t = sb("a_pt_t", [P, 2, S])
        a_stat = sb("a_stat", [P, 5, 64])
        v_tmp = a_prob_t[:, 0:2, :]
        q_root_t = a_prob_t[:, 2:4, :]
        a_common = cursor[0]
        qk = sb("qk", [P, 13, S])
        v_tok = sb("v_tok", [P, NT, 640])
        alibi_b = sb("alibi_b", [P, 8, 256], BF16)
        head_ones = sb("head_ones", [P, P])
        sink_c = sb("sink_c", [P, 8])
        flip = sb("flip", [P, P])
        rel = sb("rel", [P, 2, 640])
        cursor[0] = arena
        rel_row = sb("rel_row", [8, 767])
        cst = sb("cst", [P, NCST])
        rel_dram = nc.dram_tensor("rel_table", [8, 767], F32)

        cursor[0] = a_common
        m_q = sb("m_q", [P, KD, S])
        m_k = sb("m_k", [P, KD, M])
        m_v = sb("m_v", [P, M // P, D])
        m_hi = sb("m_hi", [P, KD, M], F32R)
        m_lo = sb("m_lo", [P, KD, M], F32R)
        m_in = m_q[:, 0:KD // 2, :].rearrange("p (a) (b n) -> p (a b) n", b=2)

        cursor[0] = a_common
        d_q = sb("d_q", [P, KD, S])
        d_k = sb("d_k", [P, KD, S])
        d_v = sb("d_v", [P, NT, D])
        cosine = sb("cosine", [P, S])
        sine = sb("sine", [P, S])
        rot = sb("rot", [P, P])
        freq = sb("freq", [P, 1])
        lam_v = d_q[:, 0, 0:256].rearrange("p (a n) -> p a n", a=4)
        lam_t = d_q[:, 1, 0:128].rearrange("p (a n) -> p a n", a=2)
        lam_e = sb("lam_e", [P, 4])
        pos_i = d_v[:, 0, 0:S].bitcast(I32)
        d_t = d_v[:, 1:3, 0:S]

        cursor[0] = a_common
        CPE = 7
        c_u = sb("c_u", [P, 2, CONVW - 1 + S])
        c_y = sb("c_y", [P, KD, S])
        c_diag = sb("c_diag", [P, 2, CPE, P])
        c_mean = sb("c_mean", [P, S])
        c_a = sb("c_a", [P, S])
        c_g = sb("c_g", [P, S])
        c_s = sb("c_s", [P, 2, S])

        cursor[0] = arena
        s_z = sb("s_z", [P, KI, S])
        s_xbc = sb("s_xbc", [P, 24, S])
        s_acs = sb("s_acs", [32, S])
        s_tok = sb("s_tok", [P, 3, NT, SSMH])
        s_el = sb("s_el", [P, NT, SSMH])
        s_ea = sb("s_ea", [P, 2, S])
        s_cb = sb("s_cb", [P, 2, NT, P])
        s_pad = s_cb[:, :, :, :].rearrange("p a b n -> p (a b n)")[:, 0:S + 3]
        cursor[0] = arena
        s_dt = sb("s_dt", [32, 8, S])
        cursor[0] = arena
        yh = sb("yh", [P, KI, S], F32R)
        cursor[0] += 8 * S * 4
        yl = sb("yl", [P, KI, S], F32R)
        cursor[0] = x_start
        s_xt = sb("s_xt", [P, 2, NT, S])
        s_xw = sb("s_xw", [P, NT - 1, S])
        s_st = sb("s_st", [P, NT - 1, S])
        s_dk = sb("s_dk", [P, 2, S])

        bank = [ctx.enter_context(nc.psum_tensor(f"bank{i}", [P, 512], F32)) for i in range(8)]
        NORM_BANK = bank[7]

        def col(name, c=0):
            return cols[:, ds(COL[name] + c, 1)] if not isinstance(c, int) else cols[:, COL[name] + c:COL[name] + c + 1]

        w_landed = [sem(f"w_landed{i}") for i in range(SLOTS)]
        w_split = sem("w_split")
        w_half = sem("w_half")
        w_used = sem("w_used")
        chunk_done = sem("chunk_done")
        bank_free = sem("bank_free")
        const_in = sem("const_in")
        x_in = sem("x_in")
        init_done = sem("init_done")
        x_new, x_sq, x_hi, x_lo, x_acc = (sem(n) for n in ("x_new", "x_sq", "x_hi", "x_lo", "x_acc"))
        acc_zero = sem("acc_zero")
        nrm_sum, nrm_root, nrm_ready = (sem(n) for n in ("nrm_sum", "nrm_root", "nrm_ready"))
        dve_step = sem("dve_step")
        f_gate, f_tap, f_conv, f_silu, f_prod, f_hi, f_lo, f_up = (
            sem(n) for n in ("f_gate", "f_tap", "f_conv", "f_silu", "f_prod", "f_hi", "f_lo", "f_up"))
        out_ready, out_done = sem("out_ready"), sem("out_done")

        q_sq, q_sum, q_root, q_rec, q_ready = (sem(n) for n in ("q_sq", "q_sum", "q_root", "q_rec", "q_ready"))
        v_new, v_turned, v_ready = (sem(n) for n in ("v_new", "v_turned", "v_ready"))
        a_score, a_max, a_exp, a_prob, a_turn, a_pt, a_pv, a_oh, a_ol = (
            sem(n) for n in ("a_score", "a_max", "a_exp", "a_prob", "a_turn", "a_pt", "a_pv", "a_oh", "a_ol"))
        cst_in, cst_ready, rel_in, rel_ready, rel_out = (
            sem(n) for n in ("cst_in", "cst_ready", "rel_in", "rel_ready", "rel_out"))
        sink_in, flip_done = sem("sink_in"), sem("flip_done")
        rel_buf = [sem("rel_buf0"), sem("rel_buf1")]

        def attn_units():
            units, turns, groups = [], [], []
            for pair in range(8):
                first = len(units)
                for half in range(2):
                    lo, hi = 64 * half, 64 * half + 64
                    for t in range(NT):
                        if pair < 4:
                            h, kc, nk, k0 = 2 * pair + half, 4 + pair, P * (t + 1), 0
                            vcol = h * 64
                            bias = [(flip[:], rel[:, h % 2, 512 - P * t:640], 0, nk),
                                    (ident_b[:], masks_b[:, 0, :], nk - P, P)]
                        else:
                            h, kc = 4 * half + pair - 4, 12
                            nk, k0 = (P, 0) if t == 0 else (2 * P, P * (t - 1))
                            vcol = 512 + 64 * half
                            bias = [(ident_b[:], alibi_b[:, h, 256 - nk:256], 0, nk)]
                        qc = pair if pair < 4 else 8 + pair - 4
                        scores = [(qk[lo:hi, qc, t * P:(t + 1) * P], qk[lo:hi, kc, k0:k0 + nk], 0, nk)] + bias
                        u = Unit(scores, nk, 0.125, None if pair < 4 else sink_c[:, h:h + 1],
                                 h if pair < 4 else None)
                        u.pv = [(v_tok[:, k0 // P + kt, vcol:vcol + 64], kt, pair, lo, hi, t)
                                for kt in range(nk // P)]
                        units.append(u)
                groups.append((first, len(units), [pair]))
            return units, groups
        UNITS = {"attn": attn_units()}

        def mem_units():
            units, groups = [], []
            for h in range(KD // 2):
                first = len(units)
                for t in range(NT):
                    scores = [(m_q[:, 2 * h + k, t * P:(t + 1) * P], m_k[:, 2 * h + k, :], 0, M) for k in range(2)]
                    u = Unit(scores, M, 0.0625)
                    u.pv = [(m_v[:, kt, (2 * h + d) * P:(2 * h + d + 1) * P], kt, 2 * h + d, 0, P, t)
                            for d in range(2) for kt in range(M // P)]
                    units.append(u)
                groups.append((first, len(units), [2 * h, 2 * h + 1]))
            return units, groups
        UNITS["mem"] = mem_units()

        def diff_units():
            units, groups = [], []
            for h in range(KD):
                first = len(units)
                for t in range(NT):
                    nk = P * (t + 1)
                    for comp in range(2):
                        lo, hi = 64 * comp, 64 * comp + 64
                        u = Unit([(d_q[lo:hi, h, t * P:(t + 1) * P], d_k[lo:hi, h, 0:nk], 0, nk),
                                  (ident_b[:], masks_b[:, 1, :], nk - P, P)], nk, 0.125)
                        u.pv = [(d_v[:, kt, h * P:(h + 1) * P], kt, h, 0, P, t) for kt in range(t + 1)]
                        units.append(u)
                groups.append((first, len(units), [h]))
            return units, groups
        UNITS["diff"] = diff_units()
        m_landed, m_half, m_split = sem("m_landed"), sem("m_half"), sem("m_split")
        r_rot, r_t, r_c, r_done = sem("r_rot"), sem("r_t"), sem("r_c"), sem("r_done")
        y_hi, y_lo = sem("y_hi"), sem("y_lo")
        tab_in, tab_pos, tab_red, tab_sin, tab_done = (sem(n) for n in ("tab_in", "tab_pos", "tab_red", "tab_sin", "tab_done"))
        lam_in, lam_sum, lam_exp = sem("lam_in"), sem("lam_sum"), sem("lam_exp")
        o_raw, o_sq, o_sum, o_root, o_new = (sem(n) for n in ("o_raw", "o_sq", "o_sum", "o_root", "o_new"))
        c_gate, c_sig, c_new, c_dia, c_pe, c_step, c_out = (
            sem(n) for n in ("c_gate", "c_sig", "c_new", "c_dia", "c_pe", "c_step", "c_out"))
        c_msum, c_mrow, c_cent, c_csq, c_cacc, c_norm, c_silu = (
            sem(n) for n in ("c_msum", "c_mrow", "c_cent", "c_csq", "c_cacc", "c_norm", "c_silu"))
        s_tap, s_conv, s_xbc_done, s_v, s_e, s_tp, s_tokd, s_eld = (
            sem(n) for n in ("s_tap", "s_conv", "s_xbc_done", "s_v", "s_e", "s_tp", "s_tokd", "s_eld"))
        s_turn, s_copied, s_cbp, s_cbd, s_xw_d, s_xd_d, s_u, s_state = (
            sem(n) for n in ("s_turn", "s_copied", "s_cbp", "s_cbd", "s_xw_d", "s_xd_d", "s_u", "s_state"))
        s_bc, s_exp, s_mask, s_dec, s_cp, s_m, s_y, s_yb, s_yz, s_sq, s_sum, s_root, s_yn = (
            sem(n) for n in ("s_bc", "s_exp", "s_mask", "s_dec", "s_cp", "s_m", "s_y", "s_yb", "s_yz", "s_sq", "s_sum",
                             "s_root", "s_yn"))
        s_yh, s_yl, s_e0, s_zd = sem("s_yh"), sem("s_yl"), sem("s_e0"), sem("s_zd")
        block = ctx.enter_context(nc.Block())

        @block.sync
        def _(sp):
            def load_stream(st):
                w = A["w_" + st.name]

                def turn(i, chunks):
                    for j in range(chunks):
                        k = 0
                        for t, nb in enumerate(st.slabs):
                            o = j * st.per + t
                            slot = (st.slab0 + o) % SLOTS
                            sp.wait_ge(w_split, st.slab0 + o + 1 + i * 4 * st.per)
                            src = w[ds(4 * i + j, 1), :, k * P:(k + nb) * P] if not isinstance(i, int) \
                                else w[4 * i + j:4 * i + j + 1, :, k * P:(k + nb) * P]
                            sp.dma_start(w_raw[:, slot, 0:nb * P], src.rearrange("a p n -> (a p) n")) \
                                .then_inc(w_landed[slot], 16)
                            k += nb

                turns = st.chunks // 4
                with sp.Fori(0, turns) as i:
                    turn(i, 4)
                if st.chunks % 4:
                    turn(turns, st.chunks % 4)

            for st in ST.values():
                load_stream(st)

        @block.gpsimd
        def _(pool):
            pool.memset(ident[:], 0.0).then_inc(init_done, 1)
            pool.memset(ones[:], 1.0).then_inc(init_done, 1)
            pool.memset(eps[:, 0:1], RMS_EPS).then_inc(init_done, 1)
            pool.memset(eps[:, 1:2], LN_EPS).then_inc(init_done, 1)
            pool.wait_ge(init_done, 4)
            pool.affine_select(out=ident[:], in_=ident[:], compare_op=ALU.not_equal, fill=1.0, base=0,
                               pattern=[[-1, P]], channel_multiplier=1).then_inc(init_done, 1)
            if "attn" in stages:
                pool.memset(flip[:], 0.0).then_inc(flip_done, 1)
                pool.wait_ge(flip_done, 1)
                pool.affine_select(out=flip[:], in_=flip[:], compare_op=ALU.not_equal, fill=1.0, base=1 - P,
                                   pattern=[[1, P]], channel_multiplier=1).then_inc(flip_done, 1)

            def split_stream(st, first=None):
                def turn(i, chunks, between=None):
                    for j in range(chunks):
                        for t, nb in enumerate(st.slabs):
                            o = j * st.per + t
                            if between is not None and o == SLOTS:
                                between()
                            s = st.slab0 + o
                            slot = s % SLOTS
                            n = slice(0, nb * P)
                            pool.wait_ge(w_half, s + 1 + i * 4 * st.per)
                            pool.tensor_tensor(w_lo[:, slot, n], w_raw[:, slot, n], w_hi[:, slot, n].bitcast(F32),
                                               ALU.subtract).then_inc(w_split, 1)

                turns = st.chunks // 4
                if first is not None:
                    turn(0, 4, first)
                with pool.Fori(0 if first is None else 1, turns) as i:
                    turn(i, 4)
                if st.chunks % 4:
                    turn(turns, st.chunks % 4)

            def by_head(t, g, n):
                return t[:, 0:n, 8 * g:8 * g + 8].unsqueeze(3).broadcast_to([P, n, 8, 64])

            def ssm_weights():
                pool.wait_ge(s_tokd, 2)
                for g in range(NGRP):
                    x = s_xt[:, g % 2, :, :].rearrange("p a (h d) -> p a h d", d=64)
                    xw = s_xw[:].rearrange("p a (h d) -> p a h d", d=64)
                    pool.wait_ge(s_copied, 5 * g + 4)
                    if g:
                        pool.wait_ge(s_u, g)
                    pool.tensor_tensor(xw, x[:, 0:NT - 1], by_head(s_tok[:, 2], g, NT - 1), ALU.mult).then_inc(s_xw_d, 1)
                    pool.wait_ge(s_xw_d, g + 1)
                    pool.tensor_tensor(x, x, by_head(s_tok[:, 0], g, NT), ALU.mult).then_inc(s_xd_d, 1)

            for st in ST.values():
                split_stream(st, ssm_weights if st.name == "ssm_out" else None)

        @block.tensor
        def _(pe):
            nrm = [0]
            xs = [0]
            fs = [0]

            def gemm(st, hi, lo, n, ready, after=None, peel=0, tail=0, start=0, stop=None, after_i=None):
                def chunk(c, j, i):
                    b = bank[(st.chunk0 + j) % BANKS][:, 0:n]
                    pe.wait_ge(bank_free, st.chunk0 + c + 1)
                    k = 0
                    for t, nb in enumerate(st.slabs):
                        slot = (st.slab0 + j * st.per + t) % SLOTS
                        pe.wait_ge(w_split, SLOTS + st.slab0 + c * st.per + t + 1)
                        for q in range(nb):
                            if j == 0:
                                ready(k)
                            wh = w_hi[:, slot, q * P:(q + 1) * P]
                            wl = w_lo[:, slot, q * P:(q + 1) * P]
                            last = k == st.kc - 1
                            pe.matmul(b, wh, hi[:, k, 0:n], start=(k == 0), stop=False)
                            pe.matmul(b, wh, lo[:, k, 0:n], start=False, stop=False)
                            mm = pe.matmul(b, wl, hi[:, k, 0:n], start=False, stop=last)
                            k += 1
                        mm.then_inc(w_used, 1)
                    if after is not None:
                        after(c, j)
                    if after_i is not None:
                        after_i(c, j, i)

                each(pe, stop or st.chunks, chunk, peel, tail, start)

            def v_turn(src, v, new, n, bnk):
                pe.wait_ge(bank_free, new)
                pe.wait_ge(v_ready, v + 1)
                for t in range(n // P):
                    mm = pe.transpose(bnk[:, t * P:(t + 1) * P], src[:, t * P:(t + 1) * P], ident[:])
                mm.then_inc(v_turned, 1)

            def attention(units, groups, peers=1, out=None):
                U = len(units)
                u0, t0, g0, p0 = au[0], at[0], ag[0], ap[0]
                group_of = {first: (g, chunks) for g, (first, _, chunks) in enumerate(groups)}
                nch = len(groups[0][2])
                ends = {last: g for g, (_, last, _) in enumerate(groups)}
                for st_ in range(U + 3 if out is None else U + 6):
                    if out is not None and st_ - 5 in ends:
                        out(ends[st_ - 5])
                    if st_ < U:
                        u = units[st_]
                        b = bank[st_ % 3]
                        if st_ >= 3:
                            pe.wait_ge(a_exp, u0 + st_ - 2)
                        if u.rel is not None and st_ % NT == 0:
                            pe.wait_ge(rel_buf[u.rel % 2], 16 * (u.rel // 2 + 1))
                        for n, (l, r, c0, w) in enumerate(u.scores):
                            mm = pe.matmul(b[:, c0:c0 + w], l, r, start=(n == 0), stop=(n == len(u.scores) - 1),
                                           skip_group_check=True)
                        mm.then_inc(a_score, 1)
                    r = st_ - 2
                    if 0 <= r < U and (r + 1) % peers == 0:
                        u, k = units[r], r // peers
                        src = a_prob_t[:, (r - peers + 1) % 4, :]
                        pe.wait_ge(a_prob, t0 + k + 1)
                        if k >= 2:
                            pe.wait_ge(a_pt, t0 + k - 1)
                        for kt in range(u.nk // P):
                            mm = pe.transpose(bank[3 + k % 2][:, kt * P:(kt + 1) * P], src[:, kt * P:(kt + 1) * P],
                                              ident[:])
                        mm.then_inc(a_turn, 1)
                    r = st_ - 3
                    if 0 <= r < U and (r + 1) % peers == 0:
                        u, k = units[r], r // peers
                        pe.wait_ge(a_pt, t0 + k + 1)
                        first = r - peers + 1
                        if first in group_of:
                            g, chunks = group_of[first]
                            held = g * nch + nch - 2
                            if held > 0:
                                pe.wait_ge(a_ol, g0 + held)
                        nk = u.nk // P
                        for v, kt, ch, lo, hi, t in u.pv:
                            mm = pe.matmul(bank[5 + ch % 2][lo:hi, t * P:(t + 1) * P], v,
                                           a_pt_t[:, k % 2, kt * P:(kt + 1) * P], start=(kt == 0),
                                           stop=(kt == nk - 1), skip_group_check=True)
                        mm.then_inc(a_pv, 1)
                au[0] += U
                at[0] += U // peers
                ag[0] += len(groups) * nch

            def attn():
                st = ST["attn_in"]

                def fin(c):
                    if isinstance(c, int) and c >= 13:
                        v_turn(v_tmp[:, c % 2, :], c - 13, BANKS + st.chunk0 + c + 1, S, bank[5 + c % 2])
                        return
                    pe.wait_ge(q_sq, c + 1)
                    if not isinstance(c, int) or c >= 2:
                        pe.wait_ge(q_root, c - 1)
                    pe.matmul(bank[5 + jj[0] % 2][:], head_ones[:], sq[:, jj[0] % 2, :], start=True, stop=True)\
                        .then_inc(q_sum, 1)
                jj = [0]

                def after(c, j):
                    first_sum(c, j)
                    if isinstance(c, int) and c == 0:
                        pe.wait_ge(cst_ready, 4)
                    if j >= 1:
                        jj[0] = j - 1
                        fin(c - 1)
                    if j == 3 or (isinstance(c, int) and c == 17):
                        jj[0] = j
                        fin(c)
                gemm(st, xh, xl, S, x_ready(KD * nrm[0]), after, peel=4, tail=6)
                pe.wait_ge(q_ready, 13)
                pe.wait_ge(flip_done, 2)
                pe.wait_ge(v_ready, 2 + 5)
                vt[0] = 5
                attention(*UNITS["attn"])
                gemm(ST["attn_out"], oh, ol, S, lambda k: pe.wait_ge(a_ol, k + 1))
            vt, au, at, ag, ap = [0], [0], [0], [0], [0]
            rc = [0]

            def mem(l):
                kv = ST[f"mem_kv{l}"]
                v0 = vt[0]

                def fin(c, j):
                    v_turn(v_tmp[:, j % 2, 0:M], v0 + c - KD, BANKS + kv.chunk0 + c + 1, M, bank[5 + j % 2])
                pe.wait_ge(m_split, l + 1)
                gemm(kv, m_hi, m_lo, M, lambda k: None, first_sum, peel=4, stop=KD)
                gemm(kv, m_hi, m_lo, M, lambda k: None, lagged(fin, 15), start=KD)
                vt[0] += KD
                gemm(ST[f"mem_q{l}"], xh, xl, S, x_ready(KD * (nrm[0] - 1)))
                pe.wait_ge(bank_free, BANKS + ST[f"mem_q{l}"].chunk0 + KD)
                pe.wait_ge(v_ready, 2 + vt[0])
                g0 = ag[0]
                attention(*UNITS["mem"])
                gemm(ST[f"mem_out{l}"], oh, ol, S, lambda k: pe.wait_ge(a_ol, g0 + k + 1))

            def diff():
                kv, q = ST["diff_kv"], ST["diff_q"]

                def turn_rope(st, src, r0):
                    def fin(c, j):
                        pe.wait_ge(bank_free, BANKS + st.chunk0 + c + 1)
                        pe.wait_ge(r_done, r0 + c + 1)
                        if r0:
                            pe.wait_ge(v_ready, 2 + vt[0])
                        pe.matmul(bank[5 + j % 2][:], rot[:], src[:, c, :] if isinstance(c, int) else
                                  src[:, ds(c, 1), :].rearrange("p a n -> p (a n)"), start=True, stop=True)\
                            .then_inc(r_rot, 1)
                    return fin
                v0 = vt[0]

                def fin_v(c, j):
                    v_turn(v_tmp[:, j % 2, :], v0 + c - KD, BANKS + kv.chunk0 + c + 1, S, bank[5 + j % 2])

                def after(c, j):
                    first_sum(c, j)
                    if isinstance(c, int) and c == 0:
                        pe.wait_ge(tab_done, 1)
                    lagged(turn_rope(kv, d_k, 0), 7)(c, j)
                gemm(kv, xh, xl, S, x_ready(KD * nrm[0]), after, peel=4, stop=KD)
                gemm(kv, xh, xl, S, lambda k: None, lagged(fin_v, 15), start=KD)
                vt[0] += KD
                gemm(q, xh, xl, S, lambda k: pe.wait_ge(y_lo, k + 1), lagged(turn_rope(q, d_q, KD), 7))
                pe.wait_ge(r_done, 2 + 2 * KD)
                pe.wait_ge(v_ready, 2 + vt[0])
                g0 = ag[0]

                def out(g):
                    pe.wait_ge(o_sq, g + 1)
                    pe.matmul(NORM_BANK[:], ones[:], sq[:, g % 2, :], start=True, stop=True).then_inc(o_sum, 1)
                attention(*UNITS["diff"], peers=2, out=out)
                gemm(ST["diff_out"], oh, ol, S, lambda k: pe.wait_ge(a_ol, g0 + k + 1))

            def conf():
                st = ST["pw1"]

                def conv(p, q):
                    pe.wait_ge(c_new, p + 1)
                    pe.wait_ge(c_dia, CPE * (p + 1))
                    pe.wait_ge(c_out, p + 1)
                    for n in range(CPE):
                        mm = pe.matmul(bank[5 + q][:], c_diag[:, q, n, :], c_u[:, q, n:n + S],
                                       start=(n == 0), stop=(n == CPE - 1))
                    mm.then_inc(c_pe, 1)

                def after_i(c, j, i):
                    first_sum(c, j)
                    if isinstance(c, int) and c < 2:
                        return
                    if j == 3:
                        conv(2 * i, 0)
                    elif j == 1:
                        conv(2 * i - 1, 1)
                gemm(st, xh, xl, S, x_ready(KD * nrm[0]), None, peel=4, after_i=after_i)
                conv(7, 1)
                pe.wait_ge(c_step, (CONVW - CPE + 1) * KD)
                pe.matmul(NORM_BANK[:], ones[:], acc[:], start=True, stop=True).then_inc(c_msum, 1)
                pe.wait_ge(c_cacc, KD)
                pe.matmul(NORM_BANK[:], ones[:], acc[:], start=True, stop=True).then_inc(c_msum, 1)
                gemm(ST["pw2"], oh, ol, S, lambda k: pe.wait_ge(a_ol, c_ol[0] + k + 1))
                ag[0] += KD
            c_ol = ag

            def ssm():
                st = ST["ssm_in"]
                acs_of = lambda c: slice(c * P, (c + 1) * P)

                def after(c, j):
                    first_sum(c, j)
                    if isinstance(c, int) and c == 3:
                        pe.wait_ge(s_v, 1)
                        for n, src in enumerate((s_dt[:, 0, :], s_acs[:], s_dt[:, 1, :])):
                            for t in range(NT):
                                pe.transpose(bank[4][:, (NT * n + t) * SSMH:(NT * n + t + 1) * SSMH], src[:, acs_of(t)],
                                             ident[0:32, 0:32])
                        pe.matmul(bank[4][:, 3 * P:4 * P], ones[0:32, :], s_dt[:, 2, 0:P], start=True, stop=True,
                                  skip_group_check=True).then_inc(s_tp, 1)
                gemm(st, xh, xl, S, x_ready(KD * nrm[0]), after, peel=4)
                pe.wait_ge(s_xbc_done, 24)

                def prepare(g, r):
                    if r < 4:
                        b = bank[5 + r % 2]
                        n = 5 * g + r
                        if r >= 2:
                            pe.wait_ge(s_copied, n - 1)
                        elif g:
                            pe.wait_ge(s_state, 3 * g)
                        for t in range(NT):
                            mm = pe.transpose(b[:, acs_of(t)], s_xbc[:, 8 + 4 * g + r, acs_of(t)], ident[:])
                        mm.then_inc(s_turn, 1)
                        return
                    if g:
                        pe.wait_ge(s_state, 3 * g)
                    for t in range(NT):
                        mm = pe.matmul(bank[4][:, acs_of(t)], s_xbc[:, g, acs_of(t)], s_xbc[:, 4 + g, acs_of(t)],
                                       start=True, stop=True, skip_group_check=True)
                    mm.then_inc(s_cbp, 1)
                    pe.wait_ge(s_copied, 5 * g + 3)
                    for t in range(NT):
                        mm = pe.transpose(bank[5][:, acs_of(t)], s_xbc[:, g, acs_of(t)], ident[:])
                    mm.then_inc(s_turn, 1)

                def inflow(g):
                    pe.wait_ge(s_copied, 5 * g + 5)
                    pe.wait_ge(s_cbd, g + 1)
                    pe.wait_ge(s_xw_d, g + 1)
                    for t in range(NT - 1):
                        mm = pe.matmul(bank[4 + t][:], s_xbc[:, g, acs_of(t)], s_xw[:, t, :], start=True, stop=True)
                    mm.then_inc(s_u, 1)

                pe.wait_ge(s_tokd, 2)
                pe.wait_ge(s_eld, 1)
                for r in range(5):
                    prepare(0, r)
                inflow(0)
                pe.wait_ge(bank_free, BANKS + st.chunk0 + st.chunks)
                for n in range(SSMH + 7):
                    if n < SSMH:
                        if n >= 2:
                            pe.wait_ge(s_dec, n - 1)
                        pe.matmul(bank[n % 2][:], ident[0:32, n:n + 1].broadcast_to([32, P]), s_acs[:],
                                  start=True, stop=False, skip_group_check=True).then_inc(s_bc, 1)
                    k = n - 1
                    if 0 <= k < SSMH:
                        pe.wait_ge(s_exp, k + 1)
                        pe.matmul(bank[k % 2][:], ident_b[:], masks_b[:, 2:3, :].broadcast_to([P, NT, P]),
                                  start=False, stop=True, skip_group_check=True).then_inc(s_mask, 1)
                    k = n - 2
                    if 0 <= k < SSMH:
                        g, f = k // 8, k // 2
                        lo = 64 * (k % 2)
                        y = bank[2 + f % 2][lo:lo + 64, :]
                        h = slice(k % 8 * 64, k % 8 * 64 + 64)
                        if k % 8 == 0:
                            pe.wait_ge(s_xd_d, g + 1)
                            pe.wait_ge(s_state, 3 * (g + 1))
                        if k % 2 == 0 and f >= 2:
                            pe.wait_ge(s_yb, f - 1)
                        pe.wait_ge(s_cp, k + 1)
                        pe.wait_ge(s_m, k + 1)
                        for t in range(NT):
                            mm = pe.matmul(y[:, acs_of(t)], s_xt[:, g % 2, t, h], s_dk[:, k % 2, acs_of(t)],
                                           start=True, stop=(t == 0), skip_group_check=True)
                            if t:
                                mm = pe.matmul(y[:, acs_of(t)], s_st[:, t - 1, h], s_ea[:, k % 2, acs_of(t)],
                                               start=False, stop=True, skip_group_check=True)
                        mm.then_inc(s_y, 1)
                    g, r = n // 8, n % 8 - 2
                    if g + 1 < NGRP and 0 <= r < 5:
                        prepare(g + 1, r)
                    if g + 1 < NGRP and r == 5:
                        inflow(g + 1)
                    f = n // 2 - 3
                    if n % 2 == 0 and 0 <= f < KI:
                        pe.wait_ge(s_sq, f + 1)
                        if f % 4 == 0 and f:
                            pe.wait_ge(s_root, f // 4)
                        pe.matmul(NORM_BANK[:], ones[:], sq[:, f % 2, :], start=(f % 4 == 0), stop=(f % 4 == 3),
                                  skip_group_check=True).then_inc(s_sum, 1)
                gemm(ST["ssm_out"], yh, yl, S, lambda k: pe.wait_ge(s_yl, k + 1))

            def x_ready(base):
                return lambda k: pe.wait_ge(x_lo, base + k + 1)

            def norm_sum():
                nrm[0] += 1
                pe.wait_ge(x_acc, KD * nrm[0])
                pe.matmul(NORM_BANK[:], ones[:], acc[:], start=True, stop=True).then_inc(nrm_sum, 1)

            def first_sum(c, j):
                if isinstance(c, int) and c == 0:
                    norm_sum()

            def ffn(si, so):
                gemm(ST[si], xh, xl, S, x_ready(KD * nrm[0]), first_sum, peel=4)
                f0 = fs[0]
                fs[0] += KF
                gemm(ST[so], hh, hl, S, lambda k: pe.wait_ge(f_lo, f0 + k + 1))

            pe.wait_ge(init_done, 5)
            for s in stages:
                if s == "attn":
                    attn()
                elif s.startswith("mem"):
                    mem(int(s[3]))
                elif s == "diff":
                    diff()
                elif s == "conf":
                    conf()
                elif s == "ssm":
                    ssm()
                elif s.startswith("ffn"):
                    ffn("ffn_in" + s[3], "ffn_out" + s[3])
                elif s.startswith("glu"):
                    ffn("glu_in" + s[3], "glu_out" + s[3])
                elif s == "final":
                    norm_sum()

        @block.vector
        def _(dve):
            nrm = [0]
            steps = [0]

            def new_x(s):
                return GAIN[s] if s else None

            def split_x(c, k, gain):
                dve.wait_ge(x_hi, k + 1)
                dve.scalar_tensor_tensor(xl_(c), xt_(c), col(gain, c), xh_(c).bitcast(F32),
                                         ALU.mult, ALU.subtract).then_inc(x_lo, 1)

            def add_square(k, j):
                dve.wait_ge(x_sq, k + 1)
                dve.wait_ge(x_acc, k)
                dve.tensor_tensor(acc[:], acc[:], sq[:, j % 2, :], ALU.add).then_inc(x_acc, 1)

            def zero_acc():
                dve.wait_ge(nrm_sum, nrm[0]) if nrm[0] else None
                dve.memset(acc[:], 0.0).then_inc(acc_zero, 1)
                dve.wait_ge(acc_zero, nrm[0] + 1)

            def norm_recip():
                nrm[0] += 1
                dve.wait_ge(nrm_root, nrm[0])
                dve.reciprocal(rstd[:], root).then_inc(nrm_ready, 1)
                dve.wait_ge(nrm_ready, nrm[0])

            def residual(st, gain, bias=None):
                zero_acc()
                k0 = KD * nrm[0]

                def chunk(c, j, i):
                    b = bank[(st.chunk0 + j) % BANKS]
                    dve.wait_ge(w_used, SLOTS + st.slab0 + (c + 1) * st.per)
                    if bias is None:
                        dve.tensor_tensor(xt_(c), b[:], xt_(c), ALU.add).then_inc(bank_free, 1)
                    else:
                        dve.scalar_tensor_tensor(xt_(c), b[:], col(bias, c), xt_(c), ALU.add, ALU.add).then_inc(bank_free, 1)
                    dve.wait_ge(bank_free, BANKS + st.chunk0 + c + 1)
                    add_square(k0 + c, j)
                    split_x(c, k0 + c, gain)
                each(dve, KD, chunk)

            def step(ins):
                ins.then_inc(dve_step, 1)
                steps[0] += 1
                dve.wait_ge(dve_step, steps[0])

            def attention(units, groups, peers=1, out=None, lam=None):
                U = len(units)
                u0, t0, g0 = au[0], at[0], ag[0]
                ends = {last: (g, chunks) for g, (_, last, chunks) in enumerate(groups)}
                nch = len(groups[0][2])
                for s_ in range(U + 5):
                    if s_ < U:
                        u, cs = units[s_], slice(s_, s_ + 1)
                        dve.wait_ge(a_score, u0 + s_ + 1)
                        step(dve.reduce_max(a_stat[:, 0, cs], bank[s_ % 3][:, 0:u.nk], AX_X))
                        if u.sink is None:
                            dve.tensor_scalar(a_stat[:, 1, cs], a_stat[:, 0, cs], -u.scale, None, ALU.mult)\
                                .then_inc(a_max, 1)
                        else:
                            step(dve.tensor_scalar(a_stat[:, 0, cs], a_stat[:, 0, cs], u.scale, u.sink,
                                                   ALU.mult, ALU.max))
                            dve.tensor_scalar(a_stat[:, 1, cs], a_stat[:, 0, cs], -1.0, None, ALU.mult)\
                                .then_inc(a_max, 1)
                    r = s_ - 1
                    if 0 <= r < U:
                        u, cs = units[r], slice(r, r + 1)
                        dve.wait_ge(a_exp, u0 + r + 1)
                        if u.sink is not None:
                            step(dve.tensor_tensor(a_stat[:, 2, cs], a_stat[:, 2, cs], a_stat[:, 3, cs], ALU.add))
                        step(dve.reciprocal(a_stat[:, 4, cs], a_stat[:, 2, cs]))
                        pr = a_prob_t[:, r % 4, 0:u.nk]
                        if peers == 1:
                            dve.tensor_scalar(pr, pr, a_stat[:, 4, cs], None, ALU.mult).then_inc(a_prob, 1)
                        elif r % 2 == 0:
                            step(dve.tensor_scalar(pr, pr, a_stat[:, 4, cs], None, ALU.mult))
                        else:
                            step(dve.tensor_scalar(a_stat[:, 4, cs], a_stat[:, 4, cs], lam, None, ALU.mult))
                            first = a_prob_t[:, (r - 1) % 4, 0:u.nk]
                            dve.scalar_tensor_tensor(first, pr, a_stat[:, 4, cs], first, ALU.mult, ALU.add)\
                                .then_inc(a_prob, 1)
                    if s_ - 3 in ends:
                        g, chunks = ends[s_ - 3]
                        for n, ch in enumerate(chunks):
                            if out is not None:
                                out(g, ch)
                                continue
                            dve.wait_ge(a_oh, g0 + g * nch + n + 1)
                            dve.tensor_tensor(ol[:, ch, :], bank[5 + ch % 2][:], oh[:, ch, :].bitcast(F32),
                                              ALU.subtract).then_inc(a_ol, 1)
                au[0] += U
                at[0] += U // peers
                ag[0] += len(groups) * nch
            au, at, ag = [0], [0], [0]
            vt = [0]

            def row(t, c):
                return t[:, c, :] if isinstance(c, int) else t[:, ds(c, 1), :].rearrange("p a n -> p (a n)")

            def value(st, c, j, v, n, scaled):
                dve.wait_ge(w_used, SLOTS + st.slab0 + c + 1)
                if not isinstance(v, int) or v >= 2:
                    dve.wait_ge(v_turned, v - 1)
                b = bank[(st.chunk0 + j) % BANKS][:, 0:n]
                if scaled:
                    dve.tensor_tensor(v_tmp[:, j % 2, 0:n], b, rstd[:], ALU.mult).then_inc(bank_free, 1)
                else:
                    dve.tensor_copy(v_tmp[:, j % 2, 0:n], b).then_inc(bank_free, 1)

            def mem(l, s):
                kv, q = ST[f"mem_kv{l}"], ST[f"mem_q{l}"]
                v0 = vt[0]
                dve.wait_ge(m_half, l + 1)
                dve.tensor_tensor(m_lo[:], m_in, m_hi[:].bitcast(F32), ALU.subtract).then_inc(m_split, 1)

                def key(c, j, i):
                    dve.wait_ge(w_used, SLOTS + kv.slab0 + c + 1)
                    dve.tensor_copy(row(m_k, c), bank[(kv.chunk0 + j) % BANKS][:, 0:M]).then_inc(bank_free, 1)
                each(dve, KD, key)
                each(dve, 2 * KD, lambda c, j, i: value(kv, c, j, v0 + c - KD, M, False), start=KD, peel=4)
                vt[0] += KD
                norm_recip()

                def query(c, j, i):
                    dve.wait_ge(w_used, SLOTS + q.slab0 + c + 1)
                    dve.tensor_tensor(row(m_q, c), bank[(q.chunk0 + j) % BANKS][:], rstd[:], ALU.mult)\
                        .then_inc(bank_free, 1)
                each(dve, KD, query)
                attention(*UNITS["mem"])
                residual(ST[f"mem_out{l}"], new_x(nxt[s]))

            def rope(st, dst, r0, c, j):
                b = bank[5 + j % 2]
                dve.wait_ge(r_rot, r0 + c + 1)
                dve.wait_ge(r_done, 2 + r0 + c)
                dve.tensor_tensor(c_rope[:], b[:], sine[:], ALU.mult).then_inc(r_t, 1)
                dve.tensor_tensor(row(dst, c), row(dst, c), cosine[:], ALU.mult).then_inc(r_c, 1)
                dve.wait_ge(r_c, r0 + c + 1)
                dve.wait_ge(r_t, r0 + c + 1)
                dve.tensor_tensor(row(dst, c), row(dst, c), c_rope[:], ALU.add).then_inc(r_done, 1)
            c_rope = a_prob_t[:, 2, :]

            def diff(s):
                kv, q = ST["diff_kv"], ST["diff_q"]
                two_pi = 2.0 * math.pi
                c1 = 6.28125
                c2 = float(np.float32(np.round((two_pi - c1) * 2 ** 21) / 2 ** 21))
                c3 = float(np.float32(two_pi - c1 - c2))
                magic = 1.5 * 2 ** 23
                ang, turns = d_t[:, 0, :], d_t[:, 1, :]
                dve.wait_ge(tab_in, 48)
                step(dve.tensor_copy(ang, pos_i))
                step(dve.tensor_scalar(ang, ang, freq[:, 0:1], None, ALU.mult))
                step(dve.tensor_scalar(turns, ang, 1.0 / two_pi, magic, ALU.mult, ALU.add))
                step(dve.tensor_scalar(turns, turns, magic, None, ALU.subtract))
                for part in (c1, c2, c3):
                    step(dve.scalar_tensor_tensor(ang, turns, -part, ang, ALU.mult, ALU.add))
                dve.tensor_scalar(ang, ang, 3.1415925, -3.1415925, ALU.min, ALU.max).then_inc(tab_red, 1)
                dve.wait_ge(tab_sin, 2)
                step(dve.tensor_tensor(turns, turns, turns, ALU.mult))
                dve.tensor_scalar(cosine[:], turns, -2.0, 1.0, ALU.mult, ALU.add).then_inc(tab_done, 1)
                dve.wait_ge(lam_in, 16)
                step(dve.tensor_tensor(lam_t, lam_v[:, 0:4:2, :], lam_v[:, 1:4:2, :], ALU.mult))
                dve.tensor_reduce(lam_e[:, 0:2], lam_t, AX_X, ALU.add).then_inc(lam_sum, 1)
                dve.wait_ge(lam_exp, 1)
                step(dve.tensor_tensor(lam_e[:, 3:4], lam_e[:, 3:4], lam_e[:, 2:3], ALU.subtract))
                step(dve.tensor_scalar(lam_e[:, 3:4], lam_e[:, 3:4], -LAMBDA_INIT, None, ALU.add))
                norm_recip()

                def heads(st, dst, r0):
                    def chunk(c, j, i):
                        dve.wait_ge(w_used, SLOTS + st.slab0 + c + 1)
                        dve.tensor_tensor(row(dst, c), bank[(st.chunk0 + j) % BANKS][:], rstd[:], ALU.mult)\
                            .then_inc(bank_free, 1)
                        lagged(lambda c, j: rope(st, dst, r0, c, j), -1)(c, j)
                    return chunk
                v0 = vt[0]
                each(dve, KD, heads(kv, d_k, 0))
                each(dve, 2 * KD, lambda c, j, i: value(kv, c, j, v0 + c - KD, S, True), start=KD, peel=4)
                vt[0] += KD
                for c in range(KD):
                    dve.wait_ge(y_hi, c + 1)
                    dve.scalar_tensor_tensor(xl[:, c, :], xt[:, c, :], col("norm_mix2_1", c),
                                             xh[:, c, :].bitcast(F32), ALU.mult, ALU.subtract).then_inc(y_lo, 1)
                each(dve, KD, heads(q, d_q, KD))
                dve.wait_ge(r_done, 2 + 2 * KD)

                def out(g, ch):
                    o = d_q[:, g, :]
                    dve.wait_ge(a_pv, a_pv0 + NT * (g + 1))
                    dve.tensor_copy(o, bank[5 + ch % 2][:]).then_inc(o_raw, 1)
                    if g >= 1:
                        finish(g - 1)

                def finish(g):
                    o = d_q[:, g, :]
                    dve.wait_ge(o_root, g + 1)
                    step(dve.reciprocal(rstd[:], rstd[:]))
                    dve.scalar_tensor_tensor(o, o, col("subln"), rstd[:], ALU.mult, ALU.mult).then_inc(o_new, 1)
                    dve.wait_ge(o_new, g + 1)
                    dve.wait_ge(a_oh, g0 + g + 1)
                    dve.scalar_tensor_tensor(ol[:, g, :], o, 1.0 - LAMBDA_INIT, oh[:, g, :].bitcast(F32),
                                             ALU.mult, ALU.subtract).then_inc(a_ol, 1)
                a_pv0, g0 = at[0], ag[0]
                attention(*UNITS["diff"], peers=2, out=out, lam=lam_e[:, 3:4])
                finish(KD - 1)
                residual(ST["diff_out"], new_x(nxt[s]))

            def ssm(s):
                st = ST["ssm_in"]
                norm_recip()
                t = lambda n: s_dt[:, n, :]

                def softplus_and_sums():
                    dve.wait_ge(w_used, SLOTS + st.slab0 + 1)
                    dve.tensor_tensor(t(0), bank[st.chunk0 % BANKS][0:32, :], rstd[0:32, :], ALU.mult).then_inc(bank_free, 1)
                    dve.wait_ge(bank_free, BANKS + st.chunk0 + 1)
                    step(dve.tensor_scalar(t(0), t(0), col("ssm_dtb")[0:32], None, ALU.add))
                    dve.scalar_tensor_tensor(t(1), t(0), -1.0, t(0), ALU.mult, ALU.max).then_inc(s_e0, 1)
                    dve.wait_ge(s_e, 2)
                    step(dve.tensor_scalar(t(2), t(1), 2.0, None, ALU.add))
                    step(dve.reciprocal(t(2), t(2)))
                    step(dve.tensor_tensor(t(1), t(1), t(2), ALU.mult))
                    step(dve.tensor_tensor(t(2), t(1), t(1), ALU.mult))
                    step(dve.tensor_scalar(t(3), t(2), 1.0 / 15.0, None, ALU.mult))
                    for n in (13, 11, 9, 7, 5, 3):
                        step(dve.scalar_tensor_tensor(t(3), t(3), 1.0 / n, t(2), ALU.add, ALU.mult))
                    step(dve.scalar_tensor_tensor(t(3), t(3), 1.0, t(1), ALU.add, ALU.mult))
                    step(dve.tensor_scalar(t(0), t(0), 0.0, None, ALU.max))
                    step(dve.scalar_tensor_tensor(t(0), t(3), 2.0, t(0), ALU.mult, ALU.add))
                    dve.wait_ge(s_e, 2)
                    step(dve.tensor_scalar(t(4), t(0), t(5)[:, 0:1], -1.0, ALU.mult, ALU.mult))
                    for c in range(NT):
                        cs = slice(c * P, (c + 1) * P)
                        ins = dve.tensor_tensor_scan(s_acs[:, cs], ones[0:32, :], t(4)[:, cs], 0.0, ALU.mult, ALU.add)
                        step(ins)
                    last = s_acs[:].rearrange("p (a n) -> p a n", a=NT)[:, :, P - 1:P]
                    dve.tensor_tensor(t(2)[:, 0:P].rearrange("p (a n) -> p a n", a=NT),
                                      ident[0:32, 0:32].unsqueeze(1).broadcast_to([32, NT, 32]),
                                      last.broadcast_to([32, NT, 32]), ALU.mult).then_inc(s_e0, 1)
                    dve.wait_ge(s_e, 6)
                    dve.tensor_tensor(t(1), t(1), t(0), ALU.mult).then_inc(s_v, 1)

                def taps(c, j, i):
                    if isinstance(c, int) and c == 0:
                        return softplus_and_sums()
                    q = c - 1
                    y = s_ea[:, j % 2, :]
                    dve.wait_ge(w_used, SLOTS + st.slab0 + c + 1)
                    if not (isinstance(c, int) and c == 1):
                        dve.wait_ge(s_conv, 3 * q)
                    dve.tensor_tensor(s_pad[:, 3:S + 3], bank[(st.chunk0 + j) % BANKS][:], rstd[:], ALU.mult)\
                        .then_inc(bank_free, 1)
                    dve.wait_ge(s_tap, q + 1)
                    for n in range(3):
                        dve.scalar_tensor_tensor(y, s_pad[:, n:n + S], col("ssm_cw", 4 * q + n), y, ALU.mult, ALU.add)\
                            .then_inc(s_conv, 1)
                        if n < 2:
                            dve.wait_ge(s_conv, 3 * q + n + 1)

                def gate(c, j, i):
                    dve.wait_ge(w_used, SLOTS + st.slab0 + c + 1)
                    dve.tensor_tensor(row(s_z, c - 25), bank[(st.chunk0 + j) % BANKS][:], rstd[:], ALU.mult)\
                        .then_inc(bank_free, 1)
                step(dve.memset(s_pad[:, 0:3], 0.0))
                each(dve, 25, taps, peel=4)
                dve.wait_ge(s_tp, 1)
                dve.tensor_copy(s_tok[:].rearrange("p a b n -> p (a b n)"), bank[4][:, 0:3 * P]).then_inc(s_tokd, 1)
                dve.wait_ge(s_tokd, 1)
                dve.tensor_scalar(s_tok[:, 1, :, :], s_tok[:, 1, :, :], -1.0, None, ALU.mult).then_inc(s_tokd, 1)
                dve.wait_ge(s_tokd, 2)
                each(dve, 41, gate, start=25, peel=3)

                def products(g):
                    dve.wait_ge(s_cbp, g + 1)
                    dve.tensor_copy(s_cb[:, g % 2, :, :].rearrange("p a n -> p (a n)"), bank[4][:]).then_inc(s_cbd, 1)

                def states(g):
                    dve.wait_ge(s_u, g + 1)
                    if g:
                        dve.wait_ge(s_y, 8 * g)
                    for n in range(NT - 1):
                        if n == 0:
                            dve.tensor_copy(s_st[:, 0, :], bank[4][:]).then_inc(s_state, 1)
                            dve.wait_ge(s_state, 3 * g + 1)
                            continue
                        el = s_el[:, n, 8 * g:8 * g + 8].unsqueeze(2).broadcast_to([P, 8, 64])
                        step(dve.tensor_tensor(s_st[:, n, :].rearrange("p (h d) -> p h d", d=64),
                                               s_st[:, n - 1, :].rearrange("p (h d) -> p h d", d=64), el, ALU.mult))
                        dve.tensor_tensor(s_st[:, n, :], bank[4 + n][:], s_st[:, n, :], ALU.add).then_inc(s_state, 1)
                        dve.wait_ge(s_state, 3 * g + n + 1)

                dve.wait_ge(s_eld, 1)
                products(0)
                def low(f):
                    dve.wait_ge(s_yh, f + 1)
                    dve.wait_ge(s_yn, f + 1)
                    dve.tensor_tensor(yl[:, f, :], s_xbc[:, 8 + f, :], yh[:, f, :].bitcast(F32), ALU.subtract)\
                        .then_inc(s_yl, 1)

                for n in range(SSMH + 13):
                    if n < SSMH:
                        dve.wait_ge(s_exp, n + 1)
                        dve.tensor_tensor(s_ea[:, n % 2, :], s_xbc[:, 4 + n // 8, :], s_ea[:, n % 2, :], ALU.mult)\
                            .then_inc(s_cp, 1)
                    k = n - 1
                    if 0 <= k < SSMH:
                        dve.wait_ge(s_dec, k + 1)
                        if k % 8 == 0:
                            dve.wait_ge(s_cbd, k // 8 + 1)
                        dve.tensor_tensor(s_dk[:, k % 2, :], s_dk[:, k % 2, :],
                                          s_cb[:, k // 8 % 2, :, :].rearrange("p a n -> p (a n)"), ALU.mult)\
                            .then_inc(s_m, 1)
                    if n % 8 == 1 and n < SSMH:
                        states(n // 8)
                    f = n // 2 - 2
                    if n % 2 == 0 and 0 <= f < KI:
                        x = s_xbc[:, 8 + f, :]
                        dve.wait_ge(s_y, 2 * f + 2)
                        dve.scalar_tensor_tensor(x, x, col("ssm_d", f), bank[2 + f % 2][:], ALU.mult, ALU.add)\
                            .then_inc(s_yb, 1)
                        dve.wait_ge(s_yb, f + 1)
                        dve.tensor_tensor(x, x, s_z[:, f, :], ALU.mult).then_inc(s_yz, 1)
                    if n % 8 == 6 and n // 8 + 1 < NGRP:
                        products(n // 8 + 1)
                    g, q = (n - 13) // 8, (n - 13) % 8
                    if 0 <= g < NGRP:
                        if q == 0:
                            dve.wait_ge(s_root, g + 1)
                            step(dve.reciprocal(rstd[:], rstd[:]))
                            dve.wait_ge(s_yz, 4 * g + 4)
                        if q < 4:
                            f = 4 * g + q
                            dve.scalar_tensor_tensor(s_xbc[:, 8 + f, :], s_xbc[:, 8 + f, :], col("ssm_norm", f), rstd[:],
                                                     ALU.mult, ALU.mult).then_inc(s_yn, 1)
                        if 1 <= q < 5:
                            low(4 * g + q - 1)
                residual(ST["ssm_out"], new_x(nxt[s]))

            def conf(s):
                st = ST["pw1"]
                norm_recip()
                nst = CONVW - CPE
                for q in range(2):
                    step(dve.memset(c_u[:, q, 0:CONVW - 1], 0.0))
                step(dve.memset(acc[:], 0.0))

                def pair(p, q, j):
                    b0 = st.chunk0 + j
                    k0 = (nst + 1) * p
                    u, y = c_u[:, q, :], row(c_y, p)
                    dve.wait_ge(w_used, SLOTS + st.slab0 + 2 * p + 1)
                    dve.tensor_tensor(c_a[:], bank[b0 % BANKS][:], rstd[:], ALU.mult).then_inc(bank_free, 1)
                    dve.wait_ge(w_used, SLOTS + st.slab0 + 2 * p + 2)
                    dve.tensor_tensor(c_g[:], bank[(b0 + 1) % BANKS][:], rstd[:], ALU.mult).then_inc(bank_free, 1)
                    dve.wait_ge(c_sig, p + 1)
                    dve.scalar_tensor_tensor(u[:, CONVW - 1:], c_a[:], col("pw1_b", 2 * p), c_g[:], ALU.add, ALU.mult)\
                        .then_inc(c_new, 1)
                    dve.wait_ge(c_new, p + 1)
                    for n in range(nst):
                        tap = CPE + n
                        w = col("dw_w", CONVW * p + tap)
                        src = u[:, tap:tap + S]
                        if n == 0:
                            dve.tensor_scalar(y, src, w, col("dw_b", p), ALU.mult, ALU.add).then_inc(c_step, 1)
                        else:
                            dve.scalar_tensor_tensor(y, src, w, y, ALU.mult, ALU.add).then_inc(c_step, 1)
                        dve.wait_ge(c_step, k0 + n + 1)
                    dve.wait_ge(c_pe, p + 1)
                    dve.tensor_tensor(y, bank[5 + q][:], y, ALU.add).then_inc(c_out, 1)
                    dve.wait_ge(c_out, 2 + p + 1)
                    dve.tensor_tensor(acc[:], acc[:], y, ALU.add).then_inc(c_step, 1)
                    dve.wait_ge(c_step, k0 + nst + 1)

                with dve.Fori(0, KD // 2) as i:
                    pair(2 * i, 0, 0)
                    pair(2 * i + 1, 1, 2)
                dve.wait_ge(c_mrow, 1)
                step(dve.memset(acc[:], 0.0))
                for c in range(KD):
                    dve.tensor_tensor(c_y[:, c, :], c_y[:, c, :], c_mean[:], ALU.subtract).then_inc(c_cent, 1)
                    if c:
                        dve.wait_ge(c_csq, c)
                        dve.wait_ge(c_cacc, c - 1)
                        dve.tensor_tensor(acc[:], acc[:], sq[:, (c - 1) % 2, :], ALU.add).then_inc(c_cacc, 1)
                dve.wait_ge(c_csq, KD)
                dve.wait_ge(c_cacc, KD - 1)
                dve.tensor_tensor(acc[:], acc[:], sq[:, (KD - 1) % 2, :], ALU.add).then_inc(c_cacc, 1)
                dve.wait_ge(c_mrow, 2)
                step(dve.reciprocal(c_mean[:], c_mean[:]))

                def low(c):
                    dve.wait_ge(a_oh, ag[0] + c + 1)
                    dve.tensor_tensor(ol[:, c, :], c_s[:, c % 2, :], oh[:, c, :].bitcast(F32), ALU.subtract)\
                        .then_inc(a_ol, 1)
                for c in range(KD):
                    dve.tensor_tensor(c_y[:, c, :], c_y[:, c, :], c_mean[:], ALU.mult).then_inc(c_norm, 1)
                    if c:
                        low(c - 1)
                low(KD - 1)
                ag[0] += KD
                residual(ST["pw2"], new_x(nxt[s]), "pw2_b")

            def attn(s):
                st = ST["attn_in"]
                dve.wait_ge(rel_in, 16)
                step(dve.tensor_scalar(rel_row[:, 383:767], rel_row[:, 383:767], 8.0, None, ALU.mult))
                dve.tensor_copy(rel_row[:, 0:383], rel_row[:, 383:384].broadcast_to([8, 383])).then_inc(rel_ready, 1)
                norm_recip()

                def raw(c, j):
                    b = bank[(st.chunk0 + j) % BANKS]
                    dve.wait_ge(w_used, SLOTS + st.slab0 + c + 1)
                    if isinstance(c, int) and c >= 13:
                        if c >= 15:
                            dve.wait_ge(v_turned, c - 14)
                        dst = v_tmp[:, c % 2, :]
                    else:
                        dst = qk[:, ds(c, 1), :].rearrange("p a n -> p (a n)")
                    dve.tensor_tensor(dst, b[:], rstd[:], ALU.mult).then_inc(bank_free, 1)

                def fin(c, j):
                    if isinstance(c, int) and c >= 13:
                        return
                    rt = q_root_t[:, j % 2, :]
                    dve.wait_ge(q_root, c + 1)
                    dve.reciprocal(rt, rt).then_inc(q_rec, 1)
                    dve.wait_ge(q_rec, c + 1)
                    g = gq[c] if isinstance(c, int) else None
                    dst = qk[:, ds(c, 1), :].rearrange("p a n -> p (a n)")
                    dve.scalar_tensor_tensor(dst, dst, cols[:, ds(COL["g_qk"] + (c if not isinstance(c, int) else c), 1)],
                                             rt, ALU.mult, ALU.mult).then_inc(q_ready, 1)
                gq = list(range(13))

                def chunk(c, j, i):
                    raw(c, j)
                    if j >= 1:
                        fin(c - 1, j - 1)
                    if j == 3 or (isinstance(c, int) and c == 17):
                        fin(c, j)
                each(dve, 18, chunk, peel=4, tail=6)
                vt[0] += 5
                dve.wait_ge(q_ready, 13)
                attention(*UNITS["attn"])
                residual(ST["attn_out"], new_x(nxt[s]))

            def ffn(si, so, s, conv):
                norm_recip()
                st = ST[si]
                if conv:
                    dve.memset(f_g[:, 0:2], 0.0).then_inc(dve_step, 1)
                    steps[0] += 1
                    dve.wait_ge(dve_step, steps[0])
                f0 = ffns[0]
                ffns[0] += KF

                def pairs(i, jj):
                    p = i * 2 + jj
                    bg, bu = bank[(st.chunk0 + 2 * jj) % BANKS], bank[(st.chunk0 + 2 * jj + 1) % BANKS]
                    dve.wait_ge(w_used, SLOTS + st.slab0 + 2 * p + 1)
                    dve.tensor_tensor(f_g[:, 2:S + 2], bg[:], rstd[:], ALU.mult).then_inc(bank_free, 1)
                    if conv:
                        dve.wait_ge(f_tap, conv[3] * KF + p + 1)
                        dve.scalar_tensor_tensor(f_y[:], f_g[:, 1:S + 1], col(conv[0], 3 * p + 1), f_y[:],
                                                 ALU.mult, ALU.add).then_inc(f_conv, 1)
                        dve.wait_ge(f_conv, conv[3] * 2 * KF + 2 * p + 1)
                        dve.scalar_tensor_tensor(f_y[:], f_g[:, 0:S], col(conv[0], 3 * p), f_y[:],
                                                 ALU.mult, ALU.add).then_inc(f_conv, 1)
                    dve.wait_ge(w_used, SLOTS + st.slab0 + 2 * p + 2)
                    dve.tensor_tensor(f_u[:], bu[:], rstd[:], ALU.mult).then_inc(bank_free, 1)
                    dve.wait_ge(bank_free, BANKS + st.chunk0 + 2 * p + 2)
                    dve.wait_ge(f_silu, f0 + p + 1)
                    dve.tensor_tensor(f_h[:], f_y[:], f_u[:], ALU.mult).then_inc(f_prod, 1)
                    dve.wait_ge(f_hi, f0 + p + 1)
                    dve.tensor_tensor(hl[:, ds(p, 1), :].rearrange("p a n -> p (a n)"), f_h[:],
                                      hh[:, ds(p, 1), :].rearrange("p a n -> p (a n)").bitcast(F32),
                                      ALU.subtract).then_inc(f_lo, 1)

                with dve.Fori(0, KF // 2) as i:
                    for jj in range(2):
                        pairs(i, jj)
                residual(ST[so], new_x(nxt[s]))

            def xt_(c):
                return xt[:, ds(c, 1), :].rearrange("p a n -> p (a n)")

            def xh_(c):
                return xh[:, ds(c, 1), :].rearrange("p a n -> p (a n)")

            def xl_(c):
                return xl[:, ds(c, 1), :].rearrange("p a n -> p (a n)")

            ffns = [0]
            dve.sem_inc(bank_free, BANKS)
            dve.sem_inc(w_split, SLOTS)
            dve.sem_inc(w_used, SLOTS)
            dve.sem_inc(v_ready, 2)
            dve.sem_inc(r_done, 2)
            dve.sem_inc(c_out, 2)
            zero_acc()
            dve.wait_ge(init_done, 5)
            dve.tensor_copy(ident_b[:], ident[:]).then_inc(cst_ready, 1)
            if set(stages) & {"attn", "diff", "ssm"}:
                dve.wait_ge(cst_in, 16)
                dve.tensor_copy(masks_b[:], cst[:, 0:3 * P].rearrange("p (a n) -> p a n", a=3)).then_inc(cst_ready, 1)
                dve.tensor_copy(head_ones[:], cst[:, 3 * P:4 * P]).then_inc(cst_ready, 1)
                dve.tensor_copy(alibi_b[:], cst[:, 4 * P:].rearrange("p (a n) -> p a n", a=8)).then_inc(cst_ready, 1)
            dve.wait_ge(const_in, 16)

            def start_chunk(c, j, i):
                add_square(c, j)
                split_x(c, c, GAIN[stages[0]])
            each(dve, KD, start_chunk)
            nconv = 0
            for s in stages:
                if s == "attn":
                    attn(s)
                elif s.startswith("mem"):
                    mem(int(s[3]), s)
                elif s == "diff":
                    diff(s)
                elif s == "conf":
                    conf(s)
                elif s == "ssm":
                    ssm(s)
                elif s.startswith("ffn"):
                    ffn("ffn_in" + s[3], "ffn_out" + s[3], s, ("ffn_w" + s[3], "ffn_b" + s[3], None, nconv))
                    nconv += 1
                elif s.startswith("glu"):
                    ffn("glu_in" + s[3], "glu_out" + s[3], s, None)
                elif s == "final":
                    norm_recip()
                    for c in range(KD):
                        dve.scalar_tensor_tensor(xt[:, c, :], xt[:, c, :], col("norm_final", c), rstd[:],
                                                 ALU.mult, ALU.mult).then_inc(out_ready, 1)

        @block.scalar
        def _(act):
            nrm = [0]
            ffns = [0]
            nconv = [0]

            def xt_(c):
                return xt[:, ds(c, 1), :].rearrange("p a n -> p (a n)")

            def xh_(c):
                return xh[:, ds(c, 1), :].rearrange("p a n -> p (a n)")

            def prepare_x(ready, k0, gain):
                def chunk(c, j, i):
                    ready(c)
                    act.wait_ge(x_acc, k0 + c - 1) if (not isinstance(c, int) or k0 + c > 1) else None
                    act.activation(sq[:, j % 2, :], xt_(c), ACT.Square).then_inc(x_sq, 1)
                    act.activation(xh_(c), xt_(c), ACT.Copy, scale=col(gain, c)).then_inc(x_hi, 1)
                return chunk

            def half(s, slot, rounds):
                act.wait_ge(w_landed[slot], 16 * rounds)
                act.wait_ge(w_used, s + 1)
                act.activation(w_hi[:, slot, :], w_raw[:, slot, :], ACT.Copy).then_inc(w_half, 1)

            def next_half(st, j, i):
                for t in range(st.per):
                    o = st.slab0 + j * st.per + t + SLOTS
                    if isinstance(i, int) and o + 4 * st.per * i >= SLABS:
                        continue
                    half(o + 4 * st.per * i, o % SLOTS, o // SLOTS + 1 + i * st.per)

            def residual(st, gain):
                k0 = KD * nrm[0]

                def chunk(c, j, i):
                    act.wait_ge(bank_free, BANKS + st.chunk0 + c + 1)
                    next_half(st, j, i)
                    body(c, j, i)
                body = prepare_x(lambda c: None, k0, gain)
                each(act, KD, chunk, peel=KD if st.slab0 + st.chunks * st.per == SLABS else 0)

            def norm_root(k=None):
                nrm[0] += 1
                act.wait_ge(nrm_sum, nrm[0])
                act.activation(root, NORM_BANK[:], ACT.Sqrt, scale=1.0 / D, bias=eps[:, 0:1]).then_inc(nrm_root, 1)

            def attention(units, groups, peers=1, out=None, oh_lag=4):
                U = len(units)
                u0, t0, g0 = au[0], at[0], ag[0]
                ends = {last: (g, chunks) for g, (_, last, chunks) in enumerate(groups)}
                nch = len(groups[0][2])
                for s_ in range(U + 5):
                    if s_ < U:
                        u, cs = units[s_], slice(s_, s_ + 1)
                        act.wait_ge(a_max, u0 + s_ + 1)
                        if s_ >= 4:
                            act.wait_ge(a_turn, t0 + (s_ - 4) // peers + 1)
                        if u.sink is not None:
                            act.activation(a_stat[:, 3, cs], u.sink, ACT.Exp, bias=a_stat[:, 1, cs]).then_inc(a_aux, 1)
                        act.activation(a_prob_t[:, s_ % 4, 0:u.nk], bank[s_ % 3][:, 0:u.nk], ACT.Exp,
                                       bias=a_stat[:, 1, cs], scale=u.scale, accum_out=a_stat[:, 2, cs])\
                            .then_inc(a_exp, 1)
                        if u.rel is not None and s_ % NT == NT - 1 and u.rel + 2 < 8:
                            load_rel(u.rel + 2, u0 + s_ + 1)
                    r = s_ - 2
                    if 0 <= r < U and (r + 1) % peers == 0:
                        u, k = units[r], r // peers
                        act.wait_ge(a_turn, t0 + k + 1)
                        if k >= 2:
                            act.wait_ge(a_pv, t0 + k - 1)
                        act.activation(a_pt_t[:, k % 2, 0:u.nk], bank[3 + k % 2][:, 0:u.nk], ACT.Copy)\
                            .then_inc(a_pt, 1)
                    if s_ - 3 in ends:
                        g, chunks = ends[s_ - 3]
                        last = groups[g][1]
                        act.wait_ge(a_pv, t0 + last // peers)
                        for ch in chunks:
                            if out is not None:
                                out(g, ch)
                                continue
                            act.activation(oh[:, ch, :], bank[5 + ch % 2][:], ACT.Copy).then_inc(a_oh, 1)
                au[0] += U
                at[0] += U // peers
                ag[0] += len(groups) * nch
            au, at, ag = [0], [0], [0]
            a_aux = sem("a_aux")
            vt = [0]

            def row(t, c):
                return t[:, c, :] if isinstance(c, int) else t[:, ds(c, 1), :].rearrange("p a n -> p (a n)")

            def value(dst, v, vc, j, n):
                act.wait_ge(v_turned, v + 1)
                act.activation(dst[:, :, ds(vc * P, P)], bank[5 + j % 2][:, 0:n].rearrange("p (a n) -> p a n", n=P),
                               ACT.Copy).then_inc(v_ready, 1)

            def mem(l, s):
                kv, q = ST[f"mem_kv{l}"], ST[f"mem_q{l}"]
                v0 = vt[0]
                act.dma_start(m_in, A["memt"]).then_inc(m_landed, 16)
                act.wait_ge(m_landed, 16 * (l + 1))
                act.activation(m_hi[:], m_in, ACT.Copy).then_inc(m_half, 1)

                def key(c, j, i):
                    next_half(kv, j, i)
                    if isinstance(c, int) and c == 3:
                        norm_root()
                each(act, KD, key, peel=4)

                def chunk(c, j, i):
                    next_half(kv, j, i)
                    lagged(lambda c, j: value(m_v, v0 + c - KD, c - KD, j, M), 15)(c, j)
                each(act, 2 * KD, chunk, start=KD)
                vt[0] += KD
                each(act, KD, lambda c, j, i: next_half(q, j, i))
                attention(*UNITS["mem"])
                residual(ST[f"mem_out{l}"], GAIN[nxt[s]])

            def diff(s):
                kv, q = ST["diff_kv"], ST["diff_q"]
                ang, turns = d_t[:, 0, :], d_t[:, 1, :]
                act.dma_start(pos_i, A["pos"].broadcast_to([P, S])).then_inc(tab_in, 16)
                act.dma_start(freq[:], A["freq"]).then_inc(tab_in, 16)
                act.dma_start(rot[:], A["rot"]).then_inc(tab_in, 16)
                act.dma_start(d_q[:, 0, 0:256], A["lam"].broadcast_to([P, 256])).then_inc(lam_in, 16)
                act.wait_ge(tab_red, 1)
                act.activation(sine[:], ang, ACT.Sin).then_inc(tab_sin, 1)
                act.activation(turns, ang, ACT.Sin, scale=0.5).then_inc(tab_sin, 1)
                act.wait_ge(lam_sum, 1)
                act.activation(lam_e[:, 2:4], lam_e[:, 0:2], ACT.Exp).then_inc(lam_exp, 1)
                v0 = vt[0]

                def key(c, j, i):
                    next_half(kv, j, i)
                    if isinstance(c, int) and c == 0:
                        norm_root()
                each(act, KD, key, peel=4)

                def chunk(c, j, i):
                    next_half(kv, j, i)
                    lagged(lambda c, j: value(d_v, v0 + c - KD, c - KD, j, S), 15)(c, j)
                each(act, 2 * KD, chunk, start=KD)
                vt[0] += KD
                act.wait_ge(w_used, SLOTS + kv.slab0 + 2 * KD)
                for c in range(KD):
                    act.activation(xh[:, c, :], xt[:, c, :], ACT.Copy, scale=col("norm_mix2_1", c)).then_inc(y_hi, 1)
                each(act, KD, lambda c, j, i: next_half(q, j, i))

                def out(g, ch):
                    act.wait_ge(o_raw, g + 1)
                    act.activation(sq[:, g % 2, :], d_q[:, g, :], ACT.Square).then_inc(o_sq, 1)
                    if g >= 1:
                        upper(g - 1)
                    act.wait_ge(o_sum, g + 1)
                    act.activation(rstd[:], NORM_BANK[:], ACT.Sqrt, scale=1.0 / P, bias=eps[:, 1:2]).then_inc(o_root, 1)

                def upper(g):
                    act.wait_ge(o_new, g + 1)
                    act.activation(oh[:, g, :], d_q[:, g, :], ACT.Copy, scale=1.0 - LAMBDA_INIT)\
                        .then_inc(a_oh, 1)
                attention(*UNITS["diff"], peers=2, out=out)
                upper(KD - 1)
                residual(ST["diff_out"], GAIN[nxt[s]])

            def ssm(s):
                st = ST["ssm_in"]
                norm_root()
                t = lambda n: s_dt[:, n, :]
                act.activation(t(5)[:, 0:1], col("ssm_alog")[0:32], ACT.Exp).then_inc(s_e, 1)

                def taps(c, j, i):
                    act.wait_ge(bank_free, BANKS + st.chunk0 + c + 1)
                    next_half(st, j, i)
                    if isinstance(c, int) and c == 0:
                        act.wait_ge(s_e0, 1)
                        act.activation(t(1), t(1), ACT.Exp, scale=-1.0).then_inc(s_e, 1)
                        act.wait_ge(s_e0, 2)
                        for c in range(NT):
                            cs = slice(c * P, (c + 1) * P)
                            act.activation(t(1)[:, cs], s_acs[:, cs], ACT.Exp, scale=-1.0,
                                           bias=s_acs[:, (c + 1) * P - 1:(c + 1) * P]).then_inc(s_e, 1)
                        return
                    q = c - 1
                    y = s_ea[:, j % 2, :]
                    act.activation(y, s_pad[:, 3:S + 3], ACT.Identity, scale=col("ssm_cw", 4 * q + 3),
                                   bias=col("ssm_cb", q)).then_inc(s_tap, 1)
                    act.wait_ge(s_conv, 3 * q + 3)
                    act.activation(row(s_xbc, c - 1), y, ACT.Silu).then_inc(s_xbc_done, 1)

                def gate(c, j, i):
                    act.wait_ge(bank_free, BANKS + st.chunk0 + c + 1)
                    next_half(st, j, i)
                    z = row(s_z, c - 25)
                    act.activation(z, z, ACT.Silu).then_inc(s_zd, 1)
                each(act, 25, taps, peel=4)
                each(act, 41, gate, start=25, peel=3)
                act.wait_ge(s_tp, 1)
                act.activation(s_el[:].rearrange("p a n -> p (a n)"), bank[4][:, 3 * P:4 * P], ACT.Exp).then_inc(s_eld, 1)

                def copied(g, r):
                    act.wait_ge(s_turn, 5 * g + r + 1)
                    if r < 4:
                        if g >= 2 and r == 0:
                            act.wait_ge(s_y, 8 * (g - 1))
                        dst = s_xt[:, g % 2, :, r * P:(r + 1) * P]
                    else:
                        act.wait_ge(s_cbp, g + 1)
                        dst = s_xbc[:, g:g + 1, :].rearrange("p a (b n) -> p (a b) n", n=P)
                    act.activation(dst, bank[5 + r % 2][:].rearrange("p (a n) -> p a n", n=P), ACT.Copy)\
                        .then_inc(s_copied, 1)
                for r in range(5):
                    copied(0, r)
                for n in range(SSMH + 14):
                    if n < SSMH:
                        act.wait_ge(s_bc, n + 1)
                        if n >= 2:
                            act.wait_ge(s_y, n - 1)
                        act.activation(s_ea[:, n % 2, :], bank[n % 2][:], ACT.Exp).then_inc(s_exp, 1)
                    k = n - 1
                    if 0 <= k < SSMH:
                        act.wait_ge(s_mask, k + 1)
                        if k >= 2:
                            act.wait_ge(s_y, k - 1)
                        for t in range(NT):
                            cs = slice(t * P, (t + 1) * P)
                            ins = act.activation(s_dk[:, k % 2, cs], bank[k % 2][:, cs], ACT.Exp,
                                                 bias=s_tok[:, 1, t, k:k + 1])
                        ins.then_inc(s_dec, 1)
                    g, r = n // 8, n % 8 - 2
                    if g + 1 < NGRP and 0 <= r < 5:
                        copied(g + 1, r)
                    f = (n - 5) // 2
                    if n % 2 == 1 and 0 <= f < KI:
                        act.wait_ge(s_yz, f + 1)
                        if f >= 2:
                            act.wait_ge(s_sum, f - 1)
                        act.activation(sq[:, f % 2, :], s_xbc[:, 8 + f, :], ACT.Square).then_inc(s_sq, 1)
                    g, q = (n - 13) // 8, (n - 13) % 8
                    if 0 <= g < NGRP:
                        if q == 0:
                            act.wait_ge(s_sum, 4 * g + 4)
                            if g:
                                act.wait_ge(s_yn, 4 * g)
                            act.activation(rstd[:], NORM_BANK[:], ACT.Sqrt, scale=4.0 / DIN, bias=eps[:, 0:1])\
                                .then_inc(s_root, 1)
                        if q < 4:
                            f = 4 * g + q
                            act.wait_ge(s_yn, f + 1)
                            act.activation(yh[:, f, :], s_xbc[:, 8 + f, :], ACT.Copy).then_inc(s_yh, 1)
                residual(ST["ssm_out"], GAIN[nxt[s]])

            def conf(s):
                st = ST["pw1"]
                norm_root()

                def diag(p, q):
                    if not (isinstance(p, int) and p < 2):
                        act.wait_ge(c_pe, p - 1)
                    for n in range(CPE):
                        act.activation(c_diag[:, q, n, :], ident[:], ACT.Copy, scale=col("dw_w", CONVW * p + n))\
                            .then_inc(c_dia, 1)

                def pair(i, jj):
                    p = 2 * i + jj
                    next_half(st, 2 * jj, i)
                    diag(p, jj)
                    act.wait_ge(bank_free, BANKS + st.chunk0 + 2 * p + 2)
                    next_half(st, 2 * jj + 1, i)
                    act.activation(c_g[:], c_g[:], ACT.Sigmoid, bias=col("pw1_b", 2 * p + 1)).then_inc(c_sig, 1)
                pair(0, 0)
                pair(0, 1)
                with act.Fori(1, KD // 2) as i:
                    pair(i, 0)
                    pair(i, 1)
                act.wait_ge(c_msum, 1)
                act.activation(c_mean[:], NORM_BANK[:], ACT.Copy, scale=1.0 / D).then_inc(c_mrow, 1)
                for c in range(KD):
                    act.wait_ge(c_cent, c + 1)
                    if c >= 2:
                        act.wait_ge(c_cacc, c - 1)
                    act.activation(sq[:, c % 2, :], c_y[:, c, :], ACT.Square).then_inc(c_csq, 1)
                act.wait_ge(c_msum, 2)
                act.activation(c_mean[:], NORM_BANK[:], ACT.Sqrt, scale=1.0 / D, bias=eps[:, 1:2]).then_inc(c_mrow, 1)
                for c in range(KD):
                    act.wait_ge(c_norm, c + 1)
                    if c >= 2:
                        act.wait_ge(a_ol, ag[0] + c - 1)
                    act.activation(c_s[:, c % 2, :], c_y[:, c, :], ACT.Silu, scale=col("ln_g", c), bias=col("ln_b", c))\
                        .then_inc(c_silu, 1)
                    act.wait_ge(c_silu, c + 1)
                    act.activation(oh[:, c, :], c_s[:, c % 2, :], ACT.Copy).then_inc(a_oh, 1)
                ag[0] += KD
                residual(ST["pw2"], GAIN[nxt[s]])

            def load_rel(h, after):
                if after is not None:
                    act.wait_ge(a_score, after)
                src = bass.AP(rel_dram, h * 767, [[1, P], [1, 640]])
                act.dma_start(rel[:, h % 2, :], src).then_inc(rel_buf[h % 2], 16)

            def attn(s):
                st = ST["attn_in"]
                norm_root()
                act.wait_ge(rel_ready, 1)
                act.dma_start(rel_dram[:, :], rel_row[:]).then_inc(rel_out, 16)

                def fin(c, j):
                    if isinstance(c, int) and c >= 13:
                        v = c - 13
                        act.wait_ge(v_turned, v + 1)
                        dst = v_tok[:, :, 512:640] if v == 0 else v_tok[:, :, (v - 1) * P:v * P]
                        act.activation(dst, bank[5 + c % 2][:].rearrange("p (a n) -> p a n", a=NT), ACT.Copy)\
                            .then_inc(v_ready, 1)
                        return
                    act.wait_ge(q_sum, c + 1)
                    if not isinstance(c, int) or c >= 2:
                        act.wait_ge(q_ready, c - 1)
                    act.activation(q_root_t[:, j % 2, :], bank[5 + j % 2][:], ACT.Sqrt, scale=1.0 / 64,
                                   bias=eps[:, 0:1]).then_inc(q_root, 1)

                def chunk(c, j, i):
                    act.wait_ge(bank_free, BANKS + st.chunk0 + c + 1)
                    next_half(st, j, i)
                    if not (isinstance(c, int) and c >= 13):
                        if not isinstance(c, int) or c >= 2:
                            act.wait_ge(q_sum, c - 1)
                        act.activation(sq[:, j % 2, :], qk[:, ds(c, 1), :].rearrange("p a n -> p (a n)"),
                                       ACT.Square).then_inc(q_sq, 1)
                    if j >= 1:
                        fin(c - 1, j - 1)
                    if j == 3 or (isinstance(c, int) and c == 17):
                        fin(c, j)
                each(act, 18, chunk, peel=4, tail=6)
                vt[0] += 5
                act.wait_ge(rel_out, 16)
                act.wait_ge(sink_in, 16)
                load_rel(0, None)
                load_rel(1, None)
                attention(*UNITS["attn"])
                residual(ST["attn_out"], GAIN[nxt[s]])

            def ffn(si, so, s, conv):
                norm_root()
                f0 = ffns[0]
                ffns[0] += KF
                with act.Fori(0, KF // 2) as i:
                    for jj in range(2):
                        p = i * 2 + jj
                        act.wait_ge(bank_free, BANKS + ST[si].chunk0 + 2 * p + 1)
                        next_half(ST[si], 2 * jj, i)
                        if conv:
                            act.activation(f_y[:], f_g[:, 2:S + 2], ACT.Identity, bias=col(conv[1], p),
                                           scale=col(conv[0], 3 * p + 2)).then_inc(f_tap, 1)
                            act.wait_ge(f_conv, conv[3] * 2 * KF + 2 * p + 2)
                            act.activation(f_y[:], f_y[:], ACT.Silu).then_inc(f_silu, 1)
                        else:
                            act.activation(f_y[:], f_g[:, 2:S + 2], ACT.Silu).then_inc(f_silu, 1)
                        act.wait_ge(f_prod, f0 + p + 1)
                        act.activation(hh[:, ds(p, 1), :].rearrange("p a n -> p (a n)"), f_h[:], ACT.Copy)\
                            .then_inc(f_hi, 1)
                        next_half(ST[si], 2 * jj + 1, i)
                residual(ST[so], GAIN[nxt[s]])

            act.dma_start(cols[:], A["cols"]).then_inc(const_in, 16)
            if set(stages) & {"attn", "diff", "ssm"}:
                act.dma_start(cst[:], A["cst"]).then_inc(cst_in, 16)
            if "attn" in stages:
                act.dma_start(rel_row[:, 383:767], A["rel_rev"][:, 0:384]).then_inc(rel_in, 16)
                act.dma_start(sink_c[:], A["sinks"].rearrange("(a n) -> a n", a=1).broadcast_to([P, 8]))\
                    .then_inc(sink_in, 16)
            for c in range(KD):
                act.dma_start(xt[:, c, :], A["xt"][c]).then_inc(x_in, 16)
            act.wait_ge(const_in, 16)
            act.wait_ge(x_in, 16 * KD)
            for t in range(min(SLOTS, SLABS)):
                half(t, t, 1)
            each(act, KD, prepare_x(lambda c: None, 0, GAIN[stages[0]]), peel=4)
            k = 0
            for s in stages:
                if s == "attn":
                    attn(s)
                elif s.startswith("mem"):
                    mem(int(s[3]), s)
                elif s == "diff":
                    diff(s)
                elif s == "conf":
                    conf(s)
                elif s == "ssm":
                    ssm(s)
                elif s.startswith("ffn"):
                    ffn("ffn_in" + s[3], "ffn_out" + s[3], s, ("ffn_w" + s[3], "ffn_b" + s[3], None, k))
                    k += 1
                elif s.startswith("glu"):
                    ffn("glu_in" + s[3], "glu_out" + s[3], s, None)
                elif s == "final":
                    norm_root()
                    for c in range(KD):
                        act.wait_ge(out_ready, c + 1)
                        act.dma_start(out[c], xt[:, c, :]).then_inc(out_done, 16)
                    act.wait_ge(out_done, 16 * KD)


def pack(w):
    k, n = w.shape
    return np.ascontiguousarray(w.reshape(k // P, P, n // P, P).transpose(2, 1, 0, 3)).reshape(n // P, P, k)


def fcol(v):
    return np.ascontiguousarray(np.asarray(v).reshape(-1, P).T)


def interleave(w, half):
    k = w.shape[0]
    return np.ascontiguousarray(w.reshape(k, 2, half // P, P).transpose(0, 2, 1, 3)).reshape(k, 2 * half)


EXTRA = {"ssm": ("cst",), "attn": ("cst", "rel_rev", "sinks"), "mem0": ("memt",), "mem1": ("memt",), "diff": ("cst", "pos", "freq", "rot", "lam")}


def constants():
    p, m = np.arange(P)[:, None], np.arange(P)[None, :]
    chunk = np.where((p < 64) & (m >= 64), MASKED, 0.0)
    causal = np.where(m > p, MASKED, 0.0)
    decay = np.where(m < p, MASKED, 0.0)
    heads = (p // 64 == m // 64) * 1.0
    m = np.arange(256)[None, :]
    gone = ((p < 64) & (m >= 192)) | ((p >= 64) & (m < 64))
    alibi = [np.where(gone, MASKED, -8.0 * 2.0 ** -(h + 1) * np.abs(p - m + P)) for h in range(8)]
    return np.concatenate([chunk, causal, decay, heads] + alibi, 1).astype(np.float32)


def rotary():
    freq = np.zeros((P, 1), np.float32)
    rot = np.zeros((P, P), np.float32)
    for base in (0, 64):
        for i in range(8):
            freq[base + i] = freq[base + 8 + i] = 500000.0 ** (-i / 8)
            rot[base + 8 + i, base + i] = -1.0
            rot[base + i, base + 8 + i] = 1.0
    return freq, rot


def attn_in_cols(w):
    qa, ka, va, qb, kb, vb = np.split(w, [512, 1024, 1536, 2048, 2176], axis=1)
    qb = qb.reshape(-1, 2, 4, 64).transpose(0, 2, 1, 3).reshape(-1, 512)
    return np.concatenate([qa, ka, qb, kb, vb, va], 1)


def layout(I):
    A = {}
    A["cst"] = constants()
    A["rel_rev"] = np.ascontiguousarray(I["relpos_table"][0][:, ::-1])
    A["sinks"] = np.ascontiguousarray(I["sinks"][0])
    A["w_attn_in"] = pack(attn_in_cols(I["attn_w_in"][0]))
    wo = I["attn_w_out"][0]
    A["w_attn_out"] = pack(np.concatenate(
        [wo[:512], wo[512:].reshape(2, 4, 64, D).transpose(1, 0, 2, 3).reshape(512, D)], 0))
    A["xt"] = np.ascontiguousarray(np.asarray(I["x"])[0].T).reshape(KD, P, S)
    A["memt"] = np.ascontiguousarray(np.asarray(I["mem_2"])[0].T.reshape(KD, P, M).transpose(1, 0, 2))
    for l in range(2):
        A[f"w_mem_kv{l}"] = pack(np.concatenate([I["mem_w_k_2"][l], I["mem_w_v_2"][l]], 1))
        A[f"w_mem_q{l}"] = pack(I["mem_w_q_2"][l])
        A[f"w_mem_out{l}"] = pack(I["mem_w_o_2"][l])
    A["w_diff_kv"] = pack(np.concatenate([I["w_k_shared_2"], I["w_v_shared_2"]], 1))
    A["w_diff_q"] = pack(I["diff_w_q_2"][0])
    A["w_diff_out"] = pack(I["diff_w_o_2"][0])
    A["pos"] = np.ascontiguousarray(I["positions_2"])
    A["lam"] = np.stack([I["diff_lambda_q1_2"][0], I["diff_lambda_k1_2"][0], I["diff_lambda_q2_2"][0],
                         I["diff_lambda_k2_2"][0]]).reshape(1, 256)
    A["freq"], A["rot"] = rotary()
    A["w_pw1"] = pack(interleave(I["conv_w_pw1_2"][0], D))
    A["w_pw2"] = pack(I["conv_w_pw2_2"][0])
    z, xs, bc, dt = np.split(I["ssm_w_in"][0], [DIN, 2 * DIN, 2 * DIN + 2 * NGRP * NSTATE], axis=1)
    A["w_ssm_in"] = pack(np.concatenate([dt, np.zeros((D, P - SSMH), np.float32), bc, xs, z], 1))
    A["w_ssm_out"] = pack(I["ssm_w_out"][0])
    c = {}
    turned = lambda a: np.concatenate([a[..., DIN:], a[..., :DIN]], -1)
    c["ssm_cw"] = np.ascontiguousarray(turned(I["ssm_conv_w"][0]).reshape(4, 24, P).transpose(2, 1, 0)).reshape(P, -1)
    c["ssm_cb"] = fcol(turned(I["ssm_conv_b"][0]))
    c["ssm_d"] = fcol(np.repeat(I["ssm_d"][0], 64))
    c["ssm_norm"] = fcol(I["ssm_norm"][0])
    on_heads = lambda v: np.concatenate([v, np.zeros(P - SSMH, np.float32)])[:, None]
    c["ssm_dtb"] = on_heads(I["ssm_dt_bias"][0])
    c["ssm_alog"] = on_heads(I["ssm_a_log"][0])
    c["pw1_b"] = fcol(I["conv_b_pw1_2"][0].reshape(2, KD, P).transpose(1, 0, 2).reshape(-1))
    c["dw_w"] = np.ascontiguousarray(I["conv_w_dw_2"][0].reshape(CONVW, KD, P).transpose(2, 1, 0)).reshape(P, -1)
    c["dw_b"] = fcol(I["conv_b_dw_2"][0])
    c["ln_g"] = fcol(I["conv_ln_g_2"][0])
    c["ln_b"] = fcol(I["conv_ln_b_2"][0])
    c["pw2_b"] = fcol(I["conv_b_pw2_2"][0])
    c["subln"] = fcol(I["diff_subln_g_2"][0])
    pair = lambda v: np.concatenate([v, v])[:, None]
    c["g_qk"] = np.concatenate([pair(I["q_norm_a"][0])] * 4 + [pair(I["k_norm_a"][0])] * 4
                               + [pair(I["q_norm_b"][0])] * 4 + [pair(I["k_norm_b"][0])], 1)
    for l in range(2):
        c[f"norm_mix{l}"] = fcol(I["norm_mix"][l])
        c[f"norm_ffn{l}"] = fcol(I["norm_ffn"][l])
        A[f"w_ffn_in{l}"] = pack(interleave(I["ffn_w_in"][l], DFF))
        A[f"w_ffn_out{l}"] = pack(I["ffn_w_out"][l])
        c[f"ffn_w{l}"] = np.ascontiguousarray(I["ffn_conv_w"][l].reshape(3, KF, P).transpose(2, 1, 0)).reshape(P, -1)
        c[f"ffn_b{l}"] = fcol(I["ffn_conv_b"][l])
        c[f"norm_mix2_{l}"] = fcol(I["norm_mix_2"][l])
        c[f"norm_mem2_{l}"] = fcol(I["norm_mem_2"][l])
        c[f"norm_ffn2_{l}"] = fcol(I["norm_ffn_2"][l])
        A[f"w_glu_in{l}"] = pack(interleave(np.concatenate([I["ffn_w_gate_2"][l], I["ffn_w_up_2"][l]], 1), DFF))
        A[f"w_glu_out{l}"] = pack(I["ffn_w_down_2"][l])
    c["norm_final"] = fcol(I["norm_final_2"])
    c["kv_norm"] = fcol(I["kv_norm_2"])
    full = np.zeros((P, NCOL), np.float32)
    for name, n in COLUMNS:
        if name in c:
            full[:, COL[name]:COL[name] + n] = c[name]
    A["cols"] = full
    return A


def kernel(**inputs):
    import concourse.bacc as bacc
    from concourse.bass_utils import run_bass_kernel_spmd

    A = layout({name: np.asarray(value) for name, value in inputs.items()})
    nc = bacc.Bacc("TRN2", target_bir_lowering=False, num_devices=1)
    args = {name: nc.dram_tensor(name, a.shape, mybir.dt.from_np(a.dtype), kind="ExternalInput").ap()
            for name, a in A.items()}
    out = nc.dram_tensor("out", (KD, P, S), F32, kind="ExternalOutput").ap()
    build(nc, args, out)
    result = run_bass_kernel_spmd(nc, [A], core_ids=[0])
    return np.ascontiguousarray(result.results[0]["out"].reshape(D, S).T)[None]
```

```python
import math
from contextlib import ExitStack

import numpy as np

import concourse.bass as bass
from concourse import mybir

F32 = mybir.dt.float32
F32R = mybir.dt.float32r
BF16 = mybir.dt.bfloat16
I32 = mybir.dt.int32
ALU = mybir.AluOpType
ACT = mybir.ActivationFunctionType
AX_X = mybir.AxisListType.X
ds = bass.ds

P = 128
S = 512
D = 1024
KD = D // P
NT = S // P
DFF = 2816
KF = DFF // P
DIN = 2048
KI = DIN // P
NGRP = 4
NSTATE = 128
SSMH = 32
M = 256
CONVW = 31
RMS_EPS = 1e-6
LN_EPS = 1e-5
MASKED = -1e30
LAMBDA_INIT = 0.8 - 0.6 * math.exp(-0.3 * 1)

BANKS = 4
SLOTS = 4
SLAB = 8
PROB_LAG, TURN_LAG = 1, 3
PROBS = 4

STREAMS = [
    ("attn_in", 18, KD), ("attn_out", KD, KD),
    ("ffn_in0", 2 * KF, KD), ("ffn_out0", KD, KF),
    ("ssm_in", 41, KD), ("ssm_out", KD, KI),
    ("ffn_in1", 2 * KF, KD), ("ffn_out1", KD, KF),
    ("pw1", 2 * KD, KD), ("mem_kv0", 2 * KD, KD), ("pw2", KD, KD),
    ("mem_q0", KD, KD), ("mem_out0", KD, KD),
    ("glu_in0", 2 * KF, KD), ("glu_out0", KD, KF),
    ("diff_kv", 2 * KD, KD), ("diff_q", KD, KD), ("mem_kv1", 2 * KD, KD), ("diff_out", KD, KD),
    ("mem_q1", KD, KD), ("mem_out1", KD, KD),
    ("glu_in1", 2 * KF, KD), ("glu_out1", KD, KF),
]

COLUMNS = [
    ("norm_mix0", KD), ("norm_mix1", KD), ("norm_ffn0", KD), ("norm_ffn1", KD),
    ("g_qk", 13),
    ("ffn_w0", 3 * KF), ("ffn_w1", 3 * KF), ("ffn_b0", KF), ("ffn_b1", KF),
    ("ssm_cw", 4 * 24), ("ssm_cb", 24), ("ssm_d", KI), ("ssm_norm", KI), ("ssm_dtb", 1), ("ssm_alog", 1),
    ("norm_mix2_0", KD), ("norm_mix2_1", KD), ("norm_mem2_0", KD), ("norm_mem2_1", KD),
    ("norm_ffn2_0", KD), ("norm_ffn2_1", KD), ("norm_final", KD), ("kv_norm", KD),
    ("pw1_b", 2 * KD), ("dw_w", CONVW * KD), ("dw_b", KD), ("ln_g", KD), ("ln_b", KD), ("pw2_b", KD),
    ("subln", 1),
]
CONSTS = [("masks", 3 * P), ("head_ones", P), ("alibi", 8 * 256)]
NCST = sum(n for _, n in CONSTS)
COL = {}
NCOL = 0
for _name, _n in COLUMNS:
    COL[_name] = NCOL
    NCOL += _n


class Stream:

    def __init__(self, name, chunks, kc, slab0, chunk0):
        self.name, self.chunks, self.kc = name, chunks, kc
        self.slab0, self.chunk0 = slab0, chunk0
        self.slabs = [min(SLAB, kc - k) for k in range(0, kc, SLAB)]
        self.per = len(self.slabs)


def plan(names):
    out, slab, chunk = {}, 0, 0
    for name, chunks, kc in STREAMS:
        if name not in names:
            continue
        st = Stream(name, chunks, kc, slab, chunk)
        out[name] = st
        slab += chunks * st.per
        chunk += chunks
    return out


def each(eng, n, body, peel=0, tail=0, start=0):
    first = start + peel
    turns = max(n - tail - first, 0) // 4
    for c in range(start, min(first, n)):
        body(c, c % 4, c // 4)
    if turns > 1:
        with eng.Fori(0, turns) as i:
            for j in range(4):
                body(first + 4 * i + j, j, i + first // 4)
    for c in range(first + (4 * turns if turns > 1 else 0), n):
        body(c, c % 4, c // 4)


def lagged(fin, last):
    def after(c, j):
        if j >= 1:
            fin(c - 1, j - 1)
        if j == 3 or (isinstance(c, int) and c == last):
            fin(c, j)
    return after


class Unit:

    def __init__(self, scores, nk, scale, sink=None, rel=None):
        self.scores, self.nk, self.scale, self.sink, self.rel = scores, nk, scale, sink, rel


ALL = ("attn", "ffn0", "ssm", "ffn1", "conf", "mem0", "glu0", "diff", "mem1", "glu1", "final")
OF = {"attn": ("attn_in", "attn_out"), "ffn0": ("ffn_in0", "ffn_out0"), "ssm": ("ssm_in", "ssm_out"),
      "ffn1": ("ffn_in1", "ffn_out1"), "conf": ("pw1", "mem_kv0", "pw2"), "mem0": ("mem_q0", "mem_out0"),
      "glu0": ("glu_in0", "glu_out0"), "diff": ("diff_kv", "diff_q", "mem_kv1", "diff_out"),
      "mem1": ("mem_q1", "mem_out1"), "glu1": ("glu_in1", "glu_out1"), "final": ()}
GAIN = {"attn": "norm_mix0", "ffn0": "norm_ffn0", "ssm": "norm_mix1", "ffn1": "norm_ffn1", "conf": "norm_mix2_0",
        "mem0": "norm_mem2_0", "glu0": "norm_ffn2_0", "diff": "kv_norm", "mem1": "norm_mem2_1",
        "glu1": "norm_ffn2_1", "final": "norm_final"}


def build(nc, A, out, stages=ALL):
    ST = plan([n for s in stages for n in OF[s]])
    SLABS = sum(st.chunks * st.per for st in ST.values())
    nxt = {s: stages[i + 1] if i + 1 < len(stages) else None for i, s in enumerate(stages)}

    with ExitStack() as ctx:
        sems = {}

        def sem(name):
            if name not in sems:
                sems[name] = ctx.enter_context(nc.semaphore(name))
            return sems[name]

        base = (nc.sbuf_base + 63) // 64 * 64
        cursor = [base]
        high = [base]

        def sb(name, shape, dt=F32):
            t = nc.alloc_sbuf_tensor_at(name, [shape[0] if shape[0] > 1 else 1] + list(shape[1:]), dt, offset=cursor[0])
            n = int(np.prod(shape[1:])) * (2 if dt == BF16 else 4)
            cursor[0] += (n + 31) // 32 * 32
            high[0] = max(high[0], cursor[0])
            assert cursor[0] <= nc.sbuf_usable_end, (name, cursor[0] - nc.sbuf_usable_end)
            return t

        xt = sb("xt", [P, KD, S])
        w_raw = sb("w_raw", [P, SLOTS, SLAB * P])
        w_hi = sb("w_hi", [P, SLOTS, SLAB * P], F32R)
        w_lo = sb("w_lo", [P, SLOTS, SLAB * P], F32R)
        cols = sb("cols", [P, NCOL])
        ident = sb("ident", [P, P])
        ones = sb("ones", [P, P])
        ident_b = sb("ident_b", [P, P], BF16)
        masks_b = sb("masks_b", [P, 3, P], BF16)
        eps = sb("eps", [P, 2])
        rstd = sb("rstd", [P, S])
        acc = sb("acc", [P, S])
        sq = sb("sq", [P, 2, S])
        root = sq[:, 0, :]
        x_start = cursor[0]
        xh = sb("xh", [P, KD, S], F32R)
        xl = sb("xl", [P, KD, S], F32R)
        arena = cursor[0]

        hh = sb("hh", [P, KF, S], F32R)
        hl = sb("hl", [P, KF, S], F32R)
        f_g = sb("f_g", [P, S + 2])
        f_y = sb("f_y", [P, S])
        f_u = sb("f_u", [P, S])
        f_h = sb("f_h", [P, S])

        cursor[0] = arena
        oh = sb("oh", [P, KD, S], F32R)
        ol = sb("ol", [P, KD, S], F32R)
        a_prob_t = sb("a_prob_t", [P, PROBS, S])
        a_pt_t = sb("a_pt_t", [P, 2, S])
        a_stat = sb("a_stat", [P, 5, 64])
        v_tmp = a_prob_t[:, 0:2, :]
        q_root_t = a_prob_t[:, 2:4, :]
        a_common = cursor[0]
        qk = sb("qk", [P, 13, S])
        v_tok = sb("v_tok", [P, NT, 640])
        alibi_b = sb("alibi_b", [P, 8, 256], BF16)
        head_ones = sb("head_ones", [P, P])
        sink_c = sb("sink_c", [P, 8])
        flip = sb("flip", [P, P])
        rel = sb("rel", [P, 2, 640])
        cursor[0] = arena
        rel_row = sb("rel_row", [8, 767])
        cst = sb("cst", [P, NCST])
        rel_dram = nc.dram_tensor("rel_table", [8, 767], F32)

        cursor[0] = a_common
        m_q = sb("m_q", [P, KD, S])
        m_k = sb("m_k", [P, KD, M])
        m_v = sb("m_v", [P, M // P, D])
        behind_m = cursor[0]
        cursor[0] = x_start
        m_hi = sb("m_hi", [P, KD, M], F32R)
        m_lo = sb("m_lo", [P, KD, M], F32R)
        m_in = sb("m_in", [P, KD, M])

        cursor[0] = a_common
        d_q = sb("d_q", [P, KD, S])
        d_k = sb("d_k", [P, KD, S])
        d_v = sb("d_v", [P, NT, D])
        cosine = sb("cosine", [P, S])
        sine = sb("sine", [P, S])
        rot = sb("rot", [P, P])
        freq = sb("freq", [P, 1])
        lam_v = d_q[:, 0, 0:256].rearrange("p (a n) -> p a n", a=4)
        lam_t = d_q[:, 1, 0:128].rearrange("p (a n) -> p a n", a=2)
        lam_e = sb("lam_e", [P, 4])
        pos_i = d_v[:, 0, 0:S].bitcast(I32)
        d_t = d_v[:, 1:3, 0:S]

        CPE = 8
        cursor[0] = a_common
        c_y = sb("c_y", [P, KD, S])
        cursor[0] = behind_m
        c_u = sb("c_u", [P, 2, CONVW - 1 + S])
        c_mean = sb("c_mean", [P, S])
        c_a = sb("c_a", [P, 2, S])
        c_g = sb("c_g", [P, 2, S])
        c_diag = a_prob_t[:].rearrange("p a (b n) -> p a b n", b=4)
        c_s = a_pt_t

        cursor[0] = arena
        s_z = sb("s_z", [P, KI, S])
        s_xbc = sb("s_xbc", [P, 24, S])

        s_acs_h = sb("s_acs_h", [32, S], F32R)
        s_acs_l = sb("s_acs_l", [32, S], F32R)
        s_one = sb("s_one", [32, 32], F32R)
        s_tok = sb("s_tok", [P, 3, NT, SSMH])
        s_el = sb("s_el", [P, NT, SSMH])
        s_ea = sb("s_ea", [P, 3, S])
        s_dk = sb("s_dk", [P, 3, S])
        s_pad = s_dk[:].rearrange("p a n -> p (a n)")[:, 0:S + 3]
        cursor[0] = arena
        s_dt = sb("s_dt", [32, 8, S])
        s_acs = s_dt[:, 6, :]
        cursor[0] = arena
        yh = sb("yh", [P, KI, S], F32R)
        cursor[0] += 8 * S * 4
        yl = sb("yl", [P, KI, S], F32R)
        cursor[0] = x_start
        s_xt = sb("s_xt", [P, 2, NT, S])
        s_st = sb("s_st", [P, 2, NT - 1, S])
        s_cb = sb("s_cb", [P, 2, NT, P])

        bank = [ctx.enter_context(nc.psum_tensor(f"bank{i}", [P, 512], F32)) for i in range(8)]
        NORM_BANK = bank[7]

        def col(name, c=0):
            return cols[:, ds(COL[name] + c, 1)] if not isinstance(c, int) else cols[:, COL[name] + c:COL[name] + c + 1]

        w_landed = [sem(f"w_landed{i}") for i in range(SLOTS)]
        w_split = sem("w_split")
        w_half = sem("w_half")
        w_used = sem("w_used")
        chunk_done = sem("chunk_done")
        bank_free = sem("bank_free")
        const_in = sem("const_in")
        x_in = sem("x_in")
        init_done = sem("init_done")
        x_new, x_sq, x_hi, x_lo, x_acc = (sem(n) for n in ("x_new", "x_sq", "x_hi", "x_lo", "x_acc"))
        acc_zero = sem("acc_zero")
        nrm_sum, nrm_root, nrm_ready = (sem(n) for n in ("nrm_sum", "nrm_root", "nrm_ready"))
        dve_step = sem("dve_step")
        f_gate, f_tap, f_conv, f_silu, f_prod, f_hi, f_lo, f_up = (
            sem(n) for n in ("f_gate", "f_tap", "f_conv", "f_silu", "f_prod", "f_hi", "f_lo", "f_up"))
        out_ready, out_done = sem("out_ready"), sem("out_done")

        q_sq, q_sum, q_root, q_rec, q_ready = (sem(n) for n in ("q_sq", "q_sum", "q_root", "q_rec", "q_ready"))
        v_new, v_turned, v_ready = (sem(n) for n in ("v_new", "v_turned", "v_ready"))
        a_score, a_max, a_exp, a_prob, a_turn, a_pt, a_pv, a_oh, a_ol = (
            sem(n) for n in ("a_score", "a_max", "a_exp", "a_prob", "a_turn", "a_pt", "a_pv", "a_oh", "a_ol"))
        cst_in, cst_ready, rel_in, rel_ready, rel_out = (
            sem(n) for n in ("cst_in", "cst_ready", "rel_in", "rel_ready", "rel_out"))
        sink_in, flip_done = sem("sink_in"), sem("flip_done")
        rel_buf = [sem("rel_buf0"), sem("rel_buf1")]

        def attn_units():
            units, turns, groups = [], [], []
            for pair in range(8):
                first = len(units)
                for half in range(2):
                    lo, hi = 64 * half, 64 * half + 64
                    for t in range(NT):
                        if pair < 4:
                            h, kc, nk, k0 = 2 * pair + half, 4 + pair, P * (t + 1), 0
                            vcol = h * 64
                            bias = [(flip[:], rel[:, h % 2, 512 - P * t:640], 0, nk),
                                    (ident_b[:], masks_b[:, 0, :], nk - P, P)]
                        else:
                            h, kc = 4 * half + pair - 4, 12
                            nk, k0 = (P, 0) if t == 0 else (2 * P, P * (t - 1))
                            vcol = 512 + 64 * half
                            bias = [(ident_b[:], alibi_b[:, h, 256 - nk:256], 0, nk)]
                        qc = pair if pair < 4 else 8 + pair - 4
                        scores = [(qk[lo:hi, qc, t * P:(t + 1) * P], qk[lo:hi, kc, k0:k0 + nk], 0, nk)] + bias
                        u = Unit(scores, nk, 0.125, None if pair < 4 else sink_c[:, h:h + 1],
                                 h if pair < 4 else None)
                        u.pv = [(v_tok[:, k0 // P + kt, vcol:vcol + 64], kt, pair, lo, hi, t)
                                for kt in range(nk // P)]
                        units.append(u)
                groups.append((first, len(units), [pair]))
            return units, groups
        UNITS = {"attn": attn_units()}

        def mem_units():
            units, groups = [], []
            for h in range(KD // 2):
                first = len(units)
                for t in range(NT):
                    scores = [(m_q[:, 2 * h + k, t * P:(t + 1) * P], m_k[:, 2 * h + k, :], 0, M) for k in range(2)]
                    u = Unit(scores, M, 0.0625)
                    u.pv = [(m_v[:, kt, (2 * h + d) * P:(2 * h + d + 1) * P], kt, 2 * h + d, 0, P, t)
                            for d in range(2) for kt in range(M // P)]
                    units.append(u)
                groups.append((first, len(units), [2 * h, 2 * h + 1]))
            return units, groups
        UNITS["mem"] = mem_units()

        def diff_units():
            units, groups = [], []
            for h in range(KD):
                first = len(units)
                for t in range(NT):
                    nk = P * (t + 1)
                    for comp in range(2):
                        lo, hi = 64 * comp, 64 * comp + 64
                        u = Unit([(d_q[lo:hi, h, t * P:(t + 1) * P], d_k[lo:hi, h, 0:nk], 0, nk),
                                  (ident_b[:], masks_b[:, 1, :], nk - P, P)], nk, 0.125)
                        u.pv = [(d_v[:, kt, h * P:(h + 1) * P], kt, h, 0, P, t) for kt in range(t + 1)]
                        units.append(u)
                groups.append((first, len(units), [h]))
            return units, groups
        UNITS["diff"] = diff_units()

        def kv_round(l):
            return 1 if l == 0 or "mem_kv0" not in ST else 2

        def c_steps(p):
            return (CONVW - CPE + 1) * p

        m_landed, m_half, m_split = sem("m_landed"), sem("m_half"), sem("m_split")
        r_rot, r_t, r_c, r_done = sem("r_rot"), sem("r_t"), sem("r_c"), sem("r_done")
        y_hi, y_lo = sem("y_hi"), sem("y_lo")
        tab_in, tab_pos, tab_red, tab_sin, tab_done = (sem(n) for n in ("tab_in", "tab_pos", "tab_red", "tab_sin", "tab_done"))
        lam_in, lam_sum, lam_exp = sem("lam_in"), sem("lam_sum"), sem("lam_exp")
        o_rec = sem("o_rec")
        o_raw, o_sq, o_sum, o_root, o_new = (sem(n) for n in ("o_raw", "o_sq", "o_sum", "o_root", "o_new"))
        c_gate, c_sig, c_new, c_dia, c_pe, c_step, c_out = (
            sem(n) for n in ("c_gate", "c_sig", "c_new", "c_dia", "c_pe", "c_step", "c_out"))
        c_msum, c_mrow, c_cent, c_csq, c_cacc, c_norm, c_silu = (
            sem(n) for n in ("c_msum", "c_mrow", "c_cent", "c_csq", "c_cacc", "c_norm", "c_silu"))
        s_tap, s_conv, s_xbc_done, s_v, s_e, s_tp, s_tokd, s_eld = (
            sem(n) for n in ("s_tap", "s_conv", "s_xbc_done", "s_v", "s_e", "s_tp", "s_tokd", "s_eld"))
        s_turn, s_copied, s_cbp, s_cbd, s_xw_d, s_xd_d, s_u, s_state = (
            sem(n) for n in ("s_turn", "s_copied", "s_cbp", "s_cbd", "s_xw_d", "s_xd_d", "s_u", "s_state"))
        s_bc, s_exp, s_mask, s_dec, s_cp, s_m, s_y, s_yb, s_yz, s_sq, s_sum, s_root, s_yn = (
            sem(n) for n in ("s_bc", "s_exp", "s_mask", "s_dec", "s_cp", "s_m", "s_y", "s_yb", "s_yz", "s_sq", "s_sum",
                             "s_root", "s_yn"))
        s_yh, s_yl, s_e0, s_zd = sem("s_yh"), sem("s_yl"), sem("s_e0"), sem("s_zd")
        s_split, s_rec = sem("s_split"), sem("s_rec")
        block = ctx.enter_context(nc.Block())

        @block.sync
        def _(sp):
            def load_stream(st):
                w = A["w_" + st.name]

                def turn(i, chunks):
                    for j in range(chunks):
                        k = 0
                        for t, nb in enumerate(st.slabs):
                            o = j * st.per + t
                            slot = (st.slab0 + o) % SLOTS
                            sp.wait_ge(w_split, st.slab0 + o + 1 + i * 4 * st.per)
                            src = w[ds(4 * i + j, 1), :, k * P:(k + nb) * P] if not isinstance(i, int) \
                                else w[4 * i + j:4 * i + j + 1, :, k * P:(k + nb) * P]
                            sp.dma_start(w_raw[:, slot, 0:nb * P], src.rearrange("a p n -> (a p) n")) \
                                .then_inc(w_landed[slot], 16)
                            k += nb

                turns = st.chunks // 4
                with sp.Fori(0, turns) as i:
                    turn(i, 4)
                if st.chunks % 4:
                    turn(turns, st.chunks % 4)

            for st in ST.values():
                load_stream(st)

        @block.gpsimd
        def _(pool):
            pool.memset(ident[:], 0.0).then_inc(init_done, 1)
            pool.memset(ones[:], 1.0).then_inc(init_done, 1)
            pool.memset(eps[:, 0:1], RMS_EPS).then_inc(init_done, 1)
            pool.memset(eps[:, 1:2], LN_EPS).then_inc(init_done, 1)
            pool.wait_ge(init_done, 4)
            pool.affine_select(out=ident[:], in_=ident[:], compare_op=ALU.not_equal, fill=1.0, base=0,
                               pattern=[[-1, P]], channel_multiplier=1).then_inc(init_done, 1)
            if "attn" in stages:
                pool.memset(flip[:], 0.0).then_inc(flip_done, 1)
                pool.wait_ge(flip_done, 1)
                pool.affine_select(out=flip[:], in_=flip[:], compare_op=ALU.not_equal, fill=1.0, base=1 - P,
                                   pattern=[[1, P]], channel_multiplier=1).then_inc(flip_done, 1)

            def split_stream(st, first=None):
                def turn(i, chunks, between=None):
                    for j in range(chunks):
                        for t, nb in enumerate(st.slabs):
                            o = j * st.per + t
                            if between is not None and o == SLOTS:
                                between()
                            s = st.slab0 + o
                            slot = s % SLOTS
                            n = slice(0, nb * P)
                            pool.wait_ge(w_half, s + 1 + i * 4 * st.per)
                            pool.tensor_tensor(w_lo[:, slot, n], w_raw[:, slot, n], w_hi[:, slot, n].bitcast(F32),
                                               ALU.subtract).then_inc(w_split, 1)

                turns = st.chunks // 4
                if first is not None:
                    turn(0, 4, first)
                with pool.Fori(0 if first is None else 1, turns) as i:
                    turn(i, 4)
                if st.chunks % 4:
                    turn(turns, st.chunks % 4)

            def by_head(t, g, n):
                return t[:, 0:n, 8 * g:8 * g + 8].unsqueeze(3).broadcast_to([P, n, 8, 64])

            def ssm_weights():
                pool.wait_ge(s_tokd, 2)
                for g in range(NGRP):
                    x = s_xt[:, g % 2, :, :].rearrange("p a (h d) -> p a h d", d=64)
                    xw = s_st[:, g % 2].rearrange("p a (h d) -> p a h d", d=64)
                    pool.wait_ge(s_copied, 5 * g + 4)
                    if g >= 2:
                        pool.wait_ge(s_y, 8 * (g - 1))
                    pool.tensor_tensor(xw, x[:, 0:NT - 1], by_head(s_tok[:, 2], g, NT - 1), ALU.mult).then_inc(s_xw_d, 1)
                    pool.wait_ge(s_xw_d, g + 1)
                    pool.tensor_tensor(x, x, by_head(s_tok[:, 0], g, NT), ALU.mult).then_inc(s_xd_d, 1)

            for st in ST.values():
                split_stream(st, ssm_weights if st.name == "ssm_out" else None)

        @block.tensor
        def _(pe):
            nrm = [0]
            xs = [0]
            fs = [0]

            def gemm(st, hi, lo, n, ready, after=None, peel=0, tail=0, start=0, stop=None, after_i=None):
                def chunk(c, j, i):
                    b = bank[(st.chunk0 + j) % BANKS][:, 0:n]
                    pe.wait_ge(bank_free, st.chunk0 + c + 1)
                    k = 0
                    for t, nb in enumerate(st.slabs):
                        slot = (st.slab0 + j * st.per + t) % SLOTS
                        pe.wait_ge(w_split, SLOTS + st.slab0 + c * st.per + t + 1)
                        for q in range(nb):
                            if j == 0:
                                ready(k)
                            wh = w_hi[:, slot, q * P:(q + 1) * P]
                            wl = w_lo[:, slot, q * P:(q + 1) * P]
                            last = k == st.kc - 1
                            pe.matmul(b, wh, hi[:, k, 0:n], start=(k == 0), stop=False)
                            pe.matmul(b, wh, lo[:, k, 0:n], start=False, stop=False)
                            mm = pe.matmul(b, wl, hi[:, k, 0:n], start=False, stop=last)
                            k += 1
                        mm.then_inc(w_used, 1)
                    if after is not None:
                        after(c, j)
                    if after_i is not None:
                        after_i(c, j, i)

                each(pe, stop or st.chunks, chunk, peel, tail, start)

            def v_turn(src, v, new, n, bnk):
                pe.wait_ge(bank_free, new)
                pe.wait_ge(v_ready, v + 1)
                for t in range(n // P):
                    mm = pe.transpose(bnk[:, t * P:(t + 1) * P], src[:, t * P:(t + 1) * P], ident[:])
                mm.then_inc(v_turned, 1)

            def attention(units, groups, peers=1, out=None):
                U = len(units)
                u0, t0, g0, p0 = au[0], at[0], ag[0], ap[0]
                group_of = {first: (g, chunks) for g, (first, _, chunks) in enumerate(groups)}
                nch = len(groups[0][2])
                ends = {last: g for g, (_, last, _) in enumerate(groups)}
                for st_ in range(U + TURN_LAG + 1 if out is None else U + 7):
                    if out is not None and st_ - 6 in ends:
                        out(ends[st_ - 6])
                    if st_ < U:
                        u = units[st_]
                        b = bank[st_ % 3]
                        if st_ >= 3:
                            pe.wait_ge(a_exp, u0 + st_ - 2)
                        if u.rel is not None and st_ % NT == 0:
                            pe.wait_ge(rel_buf[u.rel % 2], 16 * (u.rel // 2 + 1))
                        for n, (l, r, c0, w) in enumerate(u.scores):
                            mm = pe.matmul(b[:, c0:c0 + w], l, r, start=(n == 0), stop=(n == len(u.scores) - 1),
                                           skip_group_check=True)
                        mm.then_inc(a_score, 1)
                    r = st_ - TURN_LAG
                    if 0 <= r < U and (r + 1) % peers == 0:
                        u, k = units[r], r // peers
                        src = a_prob_t[:, (r - peers + 1) % PROBS, :]
                        pe.wait_ge(a_prob, t0 + k + 1)
                        if k >= 2:
                            pe.wait_ge(a_pt, t0 + k - 1)
                        for kt in range(u.nk // P):
                            mm = pe.transpose(bank[3 + k % 2][:, kt * P:(kt + 1) * P], src[:, kt * P:(kt + 1) * P],
                                              ident[:])
                        mm.then_inc(a_turn, 1)
                    r = st_ - TURN_LAG - 1
                    if 0 <= r < U and (r + 1) % peers == 0:
                        u, k = units[r], r // peers
                        pe.wait_ge(a_pt, t0 + k + 1)
                        first = r - peers + 1
                        if first in group_of:
                            g, chunks = group_of[first]
                            held = g * nch + nch - 2
                            if held > 0:
                                if out is None:
                                    pe.wait_ge(a_ol, g0 + held)
                                else:
                                    pe.wait_ge(o_raw, held)
                        nk = u.nk // P
                        for v, kt, ch, lo, hi, t in u.pv:
                            mm = pe.matmul(bank[5 + ch % 2][lo:hi, t * P:(t + 1) * P], v,
                                           a_pt_t[:, k % 2, kt * P:(kt + 1) * P], start=(kt == 0),
                                           stop=(kt == nk - 1), skip_group_check=True)
                        mm.then_inc(a_pv, 1)
                au[0] += U
                at[0] += U // peers
                ag[0] += len(groups) * nch

            def attn():
                st = ST["attn_in"]

                def fin(c):
                    if isinstance(c, int) and c >= 13:
                        v_turn(v_tmp[:, c % 2, :], c - 13, BANKS + st.chunk0 + c + 1, S, bank[5 + c % 2])
                        return
                    pe.wait_ge(q_sq, c + 1)
                    if not isinstance(c, int) or c >= 2:
                        pe.wait_ge(q_root, c - 1)
                    pe.matmul(bank[5 + jj[0] % 2][:], head_ones[:], sq[:, jj[0] % 2, :], start=True, stop=True)\
                        .then_inc(q_sum, 1)
                jj = [0]

                def after(c, j):
                    first_sum(c, j)
                    if isinstance(c, int) and c == 0:
                        pe.wait_ge(cst_ready, 4)
                    if j >= 1:
                        jj[0] = j - 1
                        fin(c - 1)
                    if j == 3 or (isinstance(c, int) and c == 17):
                        jj[0] = j
                        fin(c)
                gemm(st, xh, xl, S, x_ready(KD * nrm[0]), after, peel=4, tail=6)
                pe.wait_ge(q_ready, 13)
                pe.wait_ge(flip_done, 2)
                pe.wait_ge(v_ready, 2 + 5)
                vt[0] = 5
                attention(*UNITS["attn"])
                gemm(ST["attn_out"], oh, ol, S, lambda k: pe.wait_ge(a_ol, k + 1))
            vt, au, at, ag, ap = [0], [0], [0], [0], [0]
            rc = [0]

            def mem_kv(l, after=None):
                kv = ST[f"mem_kv{l}"]
                v0 = vt[0]

                def fin(c, j):
                    v_turn(v_tmp[:, j % 2, 0:M], v0 + c - KD, BANKS + kv.chunk0 + c + 1, M, bank[5 + j % 2])
                pe.wait_ge(m_split, kv_round(l))
                gemm(kv, m_hi, m_lo, M, lambda k: None, after, peel=4, stop=KD)
                gemm(kv, m_hi, m_lo, M, lambda k: None, lagged(fin, 15), start=KD)
                vt[0] += KD

            def mem(l):
                gemm(ST[f"mem_q{l}"], xh, xl, S, x_ready(KD * nrm[0]), first_sum, peel=4)
                pe.wait_ge(bank_free, BANKS + ST[f"mem_q{l}"].chunk0 + KD)
                pe.wait_ge(v_ready, 2 + vt[0])
                g0 = ag[0]
                attention(*UNITS["mem"])
                gemm(ST[f"mem_out{l}"], oh, ol, S, lambda k: pe.wait_ge(a_ol, g0 + k + 1))

            def diff():
                kv, q = ST["diff_kv"], ST["diff_q"]

                def turn_rope(st, src, r0):
                    def fin(c, j):
                        pe.wait_ge(bank_free, BANKS + st.chunk0 + c + 1)
                        pe.wait_ge(r_done, r0 + c + 1)
                        if r0:
                            pe.wait_ge(v_ready, 2 + vt[0])
                        pe.matmul(bank[5 + j % 2][:], rot[:], src[:, c, :] if isinstance(c, int) else
                                  src[:, ds(c, 1), :].rearrange("p a n -> p (a n)"), start=True, stop=True)\
                            .then_inc(r_rot, 1)
                    return fin
                v0 = vt[0]

                def fin_v(c, j):
                    v_turn(v_tmp[:, j % 2, :], v0 + c - KD, BANKS + kv.chunk0 + c + 1, S, bank[5 + j % 2])

                def after(c, j):
                    first_sum(c, j)
                    if isinstance(c, int) and c == 0:
                        pe.wait_ge(tab_done, 1)
                    lagged(turn_rope(kv, d_k, 0), 7)(c, j)
                gemm(kv, xh, xl, S, x_ready(KD * nrm[0]), after, peel=4, stop=KD)
                gemm(kv, xh, xl, S, lambda k: None, lagged(fin_v, 15), start=KD)
                vt[0] += KD
                gemm(q, xh, xl, S, lambda k: pe.wait_ge(y_lo, k + 1), lagged(turn_rope(q, d_q, KD), 7))
                pe.wait_ge(r_done, 2 + 2 * KD)
                pe.wait_ge(v_ready, 2 + vt[0])
                g0 = ag[0]

                def out(g):
                    pe.wait_ge(o_sq, g + 1)
                    pe.matmul(NORM_BANK[:], ones[:], sq[:, g % 2, :], start=True, stop=True).then_inc(o_sum, 1)
                attention(*UNITS["diff"], peers=2, out=out)
                mem_kv(1)
                gemm(ST["diff_out"], oh, ol, S, lambda k: pe.wait_ge(a_ol, g0 + k + 1))

            def conf():
                st = ST["pw1"]

                def conv(p, q):
                    pe.wait_ge(c_new, p + 1)
                    pe.wait_ge(c_dia, CPE * (p + 1))
                    pe.wait_ge(c_out, p + 1)
                    for n in range(CPE):
                        mm = pe.matmul(bank[5 + q][:], c_diag[:, 2 * q + n // 4, n % 4, :], c_u[:, q, n:n + S],
                                       start=(n == 0), stop=(n == CPE - 1))
                    mm.then_inc(c_pe, 1)

                def after_i(c, j, i):
                    first_sum(c, j)
                    if j == 3 and not (isinstance(c, int) and c == 3):
                        conv(2 * i - 2, 0)
                        conv(2 * i - 1, 1)
                gemm(st, xh, xl, S, x_ready(KD * nrm[0]), None, peel=4, after_i=after_i)
                conv(6, 0)
                conv(7, 1)
                pe.wait_ge(c_step, c_steps(KD))
                pe.matmul(NORM_BANK[:], ones[:], acc[:], start=True, stop=True).then_inc(c_msum, 1)

                def squares(c, j):
                    if isinstance(c, int) and c == 2:
                        pe.wait_ge(c_cacc, KD)
                        pe.matmul(NORM_BANK[:], ones[:], acc[:], start=True, stop=True).then_inc(c_msum, 1)
                mem_kv(0, squares)
                gemm(ST["pw2"], oh, ol, S, lambda k: pe.wait_ge(a_ol, c_ol[0] + k + 1))
                ag[0] += KD
            c_ol = ag

            def ssm():
                st = ST["ssm_in"]
                acs_of = lambda c: slice(c * P, (c + 1) * P)

                def after(c, j):
                    first_sum(c, j)
                    if isinstance(c, int) and c == 3:
                        pe.wait_ge(s_v, 1)
                        for n, src in enumerate((s_dt[:, 0, :], s_acs, s_dt[:, 1, :])):
                            for t in range(NT):
                                pe.transpose(bank[4][:, (NT * n + t) * SSMH:(NT * n + t + 1) * SSMH], src[:, acs_of(t)],
                                             ident[0:32, 0:32])
                        pe.matmul(bank[4][:, 3 * P:4 * P], ones[0:32, :], s_dt[:, 2, 0:P], start=True, stop=True,
                                  skip_group_check=True).then_inc(s_tp, 1)
                gemm(st, xh, xl, S, x_ready(KD * nrm[0]), after, peel=4)
                pe.wait_ge(s_xbc_done, 24)

                def prepare(g, r):
                    if r < 4:
                        b = bank[5 + r % 2]
                        n = 5 * g + r
                        if r >= 2:
                            pe.wait_ge(s_copied, n - 1)
                        elif g:
                            pe.wait_ge(s_state, 3 * g)
                        for t in range(NT):
                            mm = pe.transpose(b[:, acs_of(t)], s_xbc[:, 8 + 4 * g + r, acs_of(t)], ident[:])
                        mm.then_inc(s_turn, 1)
                        return
                    if g:
                        pe.wait_ge(s_state, 3 * g)
                    for t in range(NT):
                        mm = pe.matmul(bank[4][:, acs_of(t)], s_xbc[:, g, acs_of(t)], s_xbc[:, 4 + g, acs_of(t)],
                                       start=True, stop=True, skip_group_check=True)
                    mm.then_inc(s_cbp, 1)
                    pe.wait_ge(s_copied, 5 * g + 3)
                    for t in range(NT):
                        mm = pe.transpose(bank[5][:, acs_of(t)], s_xbc[:, g, acs_of(t)], ident[:])
                    mm.then_inc(s_turn, 1)

                def inflow(g):
                    pe.wait_ge(s_copied, 5 * g + 5)
                    pe.wait_ge(s_cbd, g + 1)
                    pe.wait_ge(s_xw_d, g + 1)
                    for t in range(NT - 1):
                        mm = pe.matmul(bank[4 + t][:], s_xbc[:, g, acs_of(t)], s_st[:, g % 2, t, :], start=True, stop=True)
                    mm.then_inc(s_u, 1)

                pe.wait_ge(s_tokd, 2)
                pe.wait_ge(s_eld, 1)
                pe.wait_ge(s_split, 3)
                for r in range(5):
                    prepare(0, r)
                inflow(0)
                pe.wait_ge(bank_free, BANKS + st.chunk0 + st.chunks)
                for n in range(SSMH + 7):
                    if n < SSMH:
                        if n >= 2:
                            pe.wait_ge(s_dec, n - 1)
                        pick = s_one[:, n:n + 1].broadcast_to([32, P])
                        pe.matmul(bank[n % 2][:], pick, s_acs_h[:], start=True, stop=False, skip_group_check=True)
                        pe.matmul(bank[n % 2][:], pick, s_acs_l[:], start=False, stop=False, skip_group_check=True)\
                            .then_inc(s_bc, 1)
                    k = n - 1
                    if 0 <= k < SSMH:
                        pe.wait_ge(s_exp, k + 1)
                        pe.matmul(bank[k % 2][:], ident_b[:], masks_b[:, 2:3, :].broadcast_to([P, NT, P]),
                                  start=False, stop=True, skip_group_check=True).then_inc(s_mask, 1)
                    k = n - 2
                    if 0 <= k < SSMH:
                        g, f = k // 8, k // 2
                        lo = 64 * (k % 2)
                        y = bank[2 + f % 2][lo:lo + 64, :]
                        h = slice(k % 8 * 64, k % 8 * 64 + 64)
                        if k % 8 == 0:
                            pe.wait_ge(s_xd_d, g + 1)
                            pe.wait_ge(s_state, 3 * (g + 1))
                        if k % 2 == 0 and f >= 2:
                            pe.wait_ge(s_yb, f - 1)
                        pe.wait_ge(s_cp, k + 1)
                        pe.wait_ge(s_m, k + 1)
                        for t in range(NT):
                            mm = pe.matmul(y[:, acs_of(t)], s_xt[:, g % 2, t, h], s_dk[:, k % 3, acs_of(t)],
                                           start=True, stop=(t == 0), skip_group_check=True)
                            if t:
                                mm = pe.matmul(y[:, acs_of(t)], s_st[:, g % 2, t - 1, h], s_ea[:, k % 3, acs_of(t)],
                                               start=False, stop=True, skip_group_check=True)
                        mm.then_inc(s_y, 1)
                    g, r = n // 8, n % 8 - 1
                    if g + 1 < NGRP and 0 <= r < 5:
                        prepare(g + 1, r)
                    if g + 1 < NGRP and r == 6:
                        inflow(g + 1)
                    f = n // 2 - 3
                    if n % 2 == 0 and 0 <= f < KI:
                        pe.wait_ge(s_sq, f + 1)
                        if f % 4 == 0 and f:
                            pe.wait_ge(s_root, f // 4)
                        pe.matmul(NORM_BANK[:], ones[:], sq[:, f % 2, :], start=(f % 4 == 0), stop=(f % 4 == 3),
                                  skip_group_check=True).then_inc(s_sum, 1)
                gemm(ST["ssm_out"], yh, yl, S, lambda k: pe.wait_ge(s_yl, k + 1))

            def x_ready(base):
                return lambda k: pe.wait_ge(x_lo, base + k + 1)

            def norm_sum():
                nrm[0] += 1
                pe.wait_ge(x_acc, KD * nrm[0])
                pe.matmul(NORM_BANK[:], ones[:], acc[:], start=True, stop=True).then_inc(nrm_sum, 1)

            def first_sum(c, j):
                if isinstance(c, int) and c == 0:
                    norm_sum()

            def ffn(si, so):
                gemm(ST[si], xh, xl, S, x_ready(KD * nrm[0]), first_sum, peel=4)
                f0 = fs[0]
                fs[0] += KF
                gemm(ST[so], hh, hl, S, lambda k: pe.wait_ge(f_lo, f0 + k + 1))

            pe.wait_ge(init_done, 5)
            for s in stages:
                if s == "attn":
                    attn()
                elif s.startswith("mem"):
                    mem(int(s[3]))
                elif s == "diff":
                    diff()
                elif s == "conf":
                    conf()
                elif s == "ssm":
                    ssm()
                elif s.startswith("ffn"):
                    ffn("ffn_in" + s[3], "ffn_out" + s[3])
                elif s.startswith("glu"):
                    ffn("glu_in" + s[3], "glu_out" + s[3])
                elif s == "final":
                    norm_sum()

        @block.vector
        def _(dve):
            nrm = [0]
            steps = [0]

            def new_x(s):
                return GAIN[s] if s else None

            def split_x(c, k, gain):
                dve.wait_ge(x_hi, k + 1)
                dve.scalar_tensor_tensor(xl_(c), xt_(c), col(gain, c), xh_(c).bitcast(F32),
                                         ALU.mult, ALU.subtract).then_inc(x_lo, 1)

            def add_square(k, j):
                dve.wait_ge(x_sq, k + 1)
                dve.wait_ge(x_acc, k)
                dve.tensor_tensor(acc[:], acc[:], sq[:, j % 2, :], ALU.add).then_inc(x_acc, 1)

            def zero_acc():
                dve.wait_ge(nrm_sum, nrm[0]) if nrm[0] else None
                dve.memset(acc[:], 0.0).then_inc(acc_zero, 1)
                dve.wait_ge(acc_zero, nrm[0] + 1)

            def norm_recip():
                nrm[0] += 1
                dve.wait_ge(nrm_root, nrm[0])
                dve.reciprocal(rstd[:], root).then_inc(nrm_ready, 1)
                dve.wait_ge(nrm_ready, nrm[0])

            def residual(st, gain, bias=None):
                zero_acc()
                k0 = KD * nrm[0]

                def chunk(c, j, i):
                    b = bank[(st.chunk0 + j) % BANKS]
                    dve.wait_ge(w_used, SLOTS + st.slab0 + (c + 1) * st.per)
                    if bias is None:
                        dve.tensor_tensor(xt_(c), b[:], xt_(c), ALU.add).then_inc(bank_free, 1)
                    else:
                        dve.scalar_tensor_tensor(xt_(c), b[:], col(bias, c), xt_(c), ALU.add, ALU.add).then_inc(bank_free, 1)
                    dve.wait_ge(bank_free, BANKS + st.chunk0 + c + 1)
                    add_square(k0 + c, j)
                    split_x(c, k0 + c, gain)
                each(dve, KD, chunk)

            def step(ins):
                ins.then_inc(dve_step, 1)
                steps[0] += 1
                dve.wait_ge(dve_step, steps[0])

            def attention(units, groups, peers=1, out=None, lam=None):
                U = len(units)
                u0, t0, g0 = au[0], at[0], ag[0]
                ends = {last: (g, chunks) for g, (_, last, chunks) in enumerate(groups)}
                nch = len(groups[0][2])
                for s_ in range(U + 5 if out is None else U + 13):
                    for lag, do in out or ():
                        if s_ - lag in ends:
                            do(ends[s_ - lag][0])
                    if s_ < U:
                        u, cs = units[s_], slice(s_, s_ + 1)
                        dve.wait_ge(a_score, u0 + s_ + 1)
                        step(dve.reduce_max(a_stat[:, 0, cs], bank[s_ % 3][:, 0:u.nk], AX_X))
                        if u.sink is None:
                            dve.tensor_scalar(a_stat[:, 1, cs], a_stat[:, 0, cs], -u.scale, None, ALU.mult)\
                                .then_inc(a_max, 1)
                        else:
                            step(dve.tensor_scalar(a_stat[:, 0, cs], a_stat[:, 0, cs], u.scale, u.sink,
                                                   ALU.mult, ALU.max))
                            dve.tensor_scalar(a_stat[:, 1, cs], a_stat[:, 0, cs], -1.0, None, ALU.mult)\
                                .then_inc(a_max, 1)
                    r = s_ - PROB_LAG
                    if 0 <= r < U:
                        u, cs = units[r], slice(r, r + 1)
                        dve.wait_ge(a_exp, u0 + r + 1)
                        if u.sink is not None:
                            step(dve.tensor_tensor(a_stat[:, 2, cs], a_stat[:, 2, cs], a_stat[:, 3, cs], ALU.add))
                        step(dve.reciprocal(a_stat[:, 4, cs], a_stat[:, 2, cs]))
                        pr = a_prob_t[:, r % PROBS, 0:u.nk]
                        if peers == 1:
                            dve.tensor_scalar(pr, pr, a_stat[:, 4, cs], None, ALU.mult).then_inc(a_prob, 1)
                        elif r % 2 == 0:
                            step(dve.tensor_scalar(pr, pr, a_stat[:, 4, cs], None, ALU.mult))
                        else:
                            step(dve.tensor_scalar(a_stat[:, 4, cs], a_stat[:, 4, cs], lam, None, ALU.mult))
                            first = a_prob_t[:, (r - 1) % PROBS, 0:u.nk]
                            dve.scalar_tensor_tensor(first, pr, a_stat[:, 4, cs], first, ALU.mult, ALU.add)\
                                .then_inc(a_prob, 1)
                    if s_ - TURN_LAG - 1 in ends and out is None:
                        g, chunks = ends[s_ - TURN_LAG - 1]
                        for n, ch in enumerate(chunks):
                            dve.wait_ge(a_oh, g0 + g * nch + n + 1)
                            dve.tensor_tensor(ol[:, ch, :], bank[5 + ch % 2][:], oh[:, ch, :].bitcast(F32),
                                              ALU.subtract).then_inc(a_ol, 1)
                au[0] += U
                at[0] += U // peers
                ag[0] += len(groups) * nch
            au, at, ag = [0], [0], [0]
            vt = [0]

            def row(t, c):
                return t[:, c, :] if isinstance(c, int) else t[:, ds(c, 1), :].rearrange("p a n -> p (a n)")

            def value(st, c, j, v, n, scaled):
                dve.wait_ge(w_used, SLOTS + st.slab0 + c + 1)
                if not isinstance(v, int) or v >= 2:
                    dve.wait_ge(v_turned, v - 1)
                b = bank[(st.chunk0 + j) % BANKS][:, 0:n]
                if scaled:
                    dve.tensor_tensor(v_tmp[:, j % 2, 0:n], b, rstd[:], ALU.mult).then_inc(bank_free, 1)
                else:
                    dve.tensor_copy(v_tmp[:, j % 2, 0:n], b).then_inc(bank_free, 1)

            def mem_kv(l):
                kv = ST[f"mem_kv{l}"]
                v0 = vt[0]
                vt[0] += KD
                dve.wait_ge(m_half, kv_round(l))
                dve.tensor_tensor(m_lo[:], m_in[:], m_hi[:].bitcast(F32), ALU.subtract).then_inc(m_split, 1)

                def chunk(c):
                    if c < KD:
                        dve.wait_ge(w_used, SLOTS + kv.slab0 + c + 1)
                        dve.tensor_copy(m_k[:, c, :], bank[(kv.chunk0 + c) % BANKS][:, 0:M]).then_inc(bank_free, 1)
                    else:
                        value(kv, c, c % 4, v0 + c - KD, M, False)
                return chunk

            def mem(l, s):
                q = ST[f"mem_q{l}"]
                norm_recip()

                def query(c, j, i):
                    dve.wait_ge(w_used, SLOTS + q.slab0 + c + 1)
                    dve.tensor_tensor(row(m_q, c), bank[(q.chunk0 + j) % BANKS][:], rstd[:], ALU.mult)\
                        .then_inc(bank_free, 1)
                each(dve, KD, query)
                attention(*UNITS["mem"])
                residual(ST[f"mem_out{l}"], new_x(nxt[s]))

            def rope(st, dst, r0, c, j):
                b = bank[5 + j % 2]
                dve.wait_ge(r_rot, r0 + c + 1)
                dve.wait_ge(r_done, 2 + r0 + c)
                dve.tensor_tensor(c_rope[:], b[:], sine[:], ALU.mult).then_inc(r_t, 1)
                dve.tensor_tensor(row(dst, c), row(dst, c), cosine[:], ALU.mult).then_inc(r_c, 1)
                dve.wait_ge(r_c, r0 + c + 1)
                dve.wait_ge(r_t, r0 + c + 1)
                dve.tensor_tensor(row(dst, c), row(dst, c), c_rope[:], ALU.add).then_inc(r_done, 1)
            c_rope = a_prob_t[:, 2, :]

            def diff(s):
                kv, q = ST["diff_kv"], ST["diff_q"]
                two_pi = 2.0 * math.pi
                c1 = 6.28125
                c2 = float(np.float32(np.round((two_pi - c1) * 2 ** 21) / 2 ** 21))
                c3 = float(np.float32(two_pi - c1 - c2))
                magic = 1.5 * 2 ** 23
                ang, turns = d_t[:, 0, :], d_t[:, 1, :]
                dve.wait_ge(tab_in, 48)
                step(dve.tensor_copy(ang, pos_i))
                step(dve.tensor_scalar(ang, ang, freq[:, 0:1], None, ALU.mult))
                step(dve.tensor_scalar(turns, ang, 1.0 / two_pi, magic, ALU.mult, ALU.add))
                step(dve.tensor_scalar(turns, turns, magic, None, ALU.subtract))
                for part in (c1, c2, c3):
                    step(dve.scalar_tensor_tensor(ang, turns, -part, ang, ALU.mult, ALU.add))
                dve.tensor_scalar(ang, ang, 3.1415925, -3.1415925, ALU.min, ALU.max).then_inc(tab_red, 1)
                dve.wait_ge(tab_sin, 2)
                step(dve.tensor_tensor(turns, turns, turns, ALU.mult))
                dve.tensor_scalar(cosine[:], turns, -2.0, 1.0, ALU.mult, ALU.add).then_inc(tab_done, 1)
                dve.wait_ge(lam_in, 16)
                step(dve.tensor_tensor(lam_t, lam_v[:, 0:4:2, :], lam_v[:, 1:4:2, :], ALU.mult))
                dve.tensor_reduce(lam_e[:, 0:2], lam_t, AX_X, ALU.add).then_inc(lam_sum, 1)
                dve.wait_ge(lam_exp, 1)
                step(dve.tensor_tensor(lam_e[:, 3:4], lam_e[:, 3:4], lam_e[:, 2:3], ALU.subtract))
                step(dve.tensor_scalar(lam_e[:, 3:4], lam_e[:, 3:4], -LAMBDA_INIT, None, ALU.add))
                norm_recip()

                def heads(st, dst, r0):
                    def chunk(c, j, i):
                        dve.wait_ge(w_used, SLOTS + st.slab0 + c + 1)
                        dve.tensor_tensor(row(dst, c), bank[(st.chunk0 + j) % BANKS][:], rstd[:], ALU.mult)\
                            .then_inc(bank_free, 1)
                        lagged(lambda c, j: rope(st, dst, r0, c, j), -1)(c, j)
                    return chunk
                v0 = vt[0]
                each(dve, KD, heads(kv, d_k, 0))
                each(dve, 2 * KD, lambda c, j, i: value(kv, c, j, v0 + c - KD, S, True), start=KD, peel=4)
                vt[0] += KD
                for c in range(KD):
                    dve.wait_ge(y_hi, c + 1)
                    dve.scalar_tensor_tensor(xl[:, c, :], xt[:, c, :], col("norm_mix2_1", c),
                                             xh[:, c, :].bitcast(F32), ALU.mult, ALU.subtract).then_inc(y_lo, 1)
                each(dve, KD, heads(q, d_q, KD))
                dve.wait_ge(r_done, 2 + 2 * KD)

                def raw(g):
                    dve.wait_ge(a_pv, a_pv0 + NT * (g + 1))
                    dve.tensor_copy(d_q[:, g, :], bank[5 + g % 2][:]).then_inc(o_raw, 1)

                def recip(n):
                    def do(g):
                        dve.wait_ge(o_root, g + 1)
                        part = rstd[:, n * 256:(n + 1) * 256]
                        dve.reciprocal(part, part).then_inc(o_rec, 1)
                    return do

                def normed(g):
                    dve.wait_ge(o_rec, 2 * g + 2)
                    dve.scalar_tensor_tensor(d_q[:, g, :], d_q[:, g, :], col("subln"), rstd[:], ALU.mult, ALU.mult)\
                        .then_inc(o_new, 1)

                def lower(g):
                    dve.wait_ge(a_oh, g0 + g + 1)
                    dve.scalar_tensor_tensor(ol[:, g, :], d_q[:, g, :], 1.0 - LAMBDA_INIT, oh[:, g, :].bitcast(F32),
                                             ALU.mult, ALU.subtract).then_inc(a_ol, 1)
                a_pv0, g0 = at[0], ag[0]
                attention(*UNITS["diff"], peers=2, lam=lam_e[:, 3:4],
                          out=((5, raw), (8, recip(0)), (9, recip(1)), (10, normed), (12, lower)))
                chunk = mem_kv(1)
                for c in range(2 * KD):
                    chunk(c)
                residual(ST["diff_out"], new_x(nxt[s]))

            def ssm(s):
                st = ST["ssm_in"]
                norm_recip()
                t = lambda n: s_dt[:, n, :]

                def softplus_and_sums():
                    dve.wait_ge(w_used, SLOTS + st.slab0 + 1)
                    dve.tensor_tensor(t(0), bank[st.chunk0 % BANKS][0:32, :], rstd[0:32, :], ALU.mult).then_inc(bank_free, 1)
                    dve.wait_ge(bank_free, BANKS + st.chunk0 + 1)
                    step(dve.tensor_scalar(t(0), t(0), col("ssm_dtb")[0:32], None, ALU.add))
                    dve.scalar_tensor_tensor(t(1), t(0), -1.0, t(0), ALU.mult, ALU.max).then_inc(s_e0, 1)
                    dve.wait_ge(s_e, 2)
                    step(dve.tensor_scalar(t(2), t(1), 2.0, None, ALU.add))
                    step(dve.reciprocal(t(2), t(2)))
                    step(dve.tensor_tensor(t(1), t(1), t(2), ALU.mult))
                    step(dve.tensor_tensor(t(2), t(1), t(1), ALU.mult))
                    step(dve.tensor_scalar(t(3), t(2), 1.0 / 15.0, None, ALU.mult))
                    for n in (13, 11, 9, 7, 5, 3):
                        step(dve.scalar_tensor_tensor(t(3), t(3), 1.0 / n, t(2), ALU.add, ALU.mult))
                    step(dve.scalar_tensor_tensor(t(3), t(3), 1.0, t(1), ALU.add, ALU.mult))
                    step(dve.tensor_scalar(t(0), t(0), 0.0, None, ALU.max))
                    step(dve.scalar_tensor_tensor(t(0), t(3), 2.0, t(0), ALU.mult, ALU.add))
                    dve.wait_ge(s_e, 2)
                    step(dve.tensor_scalar(t(4), t(0), t(5)[:, 0:1], -1.0, ALU.mult, ALU.mult))
                    for c in range(NT):
                        cs = slice(c * P, (c + 1) * P)
                        ins = dve.tensor_tensor_scan(s_acs[:, cs], ones[0:32, :], t(4)[:, cs], 0.0, ALU.mult, ALU.add)
                        step(ins)
                    last = s_acs.rearrange("p (a n) -> p a n", a=NT)[:, :, P - 1:P]
                    dve.tensor_tensor(t(2)[:, 0:P].rearrange("p (a n) -> p a n", a=NT),
                                      ident[0:32, 0:32].unsqueeze(1).broadcast_to([32, NT, 32]),
                                      last.broadcast_to([32, NT, 32]), ALU.mult).then_inc(s_e0, 1)
                    dve.wait_ge(s_e, 6)
                    dve.tensor_tensor(t(1), t(1), t(0), ALU.mult).then_inc(s_v, 1)

                def taps(c, j, i):
                    if isinstance(c, int) and c == 0:
                        return softplus_and_sums()
                    q = c - 1
                    y = s_ea[:, j % 2, :]
                    dve.wait_ge(w_used, SLOTS + st.slab0 + c + 1)
                    if not (isinstance(c, int) and c == 1):
                        dve.wait_ge(s_conv, 3 * q)
                    dve.tensor_tensor(s_pad[:, 3:S + 3], bank[(st.chunk0 + j) % BANKS][:], rstd[:], ALU.mult)\
                        .then_inc(bank_free, 1)
                    dve.wait_ge(s_tap, q + 1)
                    for n in range(3):
                        dve.scalar_tensor_tensor(y, s_pad[:, n:n + S], col("ssm_cw", 4 * q + n), y, ALU.mult, ALU.add)\
                            .then_inc(s_conv, 1)
                        if n < 2:
                            dve.wait_ge(s_conv, 3 * q + n + 1)

                def gate(c, j, i):
                    dve.wait_ge(w_used, SLOTS + st.slab0 + c + 1)
                    dve.tensor_tensor(row(s_z, c - 25), bank[(st.chunk0 + j) % BANKS][:], rstd[:], ALU.mult)\
                        .then_inc(bank_free, 1)
                step(dve.memset(s_pad[:, 0:3], 0.0))
                each(dve, 25, taps, peel=4)
                dve.wait_ge(s_tp, 1)
                dve.wait_ge(s_split, 2)
                dve.tensor_copy(s_tok[:].rearrange("p a b n -> p (a b n)"), bank[4][:, 0:3 * P]).then_inc(s_tokd, 1)
                dve.wait_ge(s_tokd, 1)
                dve.tensor_tensor(s_acs_l[:], s_acs, s_acs_h[:].bitcast(F32), ALU.subtract).then_inc(s_split, 1)
                dve.tensor_scalar(s_tok[:, 1, :, :], s_tok[:, 1, :, :], -1.0, None, ALU.mult).then_inc(s_tokd, 1)
                dve.wait_ge(s_tokd, 2)
                each(dve, 41, gate, start=25, peel=3)

                def products(g):
                    dve.wait_ge(s_cbp, g + 1)
                    dve.tensor_copy(s_cb[:, g % 2, :, :].rearrange("p a n -> p (a n)"), bank[4][:]).then_inc(s_cbd, 1)

                def state(g, n):
                    dve.wait_ge(s_u, g + 1)
                    st_ = s_st[:, g % 2]
                    if n == 0:
                        dve.tensor_copy(st_[:, 0, :], bank[4][:]).then_inc(s_state, 1)
                        return
                    dve.wait_ge(s_state, 3 * g + n)
                    el = s_el[:, n, 8 * g:8 * g + 8].unsqueeze(2).broadcast_to([P, 8, 64])
                    step(dve.tensor_tensor(st_[:, n, :].rearrange("p (h d) -> p h d", d=64),
                                           st_[:, n - 1, :].rearrange("p (h d) -> p h d", d=64), el, ALU.mult))
                    dve.tensor_tensor(st_[:, n, :], bank[4 + n][:], st_[:, n, :], ALU.add).then_inc(s_state, 1)

                dve.wait_ge(s_eld, 1)
                products(0)
                for n in range(NT - 1):
                    state(0, n)
                def low(f):
                    dve.wait_ge(s_yh, f + 1)
                    dve.wait_ge(s_yn, f + 1)
                    dve.tensor_tensor(yl[:, f, :], s_xbc[:, 8 + f, :], yh[:, f, :].bitcast(F32), ALU.subtract)\
                        .then_inc(s_yl, 1)

                for n in range(SSMH + 13 + 4):
                    if n < SSMH:
                        dve.wait_ge(s_exp, n + 1)
                        dve.tensor_tensor(s_ea[:, n % 3, :], s_xbc[:, 4 + n // 8, :], s_ea[:, n % 3, :], ALU.mult)\
                            .then_inc(s_cp, 1)
                    k = n - 1
                    if 0 <= k < SSMH:
                        dve.wait_ge(s_dec, k + 1)
                        if k % 8 == 0:
                            dve.wait_ge(s_cbd, k // 8 + 1)
                        dve.tensor_tensor(s_dk[:, k % 3, :], s_dk[:, k % 3, :],
                                          s_cb[:, k // 8 % 2, :, :].rearrange("p a n -> p (a n)"), ALU.mult)\
                            .then_inc(s_m, 1)
                    if n % 8 == 7 and n // 8 + 1 < NGRP:
                        state(n // 8 + 1, 0)
                        state(n // 8 + 1, 1)
                    if n % 8 == 0 and 0 < n < SSMH:
                        state(n // 8, 2)
                    f = n // 2 - 2
                    if n % 2 == 0 and 0 <= f < KI:
                        x = s_xbc[:, 8 + f, :]
                        dve.wait_ge(s_y, 2 * f + 2)
                        dve.scalar_tensor_tensor(x, x, col("ssm_d", f), bank[2 + f % 2][:], ALU.mult, ALU.add)\
                            .then_inc(s_yb, 1)
                        dve.wait_ge(s_yb, f + 1)
                        dve.tensor_tensor(x, x, s_z[:, f, :], ALU.mult).then_inc(s_yz, 1)
                    if n % 8 == 5 and n // 8 + 1 < NGRP:
                        products(n // 8 + 1)
                    for g in range(NGRP):
                        q = n - 14 - 8 * g
                        if 0 <= q < 2:
                            dve.wait_ge(s_root, g + 1)
                            part = rstd[:, q * 256:(q + 1) * 256]
                            dve.reciprocal(part, part).then_inc(s_rec, 1)
                        q = n - 16 - 8 * g
                        if 0 <= q < 4:
                            f = 4 * g + q
                            dve.wait_ge(s_rec, 2 * g + 2)
                            dve.wait_ge(s_yz, 4 * g + 4)
                            dve.scalar_tensor_tensor(s_xbc[:, 8 + f, :], s_xbc[:, 8 + f, :], col("ssm_norm", f), rstd[:],
                                                     ALU.mult, ALU.mult).then_inc(s_yn, 1)
                        q = n - 17 - 8 * g
                        if 0 <= q < 4:
                            low(4 * g + q)
                residual(ST["ssm_out"], new_x(nxt[s]))

            def conf(s):
                st = ST["pw1"]
                norm_recip()
                nst = CONVW - CPE
                for q in range(2):
                    step(dve.memset(c_u[:, q, 0:CONVW - 1], 0.0))
                step(dve.memset(acc[:], 0.0))

                def gated(p, q):
                    b0 = st.chunk0 + 2 * q
                    dve.wait_ge(w_used, SLOTS + st.slab0 + 2 * p + 1)
                    dve.tensor_tensor(c_a[:, q, :], bank[b0 % BANKS][:], rstd[:], ALU.mult).then_inc(bank_free, 1)
                    dve.wait_ge(w_used, SLOTS + st.slab0 + 2 * p + 2)
                    dve.tensor_tensor(c_g[:, q, :], bank[(b0 + 1) % BANKS][:], rstd[:], ALU.mult).then_inc(bank_free, 1)

                def entered(p, q):
                    dve.wait_ge(c_sig, p + 1)
                    dve.wait_ge(c_pe, p + 1)
                    dve.scalar_tensor_tensor(c_u[:, q, CONVW - 1:], c_a[:, q, :], col("pw1_b", 2 * p), c_g[:, q, :],
                                             ALU.add, ALU.mult).then_inc(c_new, 1)

                with dve.Fori(0, KD // 2) as i:
                    for q in range(2):
                        gated(2 * i + q, q)
                    for q in range(2):
                        entered(2 * i + q, q)
                    k0 = c_steps(1) * 2 * i
                    dve.wait_ge(c_new, 2 * i + 2)
                    for n in range(nst):
                        for q in range(2):
                            p, tap = 2 * i + q, CPE + n
                            w, src, y = col("dw_w", CONVW * p + tap), c_u[:, q, tap:tap + S], row(c_y, p)
                            if n == 0:
                                dve.tensor_scalar(y, src, w, col("dw_b", p), ALU.mult, ALU.add).then_inc(c_step, 1)
                            else:
                                dve.wait_ge(c_step, k0 + 2 * n + q - 1)
                                dve.scalar_tensor_tensor(y, src, w, y, ALU.mult, ALU.add).then_inc(c_step, 1)
                    for q in range(2):
                        p = 2 * i + q
                        dve.wait_ge(c_pe, 2 + p + 1)
                        dve.wait_ge(c_step, k0 + 2 * nst - 1 + q)
                        dve.tensor_tensor(row(c_y, p), bank[5 + q][:], row(c_y, p), ALU.add).then_inc(c_out, 1)
                    for q in range(2):
                        dve.wait_ge(c_out, 2 + 2 * i + q + 1)
                        if q:
                            dve.wait_ge(c_step, k0 + 2 * nst + 1)
                        dve.tensor_tensor(acc[:], acc[:], row(c_y, 2 * i + q), ALU.add).then_inc(c_step, 1)
                    dve.wait_ge(c_step, k0 + 2 * nst + 2)
                chunk = mem_kv(0)
                dve.wait_ge(c_mrow, 1)
                step(dve.memset(acc[:], 0.0))
                for c in range(KD):
                    dve.tensor_tensor(c_y[:, c, :], c_y[:, c, :], c_mean[:], ALU.subtract).then_inc(c_cent, 1)
                    if c:
                        dve.wait_ge(c_csq, c)
                        dve.wait_ge(c_cacc, c - 1)
                        dve.tensor_tensor(acc[:], acc[:], sq[:, (c - 1) % 2, :], ALU.add).then_inc(c_cacc, 1)
                    if c >= 6:
                        chunk(c - 6)
                dve.wait_ge(c_csq, KD)
                dve.wait_ge(c_cacc, KD - 1)
                dve.tensor_tensor(acc[:], acc[:], sq[:, (KD - 1) % 2, :], ALU.add).then_inc(c_cacc, 1)
                chunk(2)
                chunk(3)
                dve.wait_ge(c_mrow, 2)
                step(dve.reciprocal(c_mean[:], c_mean[:]))

                def low(c):
                    dve.wait_ge(a_oh, ag[0] + c + 1)
                    dve.tensor_tensor(ol[:, c, :], c_s[:, c % 2, :], oh[:, c, :].bitcast(F32), ALU.subtract)\
                        .then_inc(a_ol, 1)
                for c in range(KD):
                    dve.tensor_tensor(c_y[:, c, :], c_y[:, c, :], c_mean[:], ALU.mult).then_inc(c_norm, 1)
                    if c:
                        low(c - 1)
                    chunk(4 + c)
                low(KD - 1)
                for c in range(12, 16):
                    chunk(c)
                ag[0] += KD
                residual(ST["pw2"], new_x(nxt[s]), "pw2_b")

            def attn(s):
                st = ST["attn_in"]
                dve.wait_ge(rel_in, 16)
                step(dve.tensor_scalar(rel_row[:, 383:767], rel_row[:, 383:767], 8.0, None, ALU.mult))
                dve.tensor_copy(rel_row[:, 0:383], rel_row[:, 383:384].broadcast_to([8, 383])).then_inc(rel_ready, 1)
                norm_recip()

                def raw(c, j):
                    b = bank[(st.chunk0 + j) % BANKS]
                    dve.wait_ge(w_used, SLOTS + st.slab0 + c + 1)
                    if isinstance(c, int) and c >= 13:
                        if c >= 15:
                            dve.wait_ge(v_turned, c - 14)
                        dst = v_tmp[:, c % 2, :]
                    else:
                        dst = qk[:, ds(c, 1), :].rearrange("p a n -> p (a n)")
                    dve.tensor_tensor(dst, b[:], rstd[:], ALU.mult).then_inc(bank_free, 1)

                def fin(c, j):
                    if isinstance(c, int) and c >= 13:
                        return
                    rt = q_root_t[:, j % 2, :]
                    dve.wait_ge(q_root, c + 1)
                    dve.reciprocal(rt, rt).then_inc(q_rec, 1)
                    dve.wait_ge(q_rec, c + 1)
                    g = gq[c] if isinstance(c, int) else None
                    dst = qk[:, ds(c, 1), :].rearrange("p a n -> p (a n)")
                    dve.scalar_tensor_tensor(dst, dst, cols[:, ds(COL["g_qk"] + (c if not isinstance(c, int) else c), 1)],
                                             rt, ALU.mult, ALU.mult).then_inc(q_ready, 1)
                gq = list(range(13))

                def chunk(c, j, i):
                    raw(c, j)
                    if j >= 1:
                        fin(c - 1, j - 1)
                    if j == 3 or (isinstance(c, int) and c == 17):
                        fin(c, j)
                each(dve, 18, chunk, peel=4, tail=6)
                vt[0] += 5
                dve.wait_ge(q_ready, 13)
                attention(*UNITS["attn"])
                residual(ST["attn_out"], new_x(nxt[s]))

            def ffn(si, so, s, conv):
                norm_recip()
                st = ST[si]
                if conv:
                    dve.memset(f_g[:, 0:2], 0.0).then_inc(dve_step, 1)
                    steps[0] += 1
                    dve.wait_ge(dve_step, steps[0])
                f0 = ffns[0]
                ffns[0] += KF

                def pairs(i, jj):
                    p = i * 2 + jj
                    bg, bu = bank[(st.chunk0 + 2 * jj) % BANKS], bank[(st.chunk0 + 2 * jj + 1) % BANKS]
                    dve.wait_ge(w_used, SLOTS + st.slab0 + 2 * p + 1)
                    dve.tensor_tensor(f_g[:, 2:S + 2], bg[:], rstd[:], ALU.mult).then_inc(bank_free, 1)
                    if conv:
                        dve.wait_ge(f_tap, conv[3] * KF + p + 1)
                        dve.scalar_tensor_tensor(f_y[:], f_g[:, 1:S + 1], col(conv[0], 3 * p + 1), f_y[:],
                                                 ALU.mult, ALU.add).then_inc(f_conv, 1)
                        dve.wait_ge(f_conv, conv[3] * 2 * KF + 2 * p + 1)
                        dve.scalar_tensor_tensor(f_y[:], f_g[:, 0:S], col(conv[0], 3 * p), f_y[:],
                                                 ALU.mult, ALU.add).then_inc(f_conv, 1)
                    dve.wait_ge(w_used, SLOTS + st.slab0 + 2 * p + 2)
                    dve.tensor_tensor(f_u[:], bu[:], rstd[:], ALU.mult).then_inc(bank_free, 1)
                    dve.wait_ge(bank_free, BANKS + st.chunk0 + 2 * p + 2)
                    dve.wait_ge(f_silu, f0 + p + 1)
                    dve.tensor_tensor(f_h[:], f_y[:], f_u[:], ALU.mult).then_inc(f_prod, 1)
                    dve.wait_ge(f_hi, f0 + p + 1)
                    dve.tensor_tensor(hl[:, ds(p, 1), :].rearrange("p a n -> p (a n)"), f_h[:],
                                      hh[:, ds(p, 1), :].rearrange("p a n -> p (a n)").bitcast(F32),
                                      ALU.subtract).then_inc(f_lo, 1)

                with dve.Fori(0, KF // 2) as i:
                    for jj in range(2):
                        pairs(i, jj)
                residual(ST[so], new_x(nxt[s]))

            def xt_(c):
                return xt[:, ds(c, 1), :].rearrange("p a n -> p (a n)")

            def xh_(c):
                return xh[:, ds(c, 1), :].rearrange("p a n -> p (a n)")

            def xl_(c):
                return xl[:, ds(c, 1), :].rearrange("p a n -> p (a n)")

            ffns = [0]
            dve.sem_inc(bank_free, BANKS)
            dve.sem_inc(w_split, SLOTS)
            dve.sem_inc(w_used, SLOTS)
            dve.sem_inc(v_ready, 2)
            dve.sem_inc(r_done, 2)
            dve.sem_inc(c_out, 2)
            dve.sem_inc(c_pe, 2)
            zero_acc()
            dve.wait_ge(init_done, 5)
            dve.tensor_copy(ident_b[:], ident[:]).then_inc(cst_ready, 1)
            if set(stages) & {"attn", "diff", "ssm"}:
                dve.wait_ge(cst_in, 16)
                dve.tensor_copy(masks_b[:], cst[:, 0:3 * P].rearrange("p (a n) -> p a n", a=3)).then_inc(cst_ready, 1)
                dve.tensor_copy(head_ones[:], cst[:, 3 * P:4 * P]).then_inc(cst_ready, 1)
                dve.tensor_copy(alibi_b[:], cst[:, 4 * P:].rearrange("p (a n) -> p a n", a=8)).then_inc(cst_ready, 1)
            dve.wait_ge(const_in, 16)

            def start_chunk(c, j, i):
                add_square(c, j)
                split_x(c, c, GAIN[stages[0]])
            each(dve, KD, start_chunk)
            nconv = 0
            for s in stages:
                if s == "attn":
                    attn(s)
                elif s.startswith("mem"):
                    mem(int(s[3]), s)
                elif s == "diff":
                    diff(s)
                elif s == "conf":
                    conf(s)
                elif s == "ssm":
                    ssm(s)
                elif s.startswith("ffn"):
                    ffn("ffn_in" + s[3], "ffn_out" + s[3], s, ("ffn_w" + s[3], "ffn_b" + s[3], None, nconv))
                    nconv += 1
                elif s.startswith("glu"):
                    ffn("glu_in" + s[3], "glu_out" + s[3], s, None)
                elif s == "final":
                    norm_recip()
                    for c in range(KD):
                        dve.scalar_tensor_tensor(xt[:, c, :], xt[:, c, :], col("norm_final", c), rstd[:],
                                                 ALU.mult, ALU.mult).then_inc(out_ready, 1)

        @block.scalar
        def _(act):
            nrm = [0]
            ffns = [0]
            nconv = [0]

            def xt_(c):
                return xt[:, ds(c, 1), :].rearrange("p a n -> p (a n)")

            def xh_(c):
                return xh[:, ds(c, 1), :].rearrange("p a n -> p (a n)")

            def prepare_x(ready, k0, gain):
                def chunk(c, j, i):
                    ready(c)
                    act.wait_ge(x_acc, k0 + c - 1) if (not isinstance(c, int) or k0 + c > 1) else None
                    act.activation(sq[:, j % 2, :], xt_(c), ACT.Square).then_inc(x_sq, 1)
                    act.activation(xh_(c), xt_(c), ACT.Copy, scale=col(gain, c)).then_inc(x_hi, 1)
                return chunk

            def half(s, slot, rounds):
                act.wait_ge(w_landed[slot], 16 * rounds)
                act.wait_ge(w_used, s + 1)
                act.activation(w_hi[:, slot, :], w_raw[:, slot, :], ACT.Copy).then_inc(w_half, 1)

            def next_half(st, j, i):
                for t in range(st.per):
                    o = st.slab0 + j * st.per + t + SLOTS
                    if isinstance(i, int) and o + 4 * st.per * i >= SLABS:
                        continue
                    half(o + 4 * st.per * i, o % SLOTS, o // SLOTS + 1 + i * st.per)

            def residual(st, gain):
                k0 = KD * nrm[0]

                def chunk(c, j, i):
                    act.wait_ge(bank_free, BANKS + st.chunk0 + c + 1)
                    next_half(st, j, i)
                    body(c, j, i)
                body = prepare_x(lambda c: None, k0, gain)
                each(act, KD, chunk, peel=KD if st.slab0 + st.chunks * st.per == SLABS else 0)

            def norm_root(k=None):
                nrm[0] += 1
                act.wait_ge(nrm_sum, nrm[0])
                act.activation(root, NORM_BANK[:], ACT.Sqrt, scale=1.0 / D, bias=eps[:, 0:1]).then_inc(nrm_root, 1)

            def attention(units, groups, peers=1, out=None, oh_lag=4):
                U = len(units)
                u0, t0, g0 = au[0], at[0], ag[0]
                ends = {last: (g, chunks) for g, (_, last, chunks) in enumerate(groups)}
                nch = len(groups[0][2])
                for s_ in range(U + 5 if out is None else U + 12):
                    for lag, do in out or ():
                        if s_ - lag in ends:
                            do(ends[s_ - lag][0])
                    if s_ < U:
                        u, cs = units[s_], slice(s_, s_ + 1)
                        act.wait_ge(a_max, u0 + s_ + 1)
                        if s_ >= PROBS:
                            act.wait_ge(a_turn, t0 + (s_ - PROBS) // peers + 1)
                        if u.sink is not None:
                            act.activation(a_stat[:, 3, cs], u.sink, ACT.Exp, bias=a_stat[:, 1, cs]).then_inc(a_aux, 1)
                        act.activation(a_prob_t[:, s_ % PROBS, 0:u.nk], bank[s_ % 3][:, 0:u.nk], ACT.Exp,
                                       bias=a_stat[:, 1, cs], scale=u.scale, accum_out=a_stat[:, 2, cs])\
                            .then_inc(a_exp, 1)
                        if u.rel is not None and s_ % NT == NT - 1 and u.rel + 2 < 8:
                            load_rel(u.rel + 2, u0 + s_ + 1)
                    r = s_ - TURN_LAG
                    if 0 <= r < U and (r + 1) % peers == 0:
                        u, k = units[r], r // peers
                        act.wait_ge(a_turn, t0 + k + 1)
                        if k >= 2:
                            act.wait_ge(a_pv, t0 + k - 1)
                        act.activation(a_pt_t[:, k % 2, 0:u.nk], bank[3 + k % 2][:, 0:u.nk], ACT.Copy)\
                            .then_inc(a_pt, 1)
                    if s_ - TURN_LAG - 1 in ends and out is None:
                        g, chunks = ends[s_ - TURN_LAG - 1]
                        last = groups[g][1]
                        act.wait_ge(a_pv, t0 + last // peers)
                        for ch in chunks:
                            act.activation(oh[:, ch, :], bank[5 + ch % 2][:], ACT.Copy).then_inc(a_oh, 1)
                au[0] += U
                at[0] += U // peers
                ag[0] += len(groups) * nch
            au, at, ag = [0], [0], [0]
            a_aux = sem("a_aux")
            vt = [0]

            def row(t, c):
                return t[:, c, :] if isinstance(c, int) else t[:, ds(c, 1), :].rearrange("p a n -> p (a n)")

            def value(dst, v, vc, j, n):
                act.wait_ge(v_turned, v + 1)
                act.activation(dst[:, :, ds(vc * P, P)], bank[5 + j % 2][:, 0:n].rearrange("p (a n) -> p a n", n=P),
                               ACT.Copy).then_inc(v_ready, 1)

            def mem_kv(l, before):
                kv = ST[f"mem_kv{l}"]
                v0 = vt[0]
                vt[0] += KD
                act.wait_ge(w_used, SLOTS + before)
                act.dma_start(m_in[:], A["memt"]).then_inc(m_landed, 16)
                act.wait_ge(m_landed, 16 * kv_round(l))
                act.activation(m_hi[:], m_in[:], ACT.Copy).then_inc(m_half, 1)

                def chunk(c):
                    next_half(kv, c % 4, c // 4)
                    if c > KD:
                        value(m_v, v0 + c - KD - 1, c - KD - 1, (c - 1) % 4, M)
                    if c == 2 * KD - 1:
                        value(m_v, v0 + KD - 1, KD - 1, c % 4, M)
                return chunk

            def mem(l, s):
                q = ST[f"mem_q{l}"]
                norm_root()
                each(act, KD, lambda c, j, i: next_half(q, j, i))
                attention(*UNITS["mem"])
                residual(ST[f"mem_out{l}"], GAIN[nxt[s]])

            def diff(s):
                kv, q = ST["diff_kv"], ST["diff_q"]
                ang, turns = d_t[:, 0, :], d_t[:, 1, :]
                act.dma_start(pos_i, A["pos"].broadcast_to([P, S])).then_inc(tab_in, 16)
                act.dma_start(freq[:], A["freq"]).then_inc(tab_in, 16)
                act.dma_start(rot[:], A["rot"]).then_inc(tab_in, 16)
                act.dma_start(d_q[:, 0, 0:256], A["lam"].broadcast_to([P, 256])).then_inc(lam_in, 16)
                act.wait_ge(tab_red, 1)
                act.activation(sine[:], ang, ACT.Sin).then_inc(tab_sin, 1)
                act.activation(turns, ang, ACT.Sin, scale=0.5).then_inc(tab_sin, 1)
                act.wait_ge(lam_sum, 1)
                act.activation(lam_e[:, 2:4], lam_e[:, 0:2], ACT.Exp).then_inc(lam_exp, 1)
                v0 = vt[0]

                def key(c, j, i):
                    next_half(kv, j, i)
                    if isinstance(c, int) and c == 0:
                        norm_root()
                each(act, KD, key, peel=4)

                def chunk(c, j, i):
                    next_half(kv, j, i)
                    lagged(lambda c, j: value(d_v, v0 + c - KD, c - KD, j, S), 15)(c, j)
                each(act, 2 * KD, chunk, start=KD)
                vt[0] += KD
                act.wait_ge(w_used, SLOTS + kv.slab0 + 2 * KD)
                for c in range(KD):
                    act.activation(xh[:, c, :], xt[:, c, :], ACT.Copy, scale=col("norm_mix2_1", c)).then_inc(y_hi, 1)
                each(act, KD, lambda c, j, i: next_half(q, j, i))
                chunk = mem_kv(1, q.slab0 + KD)

                def square(g):
                    act.wait_ge(o_raw, g + 1)
                    act.activation(sq[:, g % 2, :], d_q[:, g, :], ACT.Square).then_inc(o_sq, 1)

                def rooted(g):
                    act.wait_ge(o_sum, g + 1)
                    act.activation(rstd[:], NORM_BANK[:], ACT.Sqrt, scale=1.0 / P, bias=eps[:, 1:2]).then_inc(o_root, 1)

                def upper(g):
                    act.wait_ge(o_new, g + 1)
                    act.activation(oh[:, g, :], d_q[:, g, :], ACT.Copy, scale=1.0 - LAMBDA_INIT)\
                        .then_inc(a_oh, 1)
                attention(*UNITS["diff"], peers=2, out=((5, square), (7, rooted), (11, upper)))
                for c in range(2 * KD):
                    chunk(c)
                residual(ST["diff_out"], GAIN[nxt[s]])

            def ssm(s):
                st = ST["ssm_in"]
                norm_root()
                t = lambda n: s_dt[:, n, :]
                act.activation(t(5)[:, 0:1], col("ssm_alog")[0:32], ACT.Exp).then_inc(s_e, 1)

                def taps(c, j, i):
                    act.wait_ge(bank_free, BANKS + st.chunk0 + c + 1)
                    next_half(st, j, i)
                    if isinstance(c, int) and c == 0:
                        act.wait_ge(s_e0, 1)
                        act.activation(t(1), t(1), ACT.Exp, scale=-1.0).then_inc(s_e, 1)
                        act.wait_ge(s_e0, 2)
                        for c in range(NT):
                            cs = slice(c * P, (c + 1) * P)
                            act.activation(t(1)[:, cs], s_acs[:, cs], ACT.Exp, scale=-1.0,
                                           bias=s_acs[:, (c + 1) * P - 1:(c + 1) * P]).then_inc(s_e, 1)
                        act.activation(s_acs_h[:], s_acs, ACT.Copy).then_inc(s_split, 1)
                        act.activation(s_one[:], ident[0:32, 0:32], ACT.Copy).then_inc(s_split, 1)
                        return
                    q = c - 1
                    y = s_ea[:, j % 2, :]
                    act.activation(y, s_pad[:, 3:S + 3], ACT.Identity, scale=col("ssm_cw", 4 * q + 3),
                                   bias=col("ssm_cb", q)).then_inc(s_tap, 1)
                    act.wait_ge(s_conv, 3 * q + 3)
                    act.activation(row(s_xbc, c - 1), y, ACT.Silu).then_inc(s_xbc_done, 1)

                def gate(c, j, i):
                    act.wait_ge(bank_free, BANKS + st.chunk0 + c + 1)
                    next_half(st, j, i)
                    z = row(s_z, c - 25)
                    act.activation(z, z, ACT.Silu).then_inc(s_zd, 1)
                each(act, 25, taps, peel=4)
                each(act, 41, gate, start=25, peel=3)
                act.wait_ge(s_tp, 1)
                act.activation(s_el[:].rearrange("p a n -> p (a n)"), bank[4][:, 3 * P:4 * P], ACT.Exp).then_inc(s_eld, 1)

                def copied(g, r):
                    act.wait_ge(s_turn, 5 * g + r + 1)
                    if r < 4:
                        if g >= 2 and r == 0:
                            act.wait_ge(s_y, 8 * (g - 1))
                        dst = s_xt[:, g % 2, :, r * P:(r + 1) * P]
                    else:
                        act.wait_ge(s_cbp, g + 1)
                        dst = s_xbc[:, g:g + 1, :].rearrange("p a (b n) -> p (a b) n", n=P)
                    act.activation(dst, bank[5 + r % 2][:].rearrange("p (a n) -> p a n", n=P), ACT.Copy)\
                        .then_inc(s_copied, 1)
                for r in range(5):
                    copied(0, r)
                for n in range(SSMH + 14 + 4):
                    if n < SSMH:
                        act.wait_ge(s_bc, n + 1)
                        if n >= 3:
                            act.wait_ge(s_y, n - 2)
                        act.activation(s_ea[:, n % 3, :], bank[n % 2][:], ACT.Exp).then_inc(s_exp, 1)
                    k = n - 1
                    if 0 <= k < SSMH:
                        act.wait_ge(s_mask, k + 1)
                        if k >= 3:
                            act.wait_ge(s_y, k - 2)
                        for t in range(NT):
                            cs = slice(t * P, (t + 1) * P)
                            ins = act.activation(s_dk[:, k % 3, cs], bank[k % 2][:, cs], ACT.Exp,
                                                 bias=s_tok[:, 1, t, k:k + 1])
                        ins.then_inc(s_dec, 1)
                    g, r = n // 8, n % 8 - 1
                    if g + 1 < NGRP and 0 <= r < 5:
                        copied(g + 1, r)
                    f = (n - 5) // 2
                    if n % 2 == 1 and 0 <= f < KI:
                        act.wait_ge(s_yz, f + 1)
                        if f >= 2:
                            act.wait_ge(s_sum, f - 1)
                        act.activation(sq[:, f % 2, :], s_xbc[:, 8 + f, :], ACT.Square).then_inc(s_sq, 1)
                    for g in range(NGRP):
                        if n == 13 + 8 * g:
                            act.wait_ge(s_sum, 4 * g + 4)
                            if g:
                                act.wait_ge(s_yn, 4 * g)
                            act.activation(rstd[:], NORM_BANK[:], ACT.Sqrt, scale=4.0 / DIN, bias=eps[:, 0:1])\
                                .then_inc(s_root, 1)
                        q = n - 16 - 8 * g
                        if 0 <= q < 4:
                            f = 4 * g + q
                            act.wait_ge(s_yn, f + 1)
                            act.activation(yh[:, f, :], s_xbc[:, 8 + f, :], ACT.Copy).then_inc(s_yh, 1)
                residual(ST["ssm_out"], GAIN[nxt[s]])

            def conf(s):
                st = ST["pw1"]
                norm_root()

                def diag(p, q):
                    act.wait_ge(c_pe, p + 1)
                    for n in range(CPE):
                        act.activation(c_diag[:, 2 * q + n // 4, n % 4, :], ident[:], ACT.Copy,
                                       scale=col("dw_w", CONVW * p + n)).then_inc(c_dia, 1)

                def turn(i):
                    for j in range(4):
                        next_half(st, j, i)
                    for q in range(2):
                        p = 2 * i + q
                        act.wait_ge(bank_free, BANKS + st.chunk0 + 2 * p + 2)
                        act.activation(c_g[:, q, :], c_g[:, q, :], ACT.Sigmoid, bias=col("pw1_b", 2 * p + 1))\
                            .then_inc(c_sig, 1)
                    for q in range(2):
                        diag(2 * i + q, q)
                turn(0)
                with act.Fori(1, KD // 2) as i:
                    turn(i)
                chunk = mem_kv(0, st.slab0 + 2 * KD)
                act.wait_ge(c_msum, 1)
                act.activation(c_mean[:], NORM_BANK[:], ACT.Copy, scale=1.0 / D).then_inc(c_mrow, 1)
                for c in range(KD):
                    act.wait_ge(c_cent, c + 1)
                    if c >= 2:
                        act.wait_ge(c_cacc, c - 1)
                    act.activation(sq[:, c % 2, :], c_y[:, c, :], ACT.Square).then_inc(c_csq, 1)
                for c in range(3):
                    chunk(c)
                act.wait_ge(c_msum, 2)
                act.activation(c_mean[:], NORM_BANK[:], ACT.Sqrt, scale=1.0 / D, bias=eps[:, 1:2]).then_inc(c_mrow, 1)
                chunk(3)
                for c in range(KD):
                    act.wait_ge(c_norm, c + 1)
                    if c >= 2:
                        act.wait_ge(a_ol, ag[0] + c - 1)
                    act.activation(c_s[:, c % 2, :], c_y[:, c, :], ACT.Silu, scale=col("ln_g", c), bias=col("ln_b", c))\
                        .then_inc(c_silu, 1)
                    act.wait_ge(c_silu, c + 1)
                    act.activation(oh[:, c, :], c_s[:, c % 2, :], ACT.Copy).then_inc(a_oh, 1)
                    if c >= 1:
                        chunk(3 + c)
                for c in range(11, 16):
                    chunk(c)
                ag[0] += KD
                residual(ST["pw2"], GAIN[nxt[s]])

            def load_rel(h, after):
                if after is not None:
                    act.wait_ge(a_score, after)
                src = bass.AP(rel_dram, h * 767, [[1, P], [1, 640]])
                act.dma_start(rel[:, h % 2, :], src).then_inc(rel_buf[h % 2], 16)

            def attn(s):
                st = ST["attn_in"]
                norm_root()
                act.wait_ge(rel_ready, 1)
                act.dma_start(rel_dram[:, :], rel_row[:]).then_inc(rel_out, 16)

                def fin(c, j):
                    if isinstance(c, int) and c >= 13:
                        v = c - 13
                        act.wait_ge(v_turned, v + 1)
                        dst = v_tok[:, :, 512:640] if v == 0 else v_tok[:, :, (v - 1) * P:v * P]
                        act.activation(dst, bank[5 + c % 2][:].rearrange("p (a n) -> p a n", a=NT), ACT.Copy)\
                            .then_inc(v_ready, 1)
                        return
                    act.wait_ge(q_sum, c + 1)
                    if not isinstance(c, int) or c >= 2:
                        act.wait_ge(q_ready, c - 1)
                    act.activation(q_root_t[:, j % 2, :], bank[5 + j % 2][:], ACT.Sqrt, scale=1.0 / 64,
                                   bias=eps[:, 0:1]).then_inc(q_root, 1)

                def chunk(c, j, i):
                    act.wait_ge(bank_free, BANKS + st.chunk0 + c + 1)
                    next_half(st, j, i)
                    if not (isinstance(c, int) and c >= 13):
                        if not isinstance(c, int) or c >= 2:
                            act.wait_ge(q_sum, c - 1)
                        act.activation(sq[:, j % 2, :], qk[:, ds(c, 1), :].rearrange("p a n -> p (a n)"),
                                       ACT.Square).then_inc(q_sq, 1)
                    if j >= 1:
                        fin(c - 1, j - 1)
                    if j == 3 or (isinstance(c, int) and c == 17):
                        fin(c, j)
                each(act, 18, chunk, peel=4, tail=6)
                vt[0] += 5
                act.wait_ge(rel_out, 16)
                act.wait_ge(sink_in, 16)
                load_rel(0, None)
                load_rel(1, None)
                attention(*UNITS["attn"])
                residual(ST["attn_out"], GAIN[nxt[s]])

            def ffn(si, so, s, conv):
                norm_root()
                f0 = ffns[0]
                ffns[0] += KF
                with act.Fori(0, KF // 2) as i:
                    for jj in range(2):
                        p = i * 2 + jj
                        act.wait_ge(bank_free, BANKS + ST[si].chunk0 + 2 * p + 1)
                        next_half(ST[si], 2 * jj, i)
                        if conv:
                            act.activation(f_y[:], f_g[:, 2:S + 2], ACT.Identity, bias=col(conv[1], p),
                                           scale=col(conv[0], 3 * p + 2)).then_inc(f_tap, 1)
                            act.wait_ge(f_conv, conv[3] * 2 * KF + 2 * p + 2)
                            act.activation(f_y[:], f_y[:], ACT.Silu).then_inc(f_silu, 1)
                        else:
                            act.activation(f_y[:], f_g[:, 2:S + 2], ACT.Silu).then_inc(f_silu, 1)
                        act.wait_ge(f_prod, f0 + p + 1)
                        act.activation(hh[:, ds(p, 1), :].rearrange("p a n -> p (a n)"), f_h[:], ACT.Copy)\
                            .then_inc(f_hi, 1)
                        next_half(ST[si], 2 * jj + 1, i)
                residual(ST[so], GAIN[nxt[s]])

            act.dma_start(cols[:], A["cols"]).then_inc(const_in, 16)
            if set(stages) & {"attn", "diff", "ssm"}:
                act.dma_start(cst[:], A["cst"]).then_inc(cst_in, 16)
            if "attn" in stages:
                act.dma_start(rel_row[:, 383:767], A["rel_rev"][:, 0:384]).then_inc(rel_in, 16)
                act.dma_start(sink_c[:], A["sinks"].rearrange("(a n) -> a n", a=1).broadcast_to([P, 8]))\
                    .then_inc(sink_in, 16)
            for c in range(KD):
                act.dma_start(xt[:, c, :], A["xt"][c]).then_inc(x_in, 16)
            act.wait_ge(const_in, 16)
            act.wait_ge(x_in, 16 * KD)
            for t in range(min(SLOTS, SLABS)):
                half(t, t, 1)
            each(act, KD, prepare_x(lambda c: None, 0, GAIN[stages[0]]), peel=4)
            k = 0
            for s in stages:
                if s == "attn":
                    attn(s)
                elif s.startswith("mem"):
                    mem(int(s[3]), s)
                elif s == "diff":
                    diff(s)
                elif s == "conf":
                    conf(s)
                elif s == "ssm":
                    ssm(s)
                elif s.startswith("ffn"):
                    ffn("ffn_in" + s[3], "ffn_out" + s[3], s, ("ffn_w" + s[3], "ffn_b" + s[3], None, k))
                    k += 1
                elif s.startswith("glu"):
                    ffn("glu_in" + s[3], "glu_out" + s[3], s, None)
                elif s == "final":
                    norm_root()
                    for c in range(KD):
                        act.wait_ge(out_ready, c + 1)
                        act.dma_start(out[c], xt[:, c, :]).then_inc(out_done, 16)
                    act.wait_ge(out_done, 16 * KD)


def pack(w):
    k, n = w.shape
    return np.ascontiguousarray(w.reshape(k // P, P, n // P, P).transpose(2, 1, 0, 3)).reshape(n // P, P, k)


def fcol(v):
    return np.ascontiguousarray(np.asarray(v).reshape(-1, P).T)


def interleave(w, half):
    k = w.shape[0]
    return np.ascontiguousarray(w.reshape(k, 2, half // P, P).transpose(0, 2, 1, 3)).reshape(k, 2 * half)


EXTRA = {"ssm": ("cst",), "attn": ("cst", "rel_rev", "sinks"), "conf": ("memt",), "diff": ("memt", "cst", "pos", "freq", "rot", "lam")}


def constants():
    p, m = np.arange(P)[:, None], np.arange(P)[None, :]
    chunk = np.where((p < 64) & (m >= 64), MASKED, 0.0)
    causal = np.where(m > p, MASKED, 0.0)
    decay = np.where(m < p, MASKED, 0.0)
    heads = (p // 64 == m // 64) * 1.0
    m = np.arange(256)[None, :]
    gone = ((p < 64) & (m >= 192)) | ((p >= 64) & (m < 64))
    alibi = [np.where(gone, MASKED, -8.0 * 2.0 ** -(h + 1) * np.abs(p - m + P)) for h in range(8)]
    return np.concatenate([chunk, causal, decay, heads] + alibi, 1).astype(np.float32)


def rotary():
    freq = np.zeros((P, 1), np.float32)
    rot = np.zeros((P, P), np.float32)
    for base in (0, 64):
        for i in range(8):
            freq[base + i] = freq[base + 8 + i] = 500000.0 ** (-i / 8)
            rot[base + 8 + i, base + i] = -1.0
            rot[base + i, base + 8 + i] = 1.0
    return freq, rot


def attn_in_cols(w):
    qa, ka, va, qb, kb, vb = np.split(w, [512, 1024, 1536, 2048, 2176], axis=1)
    qb = qb.reshape(-1, 2, 4, 64).transpose(0, 2, 1, 3).reshape(-1, 512)
    return np.concatenate([qa, ka, qb, kb, vb, va], 1)


def layout(I):
    A = {}
    A["cst"] = constants()
    A["rel_rev"] = np.ascontiguousarray(I["relpos_table"][0][:, ::-1])
    A["sinks"] = np.ascontiguousarray(I["sinks"][0])
    A["w_attn_in"] = pack(attn_in_cols(I["attn_w_in"][0]))
    wo = I["attn_w_out"][0]
    A["w_attn_out"] = pack(np.concatenate(
        [wo[:512], wo[512:].reshape(2, 4, 64, D).transpose(1, 0, 2, 3).reshape(512, D)], 0))
    A["xt"] = np.ascontiguousarray(np.asarray(I["x"])[0].T).reshape(KD, P, S)
    A["memt"] = np.ascontiguousarray(np.asarray(I["mem_2"])[0].T.reshape(KD, P, M).transpose(1, 0, 2))
    for l in range(2):
        A[f"w_mem_kv{l}"] = pack(np.concatenate([I["mem_w_k_2"][l], I["mem_w_v_2"][l]], 1))
        A[f"w_mem_q{l}"] = pack(I["mem_w_q_2"][l])
        A[f"w_mem_out{l}"] = pack(I["mem_w_o_2"][l])
    A["w_diff_kv"] = pack(np.concatenate([I["w_k_shared_2"], I["w_v_shared_2"]], 1))
    A["w_diff_q"] = pack(I["diff_w_q_2"][0])
    A["w_diff_out"] = pack(I["diff_w_o_2"][0])
    A["pos"] = np.ascontiguousarray(I["positions_2"])
    A["lam"] = np.stack([I["diff_lambda_q1_2"][0], I["diff_lambda_k1_2"][0], I["diff_lambda_q2_2"][0],
                         I["diff_lambda_k2_2"][0]]).reshape(1, 256)
    A["freq"], A["rot"] = rotary()
    A["w_pw1"] = pack(interleave(I["conv_w_pw1_2"][0], D))
    A["w_pw2"] = pack(I["conv_w_pw2_2"][0])
    z, xs, bc, dt = np.split(I["ssm_w_in"][0], [DIN, 2 * DIN, 2 * DIN + 2 * NGRP * NSTATE], axis=1)
    A["w_ssm_in"] = pack(np.concatenate([dt, np.zeros((D, P - SSMH), np.float32), bc, xs, z], 1))
    A["w_ssm_out"] = pack(I["ssm_w_out"][0])
    c = {}
    turned = lambda a: np.concatenate([a[..., DIN:], a[..., :DIN]], -1)
    c["ssm_cw"] = np.ascontiguousarray(turned(I["ssm_conv_w"][0]).reshape(4, 24, P).transpose(2, 1, 0)).reshape(P, -1)
    c["ssm_cb"] = fcol(turned(I["ssm_conv_b"][0]))
    c["ssm_d"] = fcol(np.repeat(I["ssm_d"][0], 64))
    c["ssm_norm"] = fcol(I["ssm_norm"][0])
    on_heads = lambda v: np.concatenate([v, np.zeros(P - SSMH, np.float32)])[:, None]
    c["ssm_dtb"] = on_heads(I["ssm_dt_bias"][0])
    c["ssm_alog"] = on_heads(I["ssm_a_log"][0])
    c["pw1_b"] = fcol(I["conv_b_pw1_2"][0].reshape(2, KD, P).transpose(1, 0, 2).reshape(-1))
    c["dw_w"] = np.ascontiguousarray(I["conv_w_dw_2"][0].reshape(CONVW, KD, P).transpose(2, 1, 0)).reshape(P, -1)
    c["dw_b"] = fcol(I["conv_b_dw_2"][0])
    c["ln_g"] = fcol(I["conv_ln_g_2"][0])
    c["ln_b"] = fcol(I["conv_ln_b_2"][0])
    c["pw2_b"] = fcol(I["conv_b_pw2_2"][0])
    c["subln"] = fcol(I["diff_subln_g_2"][0])
    pair = lambda v: np.concatenate([v, v])[:, None]
    c["g_qk"] = np.concatenate([pair(I["q_norm_a"][0])] * 4 + [pair(I["k_norm_a"][0])] * 4
                               + [pair(I["q_norm_b"][0])] * 4 + [pair(I["k_norm_b"][0])], 1)
    for l in range(2):
        c[f"norm_mix{l}"] = fcol(I["norm_mix"][l])
        c[f"norm_ffn{l}"] = fcol(I["norm_ffn"][l])
        A[f"w_ffn_in{l}"] = pack(interleave(I["ffn_w_in"][l], DFF))
        A[f"w_ffn_out{l}"] = pack(I["ffn_w_out"][l])
        c[f"ffn_w{l}"] = np.ascontiguousarray(I["ffn_conv_w"][l].reshape(3, KF, P).transpose(2, 1, 0)).reshape(P, -1)
        c[f"ffn_b{l}"] = fcol(I["ffn_conv_b"][l])
        c[f"norm_mix2_{l}"] = fcol(I["norm_mix_2"][l])
        c[f"norm_mem2_{l}"] = fcol(I["norm_mem_2"][l])
        c[f"norm_ffn2_{l}"] = fcol(I["norm_ffn_2"][l])
        A[f"w_glu_in{l}"] = pack(interleave(np.concatenate([I["ffn_w_gate_2"][l], I["ffn_w_up_2"][l]], 1), DFF))
        A[f"w_glu_out{l}"] = pack(I["ffn_w_down_2"][l])
    c["norm_final"] = fcol(I["norm_final_2"])
    c["kv_norm"] = fcol(I["kv_norm_2"])
    full = np.zeros((P, NCOL), np.float32)
    for name, n in COLUMNS:
        if name in c:
            full[:, COL[name]:COL[name] + n] = c[name]
    A["cols"] = full
    return A


def kernel(**inputs):
    import concourse.bacc as bacc
    from concourse.bass_utils import run_bass_kernel_spmd

    A = layout({name: np.asarray(value) for name, value in inputs.items()})
    nc = bacc.Bacc("TRN2", target_bir_lowering=False, num_devices=1)
    args = {name: nc.dram_tensor(name, a.shape, mybir.dt.from_np(a.dtype), kind="ExternalInput").ap()
            for name, a in A.items()}
    out = nc.dram_tensor("out", (KD, P, S), F32, kind="ExternalOutput").ap()
    build(nc, args, out)
    result = run_bass_kernel_spmd(nc, [A], core_ids=[0])
    return np.ascontiguousarray(result.results[0]["out"].reshape(D, S).T)[None]
```

```python
import math
from contextlib import ExitStack

import numpy as np

import concourse.bass as bass
from concourse import mybir

F32 = mybir.dt.float32
F32R = mybir.dt.float32r
BF16 = mybir.dt.bfloat16
I32 = mybir.dt.int32
ALU = mybir.AluOpType
ACT = mybir.ActivationFunctionType
AX_X = mybir.AxisListType.X
ds = bass.ds

P = 128
S = 512
D = 1024
KD = D // P
NT = S // P
DFF = 2816
KF = DFF // P
DIN = 2048
KI = DIN // P
NGRP = 4
NSTATE = 128
SSMH = 32
M = 256
CONVW = 31
RMS_EPS = 1e-6
LN_EPS = 1e-5
MASKED = -1e30
LAMBDA_INIT = 0.8 - 0.6 * math.exp(-0.3 * 1)

BANKS = 4
SLOTS = 4
SLAB = 8
PROBS = 4

STREAMS = [
    ("attn_in", 18, KD), ("attn_out", KD, KD),
    ("ffn_in0", 2 * KF, KD), ("ffn_out0", KD, KF),
    ("ssm_in", 41, KD), ("ssm_out", KD, KI),
    ("ffn_in1", 2 * KF, KD), ("ffn_out1", KD, KF),
    ("pw1", 2 * KD, KD), ("mem_kv0", 2 * KD, KD), ("pw2", KD, KD),
    ("mem_q0", KD, KD), ("mem_out0", KD, KD),
    ("glu_in0", 2 * KF, KD), ("glu_out0", KD, KF),
    ("diff_kv", 2 * KD, KD), ("diff_q", KD, KD), ("mem_kv1", 2 * KD, KD), ("diff_out", KD, KD),
    ("mem_q1", KD, KD), ("mem_out1", KD, KD),
    ("glu_in1", 2 * KF, KD), ("glu_out1", KD, KF),
]

COLUMNS = [
    ("norm_mix0", KD), ("norm_mix1", KD), ("norm_ffn0", KD), ("norm_ffn1", KD),
    ("g_qk", 13),
    ("ffn_w0", 3 * KF), ("ffn_w1", 3 * KF), ("ffn_b0", KF), ("ffn_b1", KF),
    ("ssm_cw", 4 * 24), ("ssm_cb", 24), ("ssm_d", KI), ("ssm_norm", KI), ("ssm_dtb", 1), ("ssm_alog", 1),
    ("norm_mix2_0", KD), ("norm_mix2_1", KD), ("norm_mem2_0", KD), ("norm_mem2_1", KD),
    ("norm_ffn2_0", KD), ("norm_ffn2_1", KD), ("norm_final", KD), ("kv_norm", KD),
    ("pw1_b", 2 * KD), ("dw_w", CONVW * KD), ("dw_b", KD), ("ln_g", KD), ("ln_b", KD), ("pw2_b", KD),
    ("subln", 1),
]
CONSTS = [("masks", 3 * P), ("head_ones", P), ("alibi", 8 * 256)]
NCST = sum(n for _, n in CONSTS)
COL = {}
NCOL = 0
for _name, _n in COLUMNS:
    COL[_name] = NCOL
    NCOL += _n


class Stream:

    def __init__(self, name, chunks, kc, slab0, chunk0):
        self.name, self.chunks, self.kc = name, chunks, kc
        self.slab0, self.chunk0 = slab0, chunk0
        self.slabs = [min(SLAB, kc - k) for k in range(0, kc, SLAB)]
        self.per = len(self.slabs)


def plan(names):
    out, slab, chunk = {}, 0, 0
    for name, chunks, kc in STREAMS:
        if name not in names:
            continue
        st = Stream(name, chunks, kc, slab, chunk)
        out[name] = st
        slab += chunks * st.per
        chunk += chunks
    return out


def each(eng, n, body, peel=0, tail=0, start=0):
    first = start + peel
    turns = max(n - tail - first, 0) // 4
    for c in range(start, min(first, n)):
        body(c, c % 4, c // 4)
    if turns > 1:
        with eng.Fori(0, turns) as i:
            for j in range(4):
                body(first + 4 * i + j, j, i + first // 4)
    for c in range(first + (4 * turns if turns > 1 else 0), n):
        body(c, c % 4, c // 4)


def lagged(fin, last):
    def after(c, j):
        if j >= 1:
            fin(c - 1, j - 1)
        if j == 3 or (isinstance(c, int) and c == last):
            fin(c, j)
    return after


class Unit:

    def __init__(self, scores, nk, scale, sink=None, rel=None):
        self.scores, self.nk, self.scale, self.sink, self.rel = scores, nk, scale, sink, rel


ALL = ("attn", "ffn0", "ssm", "ffn1", "conf", "mem0", "glu0", "diff", "mem1", "glu1", "final")
OF = {"attn": ("attn_in", "attn_out"), "ffn0": ("ffn_in0", "ffn_out0"), "ssm": ("ssm_in", "ssm_out"),
      "ffn1": ("ffn_in1", "ffn_out1"), "conf": ("pw1", "mem_kv0", "pw2"), "mem0": ("mem_q0", "mem_out0"),
      "glu0": ("glu_in0", "glu_out0"), "diff": ("diff_kv", "diff_q", "mem_kv1", "diff_out"),
      "mem1": ("mem_q1", "mem_out1"), "glu1": ("glu_in1", "glu_out1"), "final": ()}
GAIN = {"attn": "norm_mix0", "ffn0": "norm_ffn0", "ssm": "norm_mix1", "ffn1": "norm_ffn1", "conf": "norm_mix2_0",
        "mem0": "norm_mem2_0", "glu0": "norm_ffn2_0", "diff": "kv_norm", "mem1": "norm_mem2_1",
        "glu1": "norm_ffn2_1", "final": "norm_final"}


def build(nc, A, out, stages=ALL):
    ST = plan([n for s in stages for n in OF[s]])
    SLABS = sum(st.chunks * st.per for st in ST.values())
    nxt = {s: stages[i + 1] if i + 1 < len(stages) else None for i, s in enumerate(stages)}

    with ExitStack() as ctx:
        sems = {}

        def sem(name):
            if name not in sems:
                sems[name] = ctx.enter_context(nc.semaphore(name))
            return sems[name]

        base = (nc.sbuf_base + 63) // 64 * 64
        cursor = [base]

        def sb(name, shape, dt=F32):
            t = nc.alloc_sbuf_tensor_at(name, list(shape), dt, offset=cursor[0])
            n = int(np.prod(shape[1:])) * (2 if dt == BF16 else 4)
            cursor[0] += (n + 31) // 32 * 32
            assert cursor[0] <= nc.sbuf_usable_end, (name, cursor[0] - nc.sbuf_usable_end)
            return t

        xt = sb("xt", [P, KD, S])
        w_raw = sb("w_raw", [P, SLOTS, SLAB * P])
        w_hi = sb("w_hi", [P, SLOTS, SLAB * P], F32R)
        w_lo = sb("w_lo", [P, SLOTS, SLAB * P], F32R)
        cols = sb("cols", [P, NCOL])
        ident = sb("ident", [P, P])
        ones = sb("ones", [P, P])
        ident_b = sb("ident_b", [P, P], BF16)
        masks_b = sb("masks_b", [P, 3, P], BF16)
        eps = sb("eps", [P, 2])
        rstd = sb("rstd", [P, S])
        acc = sb("acc", [P, S])
        sq = sb("sq", [P, 2, S])
        root = sq[:, 0, :]
        x_start = cursor[0]
        xh = sb("xh", [P, KD, S], F32R)
        xl = sb("xl", [P, KD, S], F32R)
        arena = cursor[0]

        hh = sb("hh", [P, KF, S], F32R)
        hl = sb("hl", [P, KF, S], F32R)
        f_g = sb("f_g", [P, S + 2])
        f_y = sb("f_y", [P, S])
        f_u = sb("f_u", [P, S])
        f_h = sb("f_h", [P, S])

        cursor[0] = arena
        oh = sb("oh", [P, KD, S], F32R)
        ol = sb("ol", [P, KD, S], F32R)
        a_prob_t = sb("a_prob_t", [P, PROBS, S])
        a_pt_t = sb("a_pt_t", [P, 2, S])
        a_stat = sb("a_stat", [P, 5, 64])
        v_tmp = a_prob_t[:, 0:2, :]
        q_root_t = a_prob_t[:, 2:4, :]
        a_common = cursor[0]
        qk = sb("qk", [P, 13, S])
        v_tok = sb("v_tok", [P, NT, 640])
        alibi_b = sb("alibi_b", [P, 8, 256], BF16)
        head_ones = sb("head_ones", [P, P])
        sink_c = sb("sink_c", [P, 8])
        flip = sb("flip", [P, P])
        rel = sb("rel", [P, 4, 640])
        cursor[0] = arena
        rel_row = sb("rel_row", [8, 767])
        cst = sb("cst", [P, NCST])
        rel_dram = nc.dram_tensor("rel_table", [8, 767], F32)

        cursor[0] = a_common
        m_q = sb("m_q", [P, KD, S])
        m_k = sb("m_k", [P, KD, M])
        m_v = sb("m_v", [P, M // P, D])
        behind_m = cursor[0]
        cursor[0] = x_start
        m_hi = sb("m_hi", [P, KD, M], F32R)
        m_lo = sb("m_lo", [P, KD, M], F32R)
        m_in = sb("m_in", [P, KD, M])

        cursor[0] = a_common
        d_q = sb("d_q", [P, KD, S])
        d_k = sb("d_k", [P, KD, S])
        d_v = sb("d_v", [P, NT, D])
        cosine = sb("cosine", [P, S])
        sine = sb("sine", [P, S])
        rot = sb("rot", [P, P])
        freq = sb("freq", [P, 1])
        lam_v = d_q[:, 0, 0:256].rearrange("p (a n) -> p a n", a=4)
        lam_t = d_q[:, 1, 0:128].rearrange("p (a n) -> p a n", a=2)
        lam_e = sb("lam_e", [P, 4])
        o_r = sb("o_r", [P, NT * KD])
        o_diag = a_pt_t
        pos_i = d_v[:, 0, 0:S].bitcast(I32)
        d_t = d_v[:, 1:3, 0:S]

        CPE = 9
        cursor[0] = a_common
        c_y = sb("c_y", [P, KD, S])
        cursor[0] = behind_m
        c_u = sb("c_u", [P, 2, CONVW - 1 + S])
        c_mean = sb("c_mean", [P, S])
        c_a = sb("c_a", [P, 2, S])
        c_g = sb("c_g", [P, 2, S])
        cursor[0] = arena
        c_diag = sb("c_diag", [P, 2, CPE, P])
        c_s = a_pt_t

        cursor[0] = arena
        s_z = sb("s_z", [P, KI, S])
        s_xbc = sb("s_xbc", [P, 24, S])

        s_acs_h = sb("s_acs_h", [32, S], F32R)
        s_acs_l = sb("s_acs_l", [32, S], F32R)
        s_one = sb("s_one", [32, 32], F32R)
        s_tok = sb("s_tok", [P, 3, NT, SSMH])
        s_el = sb("s_el", [P, NT, SSMH])
        s_ea = sb("s_ea", [P, 3, S])
        s_dk = sb("s_dk", [P, 3, S])
        s_pad = s_dk[:].rearrange("p a n -> p (a n)")[:, 0:S + 3]
        cursor[0] = arena
        s_dt = sb("s_dt", [32, 8, S])
        s_acs = s_dt[:, 6, :]
        cursor[0] = arena
        yh = sb("yh", [P, KI, S], F32R)
        cursor[0] += 8 * S * 4
        yl = sb("yl", [P, KI, S], F32R)
        cursor[0] = x_start
        s_xt = sb("s_xt", [P, 2, NT, S])
        s_st = sb("s_st", [P, 2, NT - 1, S])
        s_cb = sb("s_cb", [P, 2, NT, P])

        bank = [ctx.enter_context(nc.psum_tensor(f"bank{i}", [P, 512], F32)) for i in range(8)]
        NORM_BANK = bank[7]

        def row(t, c):
            return t[:, c, :] if isinstance(c, int) else t[:, ds(c, 1), :].rearrange("p a n -> p (a n)")

        def col(name, c=0):
            return cols[:, ds(COL[name] + c, 1)] if not isinstance(c, int) else cols[:, COL[name] + c:COL[name] + c + 1]

        w_landed = [sem(f"w_landed{i}") for i in range(SLOTS)]
        w_split = sem("w_split")
        w_half = sem("w_half")
        w_used = sem("w_used")
        bank_free = sem("bank_free")
        const_first, const_in = sem("const_first"), sem("const_in")
        x_in = [sem(f"x_in{c}") for c in range(KD)]
        init_done = sem("init_done")
        x_sq, x_hi, x_lo, x_acc = (sem(n) for n in ("x_sq", "x_hi", "x_lo", "x_acc"))
        acc_zero = sem("acc_zero")
        nrm_sum, nrm_root, nrm_ready = (sem(n) for n in ("nrm_sum", "nrm_root", "nrm_ready"))
        dve_step = sem("dve_step")
        f_tap, f_conv, f_silu, f_prod, f_hi, f_lo = (sem(n) for n in ("f_tap", "f_conv", "f_silu", "f_prod", "f_hi", "f_lo"))
        out_ready, out_done = sem("out_ready"), sem("out_done")

        q_sq, q_sum, q_root, q_rec, q_ready = (sem(n) for n in ("q_sq", "q_sum", "q_root", "q_rec", "q_ready"))
        v_turned, v_ready = sem("v_turned"), sem("v_ready")
        a_score, a_max, a_exp, a_prob, a_turn, a_pt, a_pv, a_oh, a_ol = (
            sem(n) for n in ("a_score", "a_max", "a_exp", "a_prob", "a_turn", "a_pt", "a_pv", "a_oh", "a_ol"))
        cst_in, cst_ready, rel_in, rel_ready, rel_out = (
            sem(n) for n in ("cst_in", "cst_ready", "rel_in", "rel_ready", "rel_out"))
        sink_in, flip_done = sem("sink_in"), sem("flip_done")
        rel_buf = [sem(f"rel_buf{h}") for h in range(4)]

        def score_bank(n, peers):
            return bank[n % 3] if peers == 1 else bank[(0, 1, 2, 4)[n % 4]]

        def turned_bank(k, peers):
            return bank[3 + k % 2 if peers == 1 else 3]

        def attn_units():
            units, turns, groups = [], [], []
            for pair in range(8):
                first = len(units)
                for half in range(2):
                    lo, hi = 64 * half, 64 * half + 64
                    for t in range(NT):
                        if pair < 4:
                            h, kc, nk, k0 = 2 * pair + half, 4 + pair, P * (t + 1), 0
                            vcol = h * 64
                            bias = [(flip[:], rel[:, h % 4, 512 - P * t:640], 0, nk),
                                    (ident_b[:], masks_b[:, 0, :], nk - P, P)]
                        else:
                            h, kc = 4 * half + pair - 4, 12
                            nk, k0 = (P, 0) if t == 0 else (2 * P, P * (t - 1))
                            vcol = 512 + 64 * half
                            bias = [(ident_b[:], alibi_b[:, h, 256 - nk:256], 0, nk)]
                        qc = pair if pair < 4 else 8 + pair - 4
                        scores = [(qk[lo:hi, qc, t * P:(t + 1) * P], qk[lo:hi, kc, k0:k0 + nk], 0, nk)] + bias
                        u = Unit(scores, nk, 0.125, None if pair < 4 else sink_c[:, h:h + 1],
                                 h if pair < 4 else None)
                        u.pv = [(v_tok[:, k0 // P + kt, vcol:vcol + 64], kt, pair, lo, hi, t)
                                for kt in range(nk // P)]
                        units.append(u)
                groups.append((first, len(units), [pair]))
            return units, groups
        UNITS = {"attn": attn_units()}

        def mem_units():
            units, groups = [], []
            for h in range(KD // 2):
                first = len(units)
                for t in range(NT):
                    scores = [(m_q[:, 2 * h + k, t * P:(t + 1) * P], m_k[:, 2 * h + k, :], 0, M) for k in range(2)]
                    u = Unit(scores, M, 0.0625)
                    u.pv = [(m_v[:, kt, (2 * h + d) * P:(2 * h + d + 1) * P], kt, 2 * h + d, 0, P, t)
                            for d in range(2) for kt in range(M // P)]
                    units.append(u)
                groups.append((first, len(units), [2 * h, 2 * h + 1]))
            return units, groups
        UNITS["mem"] = mem_units()

        def diff_units():
            units, groups = [], []
            for h in range(KD):
                first = len(units)
                for t in range(NT):
                    nk = P * (t + 1)
                    for comp in range(2):
                        lo, hi = 64 * comp, 64 * comp + 64
                        u = Unit([(d_q[lo:hi, h, t * P:(t + 1) * P], d_k[lo:hi, h, 0:nk], 0, nk),
                                  (ident_b[:], masks_b[:, 1, :], nk - P, P)], nk, 0.125)
                        u.pv = [(d_v[:, kt, h * P:(h + 1) * P], kt, h, 0, P, t) for kt in range(t + 1)]
                        units.append(u)
                groups.append((first, len(units), [h]))
            return units, groups
        UNITS["diff"] = diff_units()

        def kv_round(l):
            return 1 if l == 0 or "mem_kv0" not in ST else 2

        def c_steps(p):
            return (CONVW - CPE + 1) * p

        m_landed, m_half, m_split = sem("m_landed"), sem("m_half"), sem("m_split")
        r_rot, r_t, r_c, r_done = sem("r_rot"), sem("r_t"), sem("r_c"), sem("r_done")
        y_hi, y_lo = sem("y_hi"), sem("y_lo")
        tab_in, tab_pos, tab_red, tab_sin, tab_done = (sem(n) for n in ("tab_in", "tab_pos", "tab_red", "tab_sin", "tab_done"))
        lam_in, lam_sum, lam_exp = sem("lam_in"), sem("lam_sum"), sem("lam_exp")
        o_dia, o_bc = sem("o_dia"), sem("o_bc")
        o_raw, o_sq, o_sum, o_root, o_new = (sem(n) for n in ("o_raw", "o_sq", "o_sum", "o_root", "o_new"))
        c_sig, c_new, c_dia, c_pe, c_step, c_out = (
            sem(n) for n in ("c_sig", "c_new", "c_dia", "c_pe", "c_step", "c_out"))
        c_msum, c_mrow, c_cent, c_csq, c_cacc, c_norm, c_silu = (
            sem(n) for n in ("c_msum", "c_mrow", "c_cent", "c_csq", "c_cacc", "c_norm", "c_silu"))
        s_tap, s_conv, s_xbc_done, s_v, s_e, s_tp, s_tokd, s_eld = (
            sem(n) for n in ("s_tap", "s_conv", "s_xbc_done", "s_v", "s_e", "s_tp", "s_tokd", "s_eld"))
        s_turn, s_copied, s_cbp, s_cbd, s_xw_d, s_xd_d, s_u, s_state = (
            sem(n) for n in ("s_turn", "s_copied", "s_cbp", "s_cbd", "s_xw_d", "s_xd_d", "s_u", "s_state"))
        s_bc, s_exp, s_mask, s_dec, s_cp, s_m, s_y, s_yb, s_yz, s_sq, s_sum, s_root, s_yn = (
            sem(n) for n in ("s_bc", "s_exp", "s_mask", "s_dec", "s_cp", "s_m", "s_y", "s_yb", "s_yz", "s_sq", "s_sum",
                             "s_root", "s_yn"))
        s_yh, s_yl, s_e0 = sem("s_yh"), sem("s_yl"), sem("s_e0")
        s_zd = sem("s_zd")
        s_split, s_rec = sem("s_split"), sem("s_rec")
        block = ctx.enter_context(nc.Block())

        @block.sync
        def _(sp):
            def load_stream(st):
                w = A["w_" + st.name]

                def turn(i, chunks):
                    for j in range(chunks):
                        k = 0
                        for t, nb in enumerate(st.slabs):
                            o = j * st.per + t
                            slot = (st.slab0 + o) % SLOTS
                            sp.wait_ge(w_split, st.slab0 + o + 1 + i * 4 * st.per)
                            src = w[ds(4 * i + j, 1), :, k * P:(k + nb) * P] if not isinstance(i, int) \
                                else w[4 * i + j:4 * i + j + 1, :, k * P:(k + nb) * P]
                            sp.dma_start(w_raw[:, slot, 0:nb * P], src.rearrange("a p n -> (a p) n")) \
                                .then_inc(w_landed[slot], 16)
                            k += nb

                turns = st.chunks // 4
                with sp.Fori(0, turns) as i:
                    turn(i, 4)
                if st.chunks % 4:
                    turn(turns, st.chunks % 4)

            for st in ST.values():
                load_stream(st)

        @block.gpsimd
        def _(pool):
            pool.memset(ident[:], 0.0).then_inc(init_done, 1)
            pool.memset(ones[:], 1.0).then_inc(init_done, 1)
            pool.memset(eps[:, 0:1], RMS_EPS).then_inc(init_done, 1)
            pool.memset(eps[:, 1:2], LN_EPS).then_inc(init_done, 1)
            pool.wait_ge(init_done, 4)
            pool.affine_select(out=ident[:], in_=ident[:], compare_op=ALU.not_equal, fill=1.0, base=0,
                               pattern=[[-1, P]], channel_multiplier=1).then_inc(init_done, 1)
            if "attn" in stages:
                pool.memset(flip[:], 0.0).then_inc(flip_done, 1)
                pool.wait_ge(flip_done, 1)
                pool.affine_select(out=flip[:], in_=flip[:], compare_op=ALU.not_equal, fill=1.0, base=1 - P,
                                   pattern=[[1, P]], channel_multiplier=1).then_inc(flip_done, 1)

            def split_stream(st, first=None):
                def turn(i, chunks, between=None):
                    for j in range(chunks):
                        for t, nb in enumerate(st.slabs):
                            o = j * st.per + t
                            if between is not None and o == SLOTS:
                                between()
                            s = st.slab0 + o
                            slot = s % SLOTS
                            n = slice(0, nb * P)
                            pool.wait_ge(w_half, s + 1 + i * 4 * st.per)
                            pool.tensor_tensor(w_lo[:, slot, n], w_raw[:, slot, n], w_hi[:, slot, n].bitcast(F32),
                                               ALU.subtract).then_inc(w_split, 1)

                turns = st.chunks // 4
                if first is not None:
                    turn(0, 4, first)
                    if 4 * st.per <= SLOTS:
                        first()
                with pool.Fori(0 if first is None else 1, turns) as i:
                    turn(i, 4)
                if st.chunks % 4:
                    turn(turns, st.chunks % 4)

            def memory_lower(l):
                def do():
                    pool.wait_ge(m_half, kv_round(l))
                    pool.tensor_tensor(m_lo[:], m_in[:], m_hi[:].bitcast(F32), ALU.subtract).then_inc(m_split, 1)
                return do

            def by_head(t, g, n):
                return t[:, 0:n, 8 * g:8 * g + 8].unsqueeze(3).broadcast_to([P, n, 8, 64])

            def ssm_weights():
                pool.wait_ge(s_tokd, 2)
                for g in range(NGRP):
                    x = s_xt[:, g % 2, :, :].rearrange("p a (h d) -> p a h d", d=64)
                    xw = s_st[:, g % 2].rearrange("p a (h d) -> p a h d", d=64)
                    pool.wait_ge(s_copied, 5 * g + 4)
                    if g >= 2:
                        pool.wait_ge(s_y, 8 * (g - 1))
                    pool.tensor_tensor(xw, x[:, 0:NT - 1], by_head(s_tok[:, 2], g, NT - 1), ALU.mult).then_inc(s_xw_d, 1)
                    pool.wait_ge(s_xw_d, g + 1)
                    pool.tensor_tensor(x, x, by_head(s_tok[:, 0], g, NT), ALU.mult).then_inc(s_xd_d, 1)

            for st in ST.values():
                split_stream(st, {"ssm_out": ssm_weights, "mem_kv0": memory_lower(0),
                                  "mem_kv1": memory_lower(1)}.get(st.name))

        @block.tensor
        def _(pe):
            nrm = [0]
            xs = [0]
            fs = [0]

            def gemm(st, hi, lo, n, ready, after=None, peel=0, tail=0, start=0, stop=None, after_i=None):
                def chunk(c, j, i):
                    b = bank[(st.chunk0 + j) % BANKS][:, 0:n]
                    pe.wait_ge(bank_free, st.chunk0 + c + 1)
                    k = 0
                    for t, nb in enumerate(st.slabs):
                        slot = (st.slab0 + j * st.per + t) % SLOTS
                        pe.wait_ge(w_split, SLOTS + st.slab0 + c * st.per + t + 1)
                        for q in range(nb):
                            if j == 0:
                                ready(k)
                            wh = w_hi[:, slot, q * P:(q + 1) * P]
                            wl = w_lo[:, slot, q * P:(q + 1) * P]
                            last = k == st.kc - 1
                            pe.matmul(b, wh, hi[:, k, 0:n], start=(k == 0), stop=False)
                            pe.matmul(b, wh, lo[:, k, 0:n], start=False, stop=False)
                            mm = pe.matmul(b, wl, hi[:, k, 0:n], start=False, stop=last)
                            k += 1
                        mm.then_inc(w_used, 1)
                    if after is not None:
                        after(c, j)
                    if after_i is not None:
                        after_i(c, j, i)

                each(pe, stop or st.chunks, chunk, peel, tail, start)

            def keep_clock(n):
                for _ in range(n):
                    pe.matmul(NORM_BANK[:, P:4 * P], ident_b[:], masks_b[:], start=True, stop=True,
                              skip_group_check=True)

            def v_turn(src, v, new, n, bnk):
                pe.wait_ge(bank_free, new)
                pe.wait_ge(v_ready, v + 1)
                for t in range(n // P):
                    mm = pe.transpose(bnk[:, t * P:(t + 1) * P], src[:, t * P:(t + 1) * P], ident[:])
                mm.then_inc(v_turned, 1)

            def attention(units, groups, peers=1, out=None):
                U = len(units)
                u0, t0, g0 = au[0], at[0], ag[0]
                group_of = {first: g for g, (first, _, _) in enumerate(groups)}
                nch = len(groups[0][2])
                ends = {last: g for g, (_, last, _) in enumerate(groups)}

                def score(m):
                    tiles = range(peers * m, peers * (m + 1))
                    if tiles[-1] >= 2 + peers:
                        pe.wait_ge(a_exp, u0 + tiles[-1] - 1 - peers)
                    for k in range(len(units[tiles[0]].scores)):
                        for n in tiles:
                            u = units[n]
                            if u.rel is not None and n % NT == 0 and k == 1:
                                pe.wait_ge(rel_buf[u.rel % 4], 16 * (u.rel // 4 + 1))
                            l, r, c0, w = u.scores[k]
                            last = k == len(u.scores) - 1
                            mm = pe.matmul(score_bank(n, peers)[:, c0:c0 + w], l, r, start=(k == 0), stop=last,
                                           skip_group_check=True)
                            if last:
                                mm.then_inc(a_score, 1)

                def turn(m):
                    u = units[peers * (m + 1) - 1]
                    src = a_prob_t[:, peers * m % PROBS, :]
                    pe.wait_ge(a_prob, t0 + m + 1)
                    if m >= 3 - peers:
                        pe.wait_ge(a_pt, t0 + m - 2 + peers)
                    for kt in range(u.nk // P):
                        mm = pe.transpose(turned_bank(m, peers)[:, kt * P:(kt + 1) * P], src[:, kt * P:(kt + 1) * P],
                                          ident[:])
                    mm.then_inc(a_turn, 1)

                def outputs(m):
                    u = units[peers * (m + 1) - 1]
                    if peers * m in group_of:
                        held = group_of[peers * m] * nch + nch - 2
                        if held > 0:
                            pe.wait_ge(a_ol, g0 + held) if out is None else pe.wait_ge(o_raw, held)
                    pe.wait_ge(a_pt, t0 + m + 1)
                    nk = u.nk // P
                    for v, kt, ch, lo, hi, t in u.pv:
                        mm = pe.matmul(bank[5 + ch % 2][lo:hi, t * P:(t + 1) * P], v,
                                       a_pt_t[:, m % 2, kt * P:(kt + 1) * P], start=(kt == 0),
                                       stop=(kt == nk - 1), skip_group_check=True)
                    mm.then_inc(a_pv, 1)

                T = U // peers
                turn_lag, out_lag = (3, 4) if peers == 1 else (1, 2)
                for m in range(T + out_lag + (0 if out is None else 2)):
                    if m < T:
                        score(m)
                    if peers == 2:
                        keep_clock(2)
                    if out is not None and peers * m - 6 in ends:
                        out(ends[peers * m - 6])
                    if peers == 2 and 0 <= m - out_lag < T:
                        outputs(m - out_lag)
                    if 0 <= m - turn_lag < T:
                        turn(m - turn_lag)
                    if peers == 1 and 0 <= m - out_lag < T:
                        outputs(m - out_lag)
                au[0] += U
                at[0] += U // peers
                ag[0] += len(groups) * nch

            def attn():
                st = ST["attn_in"]

                def fin(c, j):
                    if isinstance(c, int) and c >= 13:
                        v_turn(v_tmp[:, c % 2, :], c - 13, BANKS + st.chunk0 + c + 1, S, bank[5 + c % 2])
                        return
                    pe.wait_ge(q_sq, c + 1)
                    if not isinstance(c, int) or c >= 2:
                        pe.wait_ge(q_root, c - 1)
                    pe.matmul(bank[5 + j % 2][:], head_ones[:], sq[:, j % 2, :], start=True, stop=True)\
                        .then_inc(q_sum, 1)

                def after(c, j):
                    first_sum(c, j)
                    if isinstance(c, int) and c == 0:
                        pe.wait_ge(cst_ready, 4)
                    lagged(fin, 17)(c, j)
                gemm(st, xh, xl, S, x_ready(KD * nrm[0]), after, peel=4, tail=6)
                keep_clock(8)
                pe.wait_ge(q_ready, 13)
                pe.wait_ge(flip_done, 2)
                pe.wait_ge(v_ready, 2 + 5)
                vt[0] = 5
                attention(*UNITS["attn"])
                gemm(ST["attn_out"], oh, ol, S, lambda k: pe.wait_ge(a_ol, k + 1))
            vt, au, at, ag = [0], [0], [0], [0]

            def mem_kv(l, after=None):
                kv = ST[f"mem_kv{l}"]
                v0 = vt[0]

                def fin(c, j):
                    v_turn(v_tmp[:, j % 2, 0:M], v0 + c - KD, BANKS + kv.chunk0 + c + 1, M, bank[5 + j % 2])
                pe.wait_ge(m_split, kv_round(l))
                gemm(kv, m_hi, m_lo, M, lambda k: None, after, peel=KD, stop=KD)
                gemm(kv, m_hi, m_lo, M, lambda k: None, lagged(fin, 15), start=KD)
                vt[0] += KD

            def mem(l):
                gemm(ST[f"mem_q{l}"], xh, xl, S, x_ready(KD * nrm[0]), first_sum, peel=4)
                keep_clock(6)
                pe.wait_ge(bank_free, BANKS + ST[f"mem_q{l}"].chunk0 + KD)
                pe.wait_ge(v_ready, 2 + vt[0])
                g0 = ag[0]
                attention(*UNITS["mem"])
                gemm(ST[f"mem_out{l}"], oh, ol, S, lambda k: pe.wait_ge(a_ol, g0 + k + 1))

            def diff():
                kv, q = ST["diff_kv"], ST["diff_q"]

                def turn_rope(st, src, r0):
                    def fin(c, j):
                        pe.wait_ge(bank_free, BANKS + st.chunk0 + c + 1)
                        pe.wait_ge(r_done, r0 + c + 1)
                        if r0:
                            pe.wait_ge(v_ready, 2 + vt[0])
                        pe.matmul(bank[5 + j % 2][:], rot[:], row(src, c), start=True, stop=True)\
                            .then_inc(r_rot, 1)
                    return fin
                v0 = vt[0]

                def fin_v(c, j):
                    v_turn(v_tmp[:, j % 2, :], v0 + c - KD, BANKS + kv.chunk0 + c + 1, S, bank[5 + j % 2])

                def after(c, j):
                    first_sum(c, j)
                    if isinstance(c, int) and c == 0:
                        pe.wait_ge(tab_done, 1)
                    lagged(turn_rope(kv, d_k, 0), 7)(c, j)
                gemm(kv, xh, xl, S, x_ready(KD * nrm[0]), after, peel=4, stop=KD)
                gemm(kv, xh, xl, S, lambda k: None, lagged(fin_v, 15), start=KD)
                vt[0] += KD
                gemm(q, xh, xl, S, lambda k: pe.wait_ge(y_lo, k + 1), lagged(turn_rope(q, d_q, KD), 7))
                keep_clock(8)
                pe.wait_ge(r_done, 2 + 2 * KD)
                pe.wait_ge(v_ready, 2 + vt[0])
                g0 = ag[0]

                def out(g):
                    pe.wait_ge(o_sq, g + 1)
                    for t in range(NT):
                        mm = pe.matmul(NORM_BANK[:, NT * g + t:NT * g + t + 1], sq[:, g % 2, t * P:(t + 1) * P],
                                       ones[:, 0:1], start=True, stop=True, skip_group_check=True)
                    mm.then_inc(o_sum, 1)

                def spread(g, j):
                    pe.wait_ge(o_dia, g + 1)
                    if g >= 2:
                        pe.wait_ge(o_new, g - 1)
                    pe.matmul(bank[4 + 3 * (g % 2)][:], ones[:], o_diag[:, g % 2, :], start=True, stop=True)\
                        .then_inc(o_bc, 1)
                attention(*UNITS["diff"], peers=2, out=out)
                mem_kv(1, spread)
                gemm(ST["diff_out"], oh, ol, S, lambda k: pe.wait_ge(a_ol, g0 + k + 1))

            def conf():
                st = ST["pw1"]

                def conv(p, q):
                    pe.wait_ge(c_new, p + 1)
                    pe.wait_ge(c_dia, CPE * (p + 1))
                    pe.wait_ge(c_out, p + 1)
                    for n in range(CPE):
                        mm = pe.matmul(bank[5 + q][:], c_diag[:, q, n, :], c_u[:, q, n:n + S],
                                       start=(n == 0), stop=(n == CPE - 1))
                    mm.then_inc(c_pe, 1)

                def after_i(c, j, i):
                    first_sum(c, j)
                    if j == 3 and not (isinstance(c, int) and c == 3):
                        conv(2 * i - 2, 0)
                        conv(2 * i - 1, 1)
                gemm(st, xh, xl, S, x_ready(KD * nrm[0]), None, peel=4, after_i=after_i)
                conv(6, 0)
                conv(7, 1)
                def sums(c, j):
                    if c == 3:
                        pe.wait_ge(c_step, c_steps(KD))
                    elif c == 7:
                        pe.wait_ge(c_cacc, KD)
                    else:
                        return
                    pe.matmul(NORM_BANK[:], ones[:], acc[:], start=True, stop=True).then_inc(c_msum, 1)
                mem_kv(0, sums)
                gemm(ST["pw2"], oh, ol, S, lambda k: pe.wait_ge(a_ol, ag[0] + k + 1))
                ag[0] += KD
            def ssm():
                st = ST["ssm_in"]
                acs_of = lambda c: slice(c * P, (c + 1) * P)

                def after(c, j):
                    first_sum(c, j)
                    if isinstance(c, int) and c == 24:
                        pe.wait_ge(s_v, 1)
                        for n, src in enumerate((s_dt[:, 0, :], s_acs, s_dt[:, 1, :])):
                            for t in range(NT):
                                pe.transpose(bank[4][:, (NT * n + t) * SSMH:(NT * n + t + 1) * SSMH], src[:, acs_of(t)],
                                             ident[0:32, 0:32])
                        pe.matmul(bank[4][:, 3 * P:4 * P], ones[0:32, :], s_dt[:, 2, 0:P], start=True, stop=True,
                                  skip_group_check=True).then_inc(s_tp, 1)
                gemm(st, xh, xl, S, x_ready(KD * nrm[0]), after, peel=4, stop=25)
                gemm(st, xh, xl, S, lambda k: None, start=25, peel=3)
                pe.wait_ge(s_xbc_done, 24)

                def prepare(g, r):
                    if r < 4:
                        b = bank[5 + r % 2]
                        n = 5 * g + r
                        if r >= 2:
                            pe.wait_ge(s_copied, n - 1)
                        elif g:
                            pe.wait_ge(s_state, 3 * g)
                        for t in range(NT):
                            mm = pe.transpose(b[:, acs_of(t)], s_xbc[:, 8 + 4 * g + r, acs_of(t)], ident[:])
                        mm.then_inc(s_turn, 1)
                        return
                    if g:
                        pe.wait_ge(s_state, 3 * g)
                    for t in range(NT):
                        mm = pe.matmul(bank[4][:, acs_of(t)], s_xbc[:, g, acs_of(t)], s_xbc[:, 4 + g, acs_of(t)],
                                       start=True, stop=True, skip_group_check=True)
                    mm.then_inc(s_cbp, 1)
                    pe.wait_ge(s_copied, 5 * g + 3)
                    for t in range(NT):
                        mm = pe.transpose(bank[5][:, acs_of(t)], s_xbc[:, g, acs_of(t)], ident[:])
                    mm.then_inc(s_turn, 1)

                def inflow(g):
                    pe.wait_ge(s_copied, 5 * g + 5)
                    pe.wait_ge(s_cbd, g + 1)
                    pe.wait_ge(s_xw_d, g + 1)
                    for t in range(NT - 1):
                        mm = pe.matmul(bank[4 + t][:], s_xbc[:, g, acs_of(t)], s_st[:, g % 2, t, :], start=True, stop=True)
                    mm.then_inc(s_u, 1)

                pe.wait_ge(s_tokd, 2)
                pe.wait_ge(s_eld, 1)
                pe.wait_ge(s_split, 3)
                for r in range(5):
                    prepare(0, r)
                inflow(0)
                pe.wait_ge(bank_free, BANKS + st.chunk0 + st.chunks)
                for n in range(SSMH + 7):
                    if n < SSMH:
                        if n >= 2:
                            pe.wait_ge(s_dec, n - 1)
                        pick = s_one[:, n:n + 1].broadcast_to([32, P])
                        pe.matmul(bank[n % 2][:], pick, s_acs_h[:], start=True, stop=False, skip_group_check=True)
                        pe.matmul(bank[n % 2][:], pick, s_acs_l[:], start=False, stop=False, skip_group_check=True)\
                            .then_inc(s_bc, 1)
                    k = n - 1
                    if 0 <= k < SSMH:
                        pe.wait_ge(s_exp, k + 1)
                        pe.matmul(bank[k % 2][:], ident_b[:], masks_b[:, 2:3, :].broadcast_to([P, NT, P]),
                                  start=False, stop=True, skip_group_check=True).then_inc(s_mask, 1)
                    k = n - 2
                    if 0 <= k < SSMH:
                        g, f = k // 8, k // 2
                        lo = 64 * (k % 2)
                        y = bank[2 + f % 2][lo:lo + 64, :]
                        h = slice(k % 8 * 64, k % 8 * 64 + 64)
                        if k % 8 == 0:
                            pe.wait_ge(s_xd_d, g + 1)
                            pe.wait_ge(s_state, 3 * (g + 1))
                        if k % 2 == 0 and f >= 2:
                            pe.wait_ge(s_yb, f - 1)
                        pe.wait_ge(s_cp, k + 1)
                        pe.wait_ge(s_m, k + 1)
                        for t in range(NT):
                            mm = pe.matmul(y[:, acs_of(t)], s_xt[:, g % 2, t, h], s_dk[:, k % 3, acs_of(t)],
                                           start=True, stop=(t == 0), skip_group_check=True)
                            if t:
                                mm = pe.matmul(y[:, acs_of(t)], s_st[:, g % 2, t - 1, h], s_ea[:, k % 3, acs_of(t)],
                                               start=False, stop=True, skip_group_check=True)
                        mm.then_inc(s_y, 1)
                    g, r = n // 8, n % 8 - 1
                    if g + 1 < NGRP and 0 <= r < 5:
                        prepare(g + 1, r)
                    if g + 1 < NGRP and r == 6:
                        inflow(g + 1)
                    f = n // 2 - 3
                    if n % 2 == 0 and 0 <= f < KI:
                        pe.wait_ge(s_sq, f + 1)
                        if f % 4 == 0 and f:
                            pe.wait_ge(s_root, f // 4)
                        pe.matmul(NORM_BANK[:], ones[:], sq[:, f % 2, :], start=(f % 4 == 0), stop=(f % 4 == 3),
                                  skip_group_check=True).then_inc(s_sum, 1)
                gemm(ST["ssm_out"], yh, yl, S, lambda k: pe.wait_ge(s_yl, k + 1))

            def x_ready(base):
                return lambda k: pe.wait_ge(x_lo, base + k + 1)

            def norm_sum():
                nrm[0] += 1
                pe.wait_ge(x_acc, KD * nrm[0])
                pe.matmul(NORM_BANK[:], ones[:], acc[:], start=True, stop=True).then_inc(nrm_sum, 1)

            def first_sum(c, j):
                if isinstance(c, int) and c == 0:
                    norm_sum()

            def ffn(si, so):
                gemm(ST[si], xh, xl, S, x_ready(KD * nrm[0]), first_sum, peel=4)
                f0 = fs[0]
                fs[0] += KF
                gemm(ST[so], hh, hl, S, lambda k: pe.wait_ge(f_lo, f0 + k + 1))

            pe.wait_ge(init_done, 5)
            for s in stages:
                if s == "attn":
                    attn()
                elif s.startswith("mem"):
                    mem(int(s[3]))
                elif s == "diff":
                    diff()
                elif s == "conf":
                    conf()
                elif s == "ssm":
                    ssm()
                elif s.startswith("ffn"):
                    ffn("ffn_in" + s[3], "ffn_out" + s[3])
                elif s.startswith("glu"):
                    ffn("glu_in" + s[3], "glu_out" + s[3])
                elif s == "final":
                    norm_sum()

        @block.vector
        def _(dve):
            nrm = [0]
            steps = [0]

            def new_x(s):
                return GAIN[s] if s else None

            def split_x(c, k, gain):
                dve.wait_ge(x_hi, k + 1)
                dve.scalar_tensor_tensor(row(xl, c), row(xt, c), col(gain, c), row(xh, c).bitcast(F32),
                                         ALU.mult, ALU.subtract).then_inc(x_lo, 1)

            def add_square(k, j):
                dve.wait_ge(x_sq, k + 1)
                dve.wait_ge(x_acc, k)
                dve.tensor_tensor(acc[:], acc[:], sq[:, j % 2, :], ALU.add).then_inc(x_acc, 1)

            def zero_acc():
                if nrm[0]:
                    dve.wait_ge(nrm_sum, nrm[0])
                dve.memset(acc[:], 0.0).then_inc(acc_zero, 1)
                dve.wait_ge(acc_zero, nrm[0] + 1)

            def norm_recip():
                nrm[0] += 1
                dve.wait_ge(nrm_root, nrm[0])
                dve.reciprocal(rstd[:], root).then_inc(nrm_ready, 1)
                dve.wait_ge(nrm_ready, nrm[0])

            def residual(st, gain, bias=None):
                zero_acc()
                k0 = KD * nrm[0]

                def chunk(c, j, i):
                    b = bank[(st.chunk0 + j) % BANKS]
                    dve.wait_ge(w_used, SLOTS + st.slab0 + (c + 1) * st.per)
                    if bias is None:
                        dve.tensor_tensor(row(xt, c), b[:], row(xt, c), ALU.add).then_inc(bank_free, 1)
                    else:
                        dve.scalar_tensor_tensor(row(xt, c), b[:], col(bias, c), row(xt, c), ALU.add, ALU.add).then_inc(bank_free, 1)
                    dve.wait_ge(bank_free, BANKS + st.chunk0 + c + 1)
                    add_square(k0 + c, j)
                    split_x(c, k0 + c, gain)
                each(dve, KD, chunk)

            def step(ins):
                ins.then_inc(dve_step, 1)
                steps[0] += 1
                dve.wait_ge(dve_step, steps[0])

            def attention(units, groups, peers=1, out=None, lam=None):
                U = len(units)
                u0, t0, g0 = au[0], at[0], ag[0]
                ends = {last: (g, chunks) for g, (_, last, chunks) in enumerate(groups)}
                nch = len(groups[0][2])
                for s_ in range(U + 6):
                    for lag, do in out or ():
                        if s_ - lag in ends:
                            do(ends[s_ - lag][0])
                    if s_ < U:
                        u, cs = units[s_], slice(s_, s_ + 1)
                        dve.wait_ge(a_score, u0 + s_ + 1)
                        step(dve.reduce_max(a_stat[:, 0, cs], score_bank(s_, peers)[:, 0:u.nk], AX_X))
                        if u.sink is None:
                            dve.tensor_scalar(a_stat[:, 1, cs], a_stat[:, 0, cs], -u.scale, None, ALU.mult)\
                                .then_inc(a_max, 1)
                        else:
                            step(dve.tensor_scalar(a_stat[:, 0, cs], a_stat[:, 0, cs], u.scale, u.sink,
                                                   ALU.mult, ALU.max))
                            dve.tensor_scalar(a_stat[:, 1, cs], a_stat[:, 0, cs], -1.0, None, ALU.mult)\
                                .then_inc(a_max, 1)
                    r = s_ - 1
                    if 0 <= r < U:
                        u, cs = units[r], slice(r, r + 1)
                        dve.wait_ge(a_exp, u0 + r + 1)
                        if u.sink is not None:
                            step(dve.tensor_tensor(a_stat[:, 2, cs], a_stat[:, 2, cs], a_stat[:, 3, cs], ALU.add))
                        step(dve.reciprocal(a_stat[:, 4, cs], a_stat[:, 2, cs]))
                        pr = a_prob_t[:, r % PROBS, 0:u.nk]
                        if peers == 1:
                            dve.tensor_scalar(pr, pr, a_stat[:, 4, cs], None, ALU.mult).then_inc(a_prob, 1)
                        elif r % 2 == 0:
                            step(dve.tensor_scalar(pr, pr, a_stat[:, 4, cs], None, ALU.mult))
                        else:
                            step(dve.tensor_scalar(a_stat[:, 4, cs], a_stat[:, 4, cs], lam, None, ALU.mult))
                            first = a_prob_t[:, (r - 1) % PROBS, 0:u.nk]
                            dve.scalar_tensor_tensor(first, pr, a_stat[:, 4, cs], first, ALU.mult, ALU.add)\
                                .then_inc(a_prob, 1)
                    if s_ - 4 in ends and out is None:
                        g, chunks = ends[s_ - 4]
                        for n, ch in enumerate(chunks):
                            dve.wait_ge(a_oh, g0 + g * nch + n + 1)
                            dve.tensor_tensor(ol[:, ch, :], bank[5 + ch % 2][:], oh[:, ch, :].bitcast(F32),
                                              ALU.subtract).then_inc(a_ol, 1)
                au[0] += U
                at[0] += U // peers
                ag[0] += len(groups) * nch
            au, at, ag = [0], [0], [0]
            vt = [0]

            def value(st, c, j, v, n, scaled):
                dve.wait_ge(w_used, SLOTS + st.slab0 + c + 1)
                if not isinstance(v, int) or v >= 2:
                    dve.wait_ge(v_turned, v - 1)
                b = bank[(st.chunk0 + j) % BANKS][:, 0:n]
                if scaled:
                    dve.tensor_tensor(v_tmp[:, j % 2, 0:n], b, rstd[:], ALU.mult).then_inc(bank_free, 1)
                else:
                    dve.tensor_copy(v_tmp[:, j % 2, 0:n], b).then_inc(bank_free, 1)

            def mem_kv(l):
                kv = ST[f"mem_kv{l}"]
                v0 = vt[0]
                vt[0] += KD

                def chunk(c):
                    if c < KD:
                        dve.wait_ge(w_used, SLOTS + kv.slab0 + c + 1)
                        dve.tensor_copy(m_k[:, c, :], bank[(kv.chunk0 + c) % BANKS][:, 0:M]).then_inc(bank_free, 1)
                    else:
                        value(kv, c, c % 4, v0 + c - KD, M, False)
                return chunk

            def mem(l, s):
                q = ST[f"mem_q{l}"]
                norm_recip()

                def query(c, j, i):
                    dve.wait_ge(w_used, SLOTS + q.slab0 + c + 1)
                    dve.tensor_tensor(row(m_q, c), bank[(q.chunk0 + j) % BANKS][:], rstd[:], ALU.mult)\
                        .then_inc(bank_free, 1)
                each(dve, KD, query)
                attention(*UNITS["mem"])
                residual(ST[f"mem_out{l}"], new_x(nxt[s]))

            def rope(st, dst, r0, c, j):
                b = bank[5 + j % 2]
                dve.wait_ge(r_rot, r0 + c + 1)
                dve.wait_ge(r_done, 2 + r0 + c)
                dve.tensor_tensor(c_rope[:], b[:], sine[:], ALU.mult).then_inc(r_t, 1)
                dve.tensor_tensor(row(dst, c), row(dst, c), cosine[:], ALU.mult).then_inc(r_c, 1)
                dve.wait_ge(r_c, r0 + c + 1)
                dve.wait_ge(r_t, r0 + c + 1)
                dve.tensor_tensor(row(dst, c), row(dst, c), c_rope[:], ALU.add).then_inc(r_done, 1)
            c_rope = a_prob_t[:, 2, :]

            def diff(s):
                kv, q = ST["diff_kv"], ST["diff_q"]
                two_pi = 2.0 * math.pi
                c1 = 6.28125
                c2 = float(np.float32(np.round((two_pi - c1) * 2 ** 21) / 2 ** 21))
                c3 = float(np.float32(two_pi - c1 - c2))
                magic = 1.5 * 2 ** 23
                ang, turns = d_t[:, 0, :], d_t[:, 1, :]
                dve.wait_ge(tab_in, 48)
                step(dve.tensor_copy(ang, pos_i))
                step(dve.tensor_scalar(ang, ang, freq[:, 0:1], None, ALU.mult))
                step(dve.tensor_scalar(turns, ang, 1.0 / two_pi, magic, ALU.mult, ALU.add))
                step(dve.tensor_scalar(turns, turns, magic, None, ALU.subtract))
                for part in (c1, c2, c3):
                    step(dve.scalar_tensor_tensor(ang, turns, -part, ang, ALU.mult, ALU.add))
                dve.tensor_scalar(ang, ang, 3.1415925, -3.1415925, ALU.min, ALU.max).then_inc(tab_red, 1)
                dve.wait_ge(tab_sin, 2)
                step(dve.tensor_tensor(turns, turns, turns, ALU.mult))
                dve.tensor_scalar(cosine[:], turns, -2.0, 1.0, ALU.mult, ALU.add).then_inc(tab_done, 1)
                dve.wait_ge(lam_in, 16)
                step(dve.tensor_tensor(lam_t, lam_v[:, 0:4:2, :], lam_v[:, 1:4:2, :], ALU.mult))
                dve.tensor_reduce(lam_e[:, 0:2], lam_t, AX_X, ALU.add).then_inc(lam_sum, 1)
                dve.wait_ge(lam_exp, 1)
                step(dve.tensor_tensor(lam_e[:, 3:4], lam_e[:, 3:4], lam_e[:, 2:3], ALU.subtract))
                step(dve.tensor_scalar(lam_e[:, 3:4], lam_e[:, 3:4], -LAMBDA_INIT, None, ALU.add))
                norm_recip()

                def heads(st, dst, r0):
                    def chunk(c, j, i):
                        dve.wait_ge(w_used, SLOTS + st.slab0 + c + 1)
                        dve.tensor_tensor(row(dst, c), bank[(st.chunk0 + j) % BANKS][:], rstd[:], ALU.mult)\
                            .then_inc(bank_free, 1)
                        lagged(lambda c, j: rope(st, dst, r0, c, j), -1)(c, j)
                    return chunk
                v0 = vt[0]
                each(dve, KD, heads(kv, d_k, 0))
                each(dve, 2 * KD, lambda c, j, i: value(kv, c, j, v0 + c - KD, S, True), start=KD, peel=4)
                vt[0] += KD
                for c in range(KD):
                    dve.wait_ge(y_hi, c + 1)
                    dve.scalar_tensor_tensor(xl[:, c, :], xt[:, c, :], col("norm_mix2_1", c),
                                             xh[:, c, :].bitcast(F32), ALU.mult, ALU.subtract).then_inc(y_lo, 1)
                each(dve, KD, heads(q, d_q, KD))
                dve.wait_ge(r_done, 2 + 2 * KD)

                def raw(g):
                    dve.wait_ge(a_pv, a_pv0 + NT * (g + 1))
                    dve.tensor_copy(d_q[:, g, :], bank[5 + g % 2][:]).then_inc(o_raw, 1)

                def diagonal(g):
                    if g >= 2:
                        dve.wait_ge(o_bc, g - 1)
                    r = o_r[:, NT * g:NT * g + NT].unsqueeze(2).broadcast_to([P, NT, P])
                    dve.tensor_tensor(o_diag[:, g % 2, :].rearrange("p (a n) -> p a n", n=P),
                                      ident[:].unsqueeze(1).broadcast_to([P, NT, P]), r, ALU.mult).then_inc(o_dia, 1)

                def normed(g):
                    dve.wait_ge(o_bc, g + 1)
                    dve.scalar_tensor_tensor(d_q[:, g, :], d_q[:, g, :], col("subln"), bank[4 + 3 * (g % 2)][:],
                                             ALU.mult, ALU.mult).then_inc(o_new, 1)

                def lower(g):
                    dve.wait_ge(a_oh, g0 + g + 1)
                    dve.scalar_tensor_tensor(ol[:, g, :], d_q[:, g, :], 1.0 - LAMBDA_INIT, oh[:, g, :].bitcast(F32),
                                             ALU.mult, ALU.subtract).then_inc(a_ol, 1)
                a_pv0, g0 = at[0], ag[0]
                attention(*UNITS["diff"], peers=2, lam=lam_e[:, 3:4], out=((5, raw),))
                chunk = mem_kv(1)
                dve.wait_ge(o_root, 1)
                step(dve.reciprocal(o_r[:], o_r[:]))
                diagonal(0)
                for c in range(KD):
                    if c + 1 < KD:
                        diagonal(c + 1)
                    chunk(c)
                    normed(c)
                    if c:
                        lower(c - 1)
                for c in range(KD, 2 * KD):
                    chunk(c)
                    if c == KD:
                        lower(KD - 1)
                residual(ST["diff_out"], new_x(nxt[s]))

            def ssm(s):
                st = ST["ssm_in"]
                norm_recip()
                t = lambda n: s_dt[:, n, :]

                def softplus_and_sums():
                    dve.wait_ge(w_used, SLOTS + st.slab0 + 1)
                    dve.tensor_tensor(t(0), bank[st.chunk0 % BANKS][0:32, :], rstd[0:32, :], ALU.mult).then_inc(bank_free, 1)
                    dve.wait_ge(bank_free, BANKS + st.chunk0 + 1)
                    step(dve.tensor_scalar(t(0), t(0), col("ssm_dtb")[0:32], None, ALU.add))
                    dve.scalar_tensor_tensor(t(1), t(0), -1.0, t(0), ALU.mult, ALU.max).then_inc(s_e0, 1)
                    dve.wait_ge(s_e, 2)
                    step(dve.tensor_scalar(t(2), t(1), 2.0, None, ALU.add))
                    step(dve.reciprocal(t(2), t(2)))
                    step(dve.tensor_tensor(t(1), t(1), t(2), ALU.mult))
                    step(dve.tensor_tensor(t(2), t(1), t(1), ALU.mult))
                    step(dve.tensor_scalar(t(3), t(2), 1.0 / 15.0, None, ALU.mult))
                    for n in (13, 11, 9, 7, 5, 3):
                        step(dve.scalar_tensor_tensor(t(3), t(3), 1.0 / n, t(2), ALU.add, ALU.mult))
                    step(dve.scalar_tensor_tensor(t(3), t(3), 1.0, t(1), ALU.add, ALU.mult))
                    step(dve.tensor_scalar(t(0), t(0), 0.0, None, ALU.max))
                    step(dve.scalar_tensor_tensor(t(0), t(3), 2.0, t(0), ALU.mult, ALU.add))
                    dve.wait_ge(s_e, 2)
                    step(dve.tensor_scalar(t(4), t(0), t(5)[:, 0:1], -1.0, ALU.mult, ALU.mult))
                    for c in range(NT):
                        cs = slice(c * P, (c + 1) * P)
                        ins = dve.tensor_tensor_scan(s_acs[:, cs], ones[0:32, :], t(4)[:, cs], 0.0, ALU.mult, ALU.add)
                        step(ins)
                    last = s_acs.rearrange("p (a n) -> p a n", a=NT)[:, :, P - 1:P]
                    dve.tensor_tensor(t(2)[:, 0:P].rearrange("p (a n) -> p a n", a=NT),
                                      ident[0:32, 0:32].unsqueeze(1).broadcast_to([32, NT, 32]),
                                      last.broadcast_to([32, NT, 32]), ALU.mult).then_inc(s_e0, 1)
                    dve.wait_ge(s_e, 6)
                    dve.tensor_tensor(t(1), t(1), t(0), ALU.mult).then_inc(s_v, 1)

                def taps(c, j, i):
                    if isinstance(c, int) and c == 0:
                        return softplus_and_sums()
                    q = c - 1
                    y = s_ea[:, j % 2, :]
                    dve.wait_ge(w_used, SLOTS + st.slab0 + c + 1)
                    if not (isinstance(c, int) and c == 1):
                        dve.wait_ge(s_conv, 3 * q)
                    dve.tensor_tensor(s_pad[:, 3:S + 3], bank[(st.chunk0 + j) % BANKS][:], rstd[:], ALU.mult)\
                        .then_inc(bank_free, 1)
                    dve.wait_ge(s_tap, q + 1)
                    for n in range(3):
                        dve.scalar_tensor_tensor(y, s_pad[:, n:n + S], col("ssm_cw", 4 * q + n), y, ALU.mult, ALU.add)\
                            .then_inc(s_conv, 1)
                        if n < 2:
                            dve.wait_ge(s_conv, 3 * q + n + 1)

                def gate(c, j, i):
                    dve.wait_ge(w_used, SLOTS + st.slab0 + c + 1)
                    dve.tensor_tensor(row(s_z, c - 25), bank[(st.chunk0 + j) % BANKS][:], rstd[:], ALU.mult)\
                        .then_inc(bank_free, 1)
                step(dve.memset(s_pad[:, 0:3], 0.0))
                each(dve, 25, taps, peel=4)
                dve.wait_ge(s_tp, 1)
                dve.wait_ge(s_split, 2)
                dve.tensor_copy(s_tok[:].rearrange("p a b n -> p (a b n)"), bank[4][:, 0:3 * P]).then_inc(s_tokd, 1)
                dve.wait_ge(s_tokd, 1)
                dve.tensor_tensor(s_acs_l[:], s_acs, s_acs_h[:].bitcast(F32), ALU.subtract).then_inc(s_split, 1)
                dve.tensor_scalar(s_tok[:, 1, :, :], s_tok[:, 1, :, :], -1.0, None, ALU.mult).then_inc(s_tokd, 1)
                dve.wait_ge(s_tokd, 2)
                each(dve, 41, gate, start=25, peel=3)

                def products(g):
                    dve.wait_ge(s_cbp, g + 1)
                    dve.tensor_copy(s_cb[:, g % 2, :, :].rearrange("p a n -> p (a n)"), bank[4][:]).then_inc(s_cbd, 1)

                def state(g, n):
                    dve.wait_ge(s_u, g + 1)
                    st_ = s_st[:, g % 2]
                    if n == 0:
                        dve.tensor_copy(st_[:, 0, :], bank[4][:]).then_inc(s_state, 1)
                        return
                    dve.wait_ge(s_state, 3 * g + n)
                    el = s_el[:, n, 8 * g:8 * g + 8].unsqueeze(2).broadcast_to([P, 8, 64])
                    step(dve.tensor_tensor(st_[:, n, :].rearrange("p (h d) -> p h d", d=64),
                                           st_[:, n - 1, :].rearrange("p (h d) -> p h d", d=64), el, ALU.mult))
                    dve.tensor_tensor(st_[:, n, :], bank[4 + n][:], st_[:, n, :], ALU.add).then_inc(s_state, 1)

                dve.wait_ge(s_eld, 1)
                products(0)
                for n in range(NT - 1):
                    state(0, n)
                def low(f):
                    dve.wait_ge(s_yh, f + 1)
                    dve.wait_ge(s_yn, f + 1)
                    dve.tensor_tensor(yl[:, f, :], s_xbc[:, 8 + f, :], yh[:, f, :].bitcast(F32), ALU.subtract)\
                        .then_inc(s_yl, 1)

                for n in range(SSMH + 13 + 4):
                    if n < SSMH:
                        dve.wait_ge(s_exp, n + 1)
                        dve.tensor_tensor(s_ea[:, n % 3, :], s_xbc[:, 4 + n // 8, :], s_ea[:, n % 3, :], ALU.mult)\
                            .then_inc(s_cp, 1)
                    k = n - 1
                    if 0 <= k < SSMH:
                        dve.wait_ge(s_dec, k + 1)
                        if k % 8 == 0:
                            dve.wait_ge(s_cbd, k // 8 + 1)
                        dve.tensor_tensor(s_dk[:, k % 3, :], s_dk[:, k % 3, :],
                                          s_cb[:, k // 8 % 2, :, :].rearrange("p a n -> p (a n)"), ALU.mult)\
                            .then_inc(s_m, 1)
                    if n % 8 == 7 and n // 8 + 1 < NGRP:
                        state(n // 8 + 1, 0)
                        state(n // 8 + 1, 1)
                    if n % 8 == 0 and 0 < n < SSMH:
                        state(n // 8, 2)
                    f = n // 2 - 2
                    if n % 2 == 0 and 0 <= f < KI:
                        x = s_xbc[:, 8 + f, :]
                        dve.wait_ge(s_y, 2 * f + 2)
                        dve.scalar_tensor_tensor(x, x, col("ssm_d", f), bank[2 + f % 2][:], ALU.mult, ALU.add)\
                            .then_inc(s_yb, 1)
                        dve.wait_ge(s_yb, f + 1)
                        dve.tensor_tensor(x, x, s_z[:, f, :], ALU.mult).then_inc(s_yz, 1)
                    if n % 8 == 5 and n // 8 + 1 < NGRP:
                        products(n // 8 + 1)
                    for g in range(NGRP):
                        q = n - 14 - 8 * g
                        if 0 <= q < 2:
                            dve.wait_ge(s_root, g + 1)
                            part = rstd[:, q * 256:(q + 1) * 256]
                            dve.reciprocal(part, part).then_inc(s_rec, 1)
                        q = n - 16 - 8 * g
                        if 0 <= q < 4:
                            f = 4 * g + q
                            dve.wait_ge(s_rec, 2 * g + 2)
                            dve.wait_ge(s_yz, 4 * g + 4)
                            dve.scalar_tensor_tensor(s_xbc[:, 8 + f, :], s_xbc[:, 8 + f, :], col("ssm_norm", f), rstd[:],
                                                     ALU.mult, ALU.mult).then_inc(s_yn, 1)
                        q = n - 17 - 8 * g
                        if 0 <= q < 4:
                            low(4 * g + q)
                residual(ST["ssm_out"], new_x(nxt[s]))

            def conf(s):
                st = ST["pw1"]
                norm_recip()
                nst = CONVW - CPE
                for q in range(2):
                    step(dve.memset(c_u[:, q, 0:CONVW - 1], 0.0))
                step(dve.memset(acc[:], 0.0))

                def gated(p, q):
                    b0 = st.chunk0 + 2 * q
                    dve.wait_ge(w_used, SLOTS + st.slab0 + 2 * p + 1)
                    dve.tensor_tensor(c_a[:, q, :], bank[b0 % BANKS][:], rstd[:], ALU.mult).then_inc(bank_free, 1)
                    dve.wait_ge(w_used, SLOTS + st.slab0 + 2 * p + 2)
                    dve.tensor_tensor(c_g[:, q, :], bank[(b0 + 1) % BANKS][:], rstd[:], ALU.mult).then_inc(bank_free, 1)

                def entered(p, q):
                    dve.wait_ge(c_sig, p + 1)
                    dve.wait_ge(c_pe, p + 1)
                    dve.scalar_tensor_tensor(c_u[:, q, CONVW - 1:], c_a[:, q, :], col("pw1_b", 2 * p), c_g[:, q, :],
                                             ALU.add, ALU.mult).then_inc(c_new, 1)

                with dve.Fori(0, KD // 2) as i:
                    for q in range(2):
                        gated(2 * i + q, q)
                    for q in range(2):
                        entered(2 * i + q, q)
                    k0 = c_steps(1) * 2 * i
                    dve.wait_ge(c_new, 2 * i + 2)
                    for n in range(nst):
                        for q in range(2):
                            p, tap = 2 * i + q, CPE + n
                            w, src, y = col("dw_w", CONVW * p + tap), c_u[:, q, tap:tap + S], row(c_y, p)
                            if n == 0:
                                dve.tensor_scalar(y, src, w, col("dw_b", p), ALU.mult, ALU.add).then_inc(c_step, 1)
                            else:
                                dve.wait_ge(c_step, k0 + 2 * n + q - 1)
                                dve.scalar_tensor_tensor(y, src, w, y, ALU.mult, ALU.add).then_inc(c_step, 1)
                    for q in range(2):
                        p = 2 * i + q
                        dve.wait_ge(c_pe, 2 + p + 1)
                        dve.wait_ge(c_step, k0 + 2 * nst - 1 + q)
                        dve.tensor_tensor(row(c_y, p), bank[5 + q][:], row(c_y, p), ALU.add).then_inc(c_out, 1)
                    for q in range(2):
                        dve.wait_ge(c_out, 2 + 2 * i + q + 1)
                        if q:
                            dve.wait_ge(c_step, k0 + 2 * nst + 1)
                        dve.tensor_tensor(acc[:], acc[:], row(c_y, 2 * i + q), ALU.add).then_inc(c_step, 1)
                    dve.wait_ge(c_step, k0 + 2 * nst + 2)
                chunk = mem_kv(0)
                for c in range(4):
                    chunk(c)
                dve.wait_ge(c_mrow, 1)
                step(dve.memset(acc[:], 0.0))
                for c in range(KD + 1):
                    if c < KD:
                        dve.tensor_tensor(c_y[:, c, :], c_y[:, c, :], c_mean[:], ALU.subtract).then_inc(c_cent, 1)
                    if c:
                        dve.wait_ge(c_csq, c)
                        dve.wait_ge(c_cacc, c - 1) if c > 1 else None
                        dve.tensor_tensor(acc[:], acc[:], sq[:, (c - 1) % 2, :], ALU.add).then_inc(c_cacc, 1)
                    if c % 2 and c < KD:
                        chunk(4 + c // 2)
                dve.wait_ge(c_mrow, 2)
                step(dve.reciprocal(c_mean[:], c_mean[:]))

                def low(c):
                    dve.wait_ge(a_oh, ag[0] + c + 1)
                    dve.tensor_tensor(ol[:, c, :], c_s[:, c % 2, :], oh[:, c, :].bitcast(F32), ALU.subtract)\
                        .then_inc(a_ol, 1)
                for c in range(KD):
                    dve.tensor_tensor(c_y[:, c, :], c_y[:, c, :], c_mean[:], ALU.mult).then_inc(c_norm, 1)
                    if c:
                        low(c - 1)
                    chunk(KD + c)
                low(KD - 1)
                ag[0] += KD
                residual(ST["pw2"], new_x(nxt[s]), "pw2_b")

            def attn(s):
                st = ST["attn_in"]
                dve.wait_ge(rel_in, 16)
                step(dve.tensor_scalar(rel_row[:, 383:767], rel_row[:, 383:767], 8.0, None, ALU.mult))
                dve.tensor_copy(rel_row[:, 0:383], rel_row[:, 383:384].broadcast_to([8, 383])).then_inc(rel_ready, 1)
                norm_recip()

                def raw(c, j):
                    b = bank[(st.chunk0 + j) % BANKS]
                    dve.wait_ge(w_used, SLOTS + st.slab0 + c + 1)
                    if isinstance(c, int) and c >= 13:
                        if c >= 15:
                            dve.wait_ge(v_turned, c - 14)
                        dst = v_tmp[:, c % 2, :]
                    else:
                        dst = row(qk, c)
                    dve.tensor_tensor(dst, b[:], rstd[:], ALU.mult).then_inc(bank_free, 1)

                def fin(c, j):
                    if isinstance(c, int) and c >= 13:
                        return
                    rt = q_root_t[:, j % 2, :]
                    dve.wait_ge(q_root, c + 1)
                    dve.reciprocal(rt, rt).then_inc(q_rec, 1)
                    dve.wait_ge(q_rec, c + 1)
                    dst = row(qk, c)
                    dve.scalar_tensor_tensor(dst, dst, col("g_qk", c),
                                             rt, ALU.mult, ALU.mult).then_inc(q_ready, 1)
                def chunk(c, j, i):
                    raw(c, j)
                    if j >= 1:
                        fin(c - 1, j - 1)
                    if j == 3 or (isinstance(c, int) and c == 17):
                        fin(c, j)
                each(dve, 18, chunk, peel=4, tail=6)
                vt[0] += 5
                dve.wait_ge(q_ready, 13)
                attention(*UNITS["attn"])
                residual(ST["attn_out"], new_x(nxt[s]))

            def ffn(si, so, s, conv):
                norm_recip()
                st = ST[si]
                if conv:
                    step(dve.memset(f_g[:, 0:2], 0.0))
                f0 = ffns[0]
                ffns[0] += KF

                def pairs(i, jj):
                    p = i * 2 + jj
                    bg, bu = bank[(st.chunk0 + 2 * jj) % BANKS], bank[(st.chunk0 + 2 * jj + 1) % BANKS]
                    dve.wait_ge(w_used, SLOTS + st.slab0 + 2 * p + 1)
                    dve.tensor_tensor(f_g[:, 2:S + 2], bg[:], rstd[:], ALU.mult).then_inc(bank_free, 1)
                    if conv:
                        dve.wait_ge(f_tap, conv[2] * KF + p + 1)
                        dve.scalar_tensor_tensor(f_y[:], f_g[:, 1:S + 1], col(conv[0], 3 * p + 1), f_y[:],
                                                 ALU.mult, ALU.add).then_inc(f_conv, 1)
                        dve.wait_ge(f_conv, conv[2] * 2 * KF + 2 * p + 1)
                        dve.scalar_tensor_tensor(f_y[:], f_g[:, 0:S], col(conv[0], 3 * p), f_y[:],
                                                 ALU.mult, ALU.add).then_inc(f_conv, 1)
                    dve.wait_ge(w_used, SLOTS + st.slab0 + 2 * p + 2)
                    dve.tensor_tensor(f_u[:], bu[:], rstd[:], ALU.mult).then_inc(bank_free, 1)
                    dve.wait_ge(bank_free, BANKS + st.chunk0 + 2 * p + 2)
                    dve.wait_ge(f_silu, f0 + p + 1)
                    dve.tensor_tensor(f_h[:], f_y[:], f_u[:], ALU.mult).then_inc(f_prod, 1)
                    dve.wait_ge(f_hi, f0 + p + 1)
                    dve.tensor_tensor(row(hl, p), f_h[:],
                                      row(hh, p).bitcast(F32),
                                      ALU.subtract).then_inc(f_lo, 1)

                with dve.Fori(0, KF // 2) as i:
                    for jj in range(2):
                        pairs(i, jj)
                residual(ST[so], new_x(nxt[s]))

            ffns = [0]
            dve.sem_inc(bank_free, BANKS)
            dve.sem_inc(w_split, SLOTS)
            dve.sem_inc(w_used, SLOTS)
            dve.sem_inc(v_ready, 2)
            dve.sem_inc(r_done, 2)
            dve.sem_inc(c_out, 2)
            dve.sem_inc(c_pe, 2)
            zero_acc()
            dve.wait_ge(init_done, 5)
            dve.tensor_copy(ident_b[:], ident[:]).then_inc(cst_ready, 1)
            dve.wait_ge(const_first, 16)

            def start_chunk(c, j, i):
                split_x(c, c, GAIN[stages[0]])
                add_square(c, j)
            each(dve, KD, start_chunk)
            dve.wait_ge(const_in, 16)
            if set(stages) & {"attn", "diff", "ssm"}:
                dve.wait_ge(cst_in, 16)
                dve.tensor_copy(masks_b[:], cst[:, 0:3 * P].rearrange("p (a n) -> p a n", a=3)).then_inc(cst_ready, 1)
                dve.tensor_copy(head_ones[:], cst[:, 3 * P:4 * P]).then_inc(cst_ready, 1)
                dve.tensor_copy(alibi_b[:], cst[:, 4 * P:].rearrange("p (a n) -> p a n", a=8)).then_inc(cst_ready, 1)
                dve.wait_ge(cst_ready, 4)
            nconv = 0
            for s in stages:
                if s == "attn":
                    attn(s)
                elif s.startswith("mem"):
                    mem(int(s[3]), s)
                elif s == "diff":
                    diff(s)
                elif s == "conf":
                    conf(s)
                elif s == "ssm":
                    ssm(s)
                elif s.startswith("ffn"):
                    ffn("ffn_in" + s[3], "ffn_out" + s[3], s, ("ffn_w" + s[3], "ffn_b" + s[3], nconv))
                    nconv += 1
                elif s.startswith("glu"):
                    ffn("glu_in" + s[3], "glu_out" + s[3], s, None)
                elif s == "final":
                    norm_recip()
                    for c in range(KD):
                        dve.scalar_tensor_tensor(xt[:, c, :], xt[:, c, :], col("norm_final", c), rstd[:],
                                                 ALU.mult, ALU.mult).then_inc(out_ready, 1)

        @block.scalar
        def _(act):
            nrm = [0]
            ffns = [0]
            def prepare_x(ready, k0, gain):
                def chunk(c, j, i):
                    ready(c)
                    if not isinstance(c, int) or k0 + c > 1:
                        act.wait_ge(x_acc, k0 + c - 1)
                    act.activation(sq[:, j % 2, :], row(xt, c), ACT.Square).then_inc(x_sq, 1)
                    act.activation(row(xh, c), row(xt, c), ACT.Copy, scale=col(gain, c)).then_inc(x_hi, 1)
                return chunk

            def half(s, slot, rounds):
                act.wait_ge(w_landed[slot], 16 * rounds)
                act.wait_ge(w_used, s + 1)
                act.activation(w_hi[:, slot, :], w_raw[:, slot, :], ACT.Copy).then_inc(w_half, 1)

            def next_half(st, j, i):
                for t in range(st.per):
                    o = st.slab0 + j * st.per + t + SLOTS
                    if isinstance(i, int) and o + 4 * st.per * i >= SLABS:
                        continue
                    half(o + 4 * st.per * i, o % SLOTS, o // SLOTS + 1 + i * st.per)

            def residual(st, gain):
                k0 = KD * nrm[0]

                def chunk(c, j, i):
                    act.wait_ge(bank_free, BANKS + st.chunk0 + c + 1)
                    next_half(st, j, i)
                    body(c, j, i)
                body = prepare_x(lambda c: None, k0, gain)
                each(act, KD, chunk, peel=KD if st.slab0 + st.chunks * st.per == SLABS else 0)

            def norm_root():
                nrm[0] += 1
                act.wait_ge(nrm_sum, nrm[0])
                act.activation(root, NORM_BANK[:], ACT.Sqrt, scale=1.0 / D, bias=eps[:, 0:1]).then_inc(nrm_root, 1)

            def attention(units, groups, peers=1, out=None):
                U = len(units)
                u0, t0, g0 = au[0], at[0], ag[0]
                ends = {last: (g, chunks) for g, (_, last, chunks) in enumerate(groups)}
                nch = len(groups[0][2])
                for s_ in range(U + 6):
                    for lag, do in out or ():
                        if s_ - lag in ends:
                            do(ends[s_ - lag][0])
                    if s_ < U:
                        u, cs = units[s_], slice(s_, s_ + 1)
                        act.wait_ge(a_max, u0 + s_ + 1)
                        if s_ >= PROBS:
                            act.wait_ge(a_turn, t0 + (s_ - PROBS) // peers + 1)
                        if u.sink is not None:
                            act.activation(a_stat[:, 3, cs], u.sink, ACT.Exp, bias=a_stat[:, 1, cs]).then_inc(a_aux, 1)
                        act.activation(a_prob_t[:, s_ % PROBS, 0:u.nk], score_bank(s_, peers)[:, 0:u.nk], ACT.Exp,
                                       bias=a_stat[:, 1, cs], scale=u.scale, accum_out=a_stat[:, 2, cs])\
                            .then_inc(a_exp, 1)
                        if u.rel is not None and s_ % NT == NT - 1 and u.rel + 4 < 8:
                            load_rel(u.rel + 4, u0 + s_ + 1)
                    r = s_ - (3 if peers == 1 else 2)
                    if 0 <= r < U and (r + 1) % peers == 0:
                        u, k = units[r], r // peers
                        act.wait_ge(a_turn, t0 + k + 1)
                        if k >= 2:
                            act.wait_ge(a_pv, t0 + k - 1)
                        act.activation(a_pt_t[:, k % 2, 0:u.nk], turned_bank(k, peers)[:, 0:u.nk], ACT.Copy)\
                            .then_inc(a_pt, 1)
                    if s_ - 4 in ends and out is None:
                        g, chunks = ends[s_ - 4]
                        last = groups[g][1]
                        act.wait_ge(a_pv, t0 + last // peers)
                        for ch in chunks:
                            act.activation(oh[:, ch, :], bank[5 + ch % 2][:], ACT.Copy).then_inc(a_oh, 1)
                au[0] += U
                at[0] += U // peers
                ag[0] += len(groups) * nch
            au, at, ag = [0], [0], [0]
            a_aux = sem("a_aux")
            vt = [0]

            def value(dst, v, vc, j, n):
                act.wait_ge(v_turned, v + 1)
                act.activation(dst[:, :, ds(vc * P, P)], bank[5 + j % 2][:, 0:n].rearrange("p (a n) -> p a n", n=P),
                               ACT.Copy).then_inc(v_ready, 1)

            def mem_kv(l, before):
                kv = ST[f"mem_kv{l}"]
                v0 = vt[0]
                vt[0] += KD
                act.wait_ge(w_used, SLOTS + before)
                act.dma_start(m_in[:], A["memt"]).then_inc(m_landed, 16)
                act.wait_ge(m_landed, 16 * kv_round(l))
                act.activation(m_hi[:], m_in[:], ACT.Copy).then_inc(m_half, 1)

                def chunk(c):
                    next_half(kv, c % 4, c // 4)
                    if c > KD:
                        value(m_v, v0 + c - KD - 1, c - KD - 1, (c - 1) % 4, M)
                    if c == 2 * KD - 1:
                        value(m_v, v0 + KD - 1, KD - 1, c % 4, M)
                return chunk

            def mem(l, s):
                q = ST[f"mem_q{l}"]
                norm_root()
                each(act, KD, lambda c, j, i: next_half(q, j, i))
                attention(*UNITS["mem"])
                residual(ST[f"mem_out{l}"], GAIN[nxt[s]])

            def diff(s):
                kv, q = ST["diff_kv"], ST["diff_q"]
                ang, turns = d_t[:, 0, :], d_t[:, 1, :]
                act.dma_start(pos_i, A["pos"].broadcast_to([P, S])).then_inc(tab_in, 16)
                act.dma_start(freq[:], A["freq"]).then_inc(tab_in, 16)
                act.dma_start(rot[:], A["rot"]).then_inc(tab_in, 16)
                act.dma_start(d_q[:, 0, 0:256], A["lam"].broadcast_to([P, 256])).then_inc(lam_in, 16)
                act.wait_ge(tab_red, 1)
                act.activation(sine[:], ang, ACT.Sin).then_inc(tab_sin, 1)
                act.activation(turns, ang, ACT.Sin, scale=0.5).then_inc(tab_sin, 1)
                act.wait_ge(lam_sum, 1)
                act.activation(lam_e[:, 2:4], lam_e[:, 0:2], ACT.Exp).then_inc(lam_exp, 1)
                v0 = vt[0]

                def key(c, j, i):
                    next_half(kv, j, i)
                    if isinstance(c, int) and c == 0:
                        norm_root()
                each(act, KD, key, peel=4)

                def chunk(c, j, i):
                    next_half(kv, j, i)
                    lagged(lambda c, j: value(d_v, v0 + c - KD, c - KD, j, S), 15)(c, j)
                each(act, 2 * KD, chunk, start=KD)
                vt[0] += KD
                act.wait_ge(w_used, SLOTS + kv.slab0 + 2 * KD)
                for c in range(KD):
                    act.activation(xh[:, c, :], xt[:, c, :], ACT.Copy, scale=col("norm_mix2_1", c)).then_inc(y_hi, 1)
                each(act, KD, lambda c, j, i: next_half(q, j, i))
                def square(g):
                    act.wait_ge(o_raw, g + 1)
                    act.activation(sq[:, g % 2, :], d_q[:, g, :], ACT.Square).then_inc(o_sq, 1)

                def upper(g):
                    act.wait_ge(o_new, g + 1)
                    act.activation(oh[:, g, :], d_q[:, g, :], ACT.Copy, scale=1.0 - LAMBDA_INIT)\
                        .then_inc(a_oh, 1)
                def memory(g):
                    if g == 0:
                        chunks.append(mem_kv(1, q.slab0 + KD))
                chunks = []
                attention(*UNITS["diff"], peers=2, out=((5, square), (6, memory)))
                chunk = chunks[0]
                act.wait_ge(o_sum, KD)
                act.activation(o_r[:], NORM_BANK[:, 0:NT * KD], ACT.Sqrt, scale=1.0 / P, bias=eps[:, 1:2]).then_inc(o_root, 1)
                for c in range(2 * KD):
                    chunk(c)
                    if c < KD:
                        upper(c)
                residual(ST["diff_out"], GAIN[nxt[s]])

            def ssm(s):
                st = ST["ssm_in"]
                norm_root()
                t = lambda n: s_dt[:, n, :]
                act.wait_ge(cst_ready, 4)
                act.activation(t(5)[:, 0:1], col("ssm_alog")[0:32], ACT.Exp).then_inc(s_e, 1)

                def taps(c, j, i):
                    act.wait_ge(bank_free, BANKS + st.chunk0 + c + 1)
                    if not (isinstance(c, int) and 1 <= c < 3):
                        next_half(st, j, i)
                    if isinstance(c, int) and c == 0:
                        act.wait_ge(s_e0, 1)
                        act.activation(t(1), t(1), ACT.Exp, scale=-1.0).then_inc(s_e, 1)
                        next_half(st, 1, 0)
                        next_half(st, 2, 0)
                        act.wait_ge(s_e0, 2)
                        for c in range(NT):
                            cs = slice(c * P, (c + 1) * P)
                            act.activation(t(1)[:, cs], s_acs[:, cs], ACT.Exp, scale=-1.0,
                                           bias=s_acs[:, (c + 1) * P - 1:(c + 1) * P]).then_inc(s_e, 1)
                        act.activation(s_acs_h[:], s_acs, ACT.Copy).then_inc(s_split, 1)
                        act.activation(s_one[:], ident[0:32, 0:32], ACT.Copy).then_inc(s_split, 1)
                        return
                    q = c - 1
                    y = s_ea[:, j % 2, :]
                    act.activation(y, s_pad[:, 3:S + 3], ACT.Identity, scale=col("ssm_cw", 4 * q + 3),
                                   bias=col("ssm_cb", q)).then_inc(s_tap, 1)
                    act.wait_ge(s_conv, 3 * q + 3)
                    act.activation(row(s_xbc, c - 1), y, ACT.Silu).then_inc(s_xbc_done, 1)

                def gate(c, j, i):
                    act.wait_ge(bank_free, BANKS + st.chunk0 + c + 1)
                    next_half(st, j, i)
                    z = row(s_z, c - 25)
                    act.activation(z, z, ACT.Silu).then_inc(s_zd, 1)
                each(act, 25, taps, peel=4)
                each(act, 41, gate, start=25, peel=3)
                act.wait_ge(s_tp, 1)
                act.activation(s_el[:].rearrange("p a n -> p (a n)"), bank[4][:, 3 * P:4 * P], ACT.Exp).then_inc(s_eld, 1)

                def copied(g, r):
                    act.wait_ge(s_turn, 5 * g + r + 1)
                    if r < 4:
                        if g >= 2 and r == 0:
                            act.wait_ge(s_y, 8 * (g - 1))
                        dst = s_xt[:, g % 2, :, r * P:(r + 1) * P]
                    else:
                        act.wait_ge(s_cbp, g + 1)
                        dst = s_xbc[:, g:g + 1, :].rearrange("p a (b n) -> p (a b) n", n=P)
                    act.activation(dst, bank[5 + r % 2][:].rearrange("p (a n) -> p a n", n=P), ACT.Copy)\
                        .then_inc(s_copied, 1)
                for r in range(5):
                    copied(0, r)
                for n in range(SSMH + 14 + 4):
                    if n < SSMH:
                        act.wait_ge(s_bc, n + 1)
                        if n >= 3:
                            act.wait_ge(s_y, n - 2)
                        act.activation(s_ea[:, n % 3, :], bank[n % 2][:], ACT.Exp).then_inc(s_exp, 1)
                    k = n - 1
                    if 0 <= k < SSMH:
                        act.wait_ge(s_mask, k + 1)
                        if k >= 3:
                            act.wait_ge(s_y, k - 2)
                        for t in range(NT):
                            cs = slice(t * P, (t + 1) * P)
                            ins = act.activation(s_dk[:, k % 3, cs], bank[k % 2][:, cs], ACT.Exp,
                                                 bias=s_tok[:, 1, t, k:k + 1])
                        ins.then_inc(s_dec, 1)
                    g, r = n // 8, n % 8 - 1
                    if g + 1 < NGRP and 0 <= r < 5:
                        copied(g + 1, r)
                    f = (n - 5) // 2
                    if n % 2 == 1 and 0 <= f < KI:
                        act.wait_ge(s_yz, f + 1)
                        if f >= 2:
                            act.wait_ge(s_sum, f - 1)
                        act.activation(sq[:, f % 2, :], s_xbc[:, 8 + f, :], ACT.Square).then_inc(s_sq, 1)
                    for g in range(NGRP):
                        if n == 13 + 8 * g:
                            act.wait_ge(s_sum, 4 * g + 4)
                            if g:
                                act.wait_ge(s_yn, 4 * g)
                            act.activation(rstd[:], NORM_BANK[:], ACT.Sqrt, scale=4.0 / DIN, bias=eps[:, 0:1])\
                                .then_inc(s_root, 1)
                        q = n - 16 - 8 * g
                        if 0 <= q < 4:
                            f = 4 * g + q
                            act.wait_ge(s_yn, f + 1)
                            act.activation(yh[:, f, :], s_xbc[:, 8 + f, :], ACT.Copy).then_inc(s_yh, 1)
                residual(ST["ssm_out"], GAIN[nxt[s]])

            def conf(s):
                st = ST["pw1"]
                norm_root()

                def diag(p, q):
                    act.wait_ge(c_pe, p + 1)
                    for n in range(CPE):
                        act.activation(c_diag[:, q, n, :], ident[:], ACT.Copy,
                                       scale=col("dw_w", CONVW * p + n)).then_inc(c_dia, 1)

                def turn(i):
                    for j in range(4):
                        next_half(st, j, i)
                    for q in range(2):
                        p = 2 * i + q
                        act.wait_ge(bank_free, BANKS + st.chunk0 + 2 * p + 2)
                        act.activation(c_g[:, q, :], c_g[:, q, :], ACT.Sigmoid, bias=col("pw1_b", 2 * p + 1))\
                            .then_inc(c_sig, 1)
                    for q in range(2):
                        diag(2 * i + q, q)
                turn(0)
                with act.Fori(1, KD // 2) as i:
                    turn(i)
                chunk = mem_kv(0, st.slab0 + 2 * KD)
                for c in range(4):
                    chunk(c)
                act.wait_ge(c_msum, 1)
                act.activation(c_mean[:], NORM_BANK[:], ACT.Copy, scale=1.0 / D).then_inc(c_mrow, 1)
                for c in range(KD):
                    act.wait_ge(c_cent, c + 1)
                    if c >= 2:
                        act.wait_ge(c_cacc, c - 1)
                    act.activation(sq[:, c % 2, :], c_y[:, c, :], ACT.Square).then_inc(c_csq, 1)
                    if c % 2:
                        chunk(4 + c // 2)
                act.wait_ge(c_msum, 2)
                act.activation(c_mean[:], NORM_BANK[:], ACT.Sqrt, scale=1.0 / D, bias=eps[:, 1:2]).then_inc(c_mrow, 1)
                for c in range(KD):
                    act.wait_ge(c_norm, c + 1)
                    if c >= 2:
                        act.wait_ge(a_ol, ag[0] + c - 1)
                    act.activation(c_s[:, c % 2, :], c_y[:, c, :], ACT.Silu, scale=col("ln_g", c), bias=col("ln_b", c))\
                        .then_inc(c_silu, 1)
                    act.wait_ge(c_silu, c + 1)
                    act.activation(oh[:, c, :], c_s[:, c % 2, :], ACT.Copy).then_inc(a_oh, 1)
                    chunk(KD + c)
                ag[0] += KD
                residual(ST["pw2"], GAIN[nxt[s]])

            def load_rel(h, after):
                if after is not None:
                    act.wait_ge(a_score, after)
                src = bass.AP(rel_dram, h * 767, [[1, P], [1, 640]])
                act.dma_start(rel[:, h % 4, :], src).then_inc(rel_buf[h % 4], 16)

            def attn(s):
                st = ST["attn_in"]
                norm_root()
                act.wait_ge(rel_ready, 1)
                act.dma_start(rel_dram[:, :], rel_row[:]).then_inc(rel_out, 16)

                def fin(c, j):
                    if isinstance(c, int) and c >= 13:
                        v = c - 13
                        act.wait_ge(v_turned, v + 1)
                        dst = v_tok[:, :, 512:640] if v == 0 else v_tok[:, :, (v - 1) * P:v * P]
                        act.activation(dst, bank[5 + c % 2][:].rearrange("p (a n) -> p a n", a=NT), ACT.Copy)\
                            .then_inc(v_ready, 1)
                        return
                    act.wait_ge(q_sum, c + 1)
                    if not isinstance(c, int) or c >= 2:
                        act.wait_ge(q_ready, c - 1)
                    act.activation(q_root_t[:, j % 2, :], bank[5 + j % 2][:], ACT.Sqrt, scale=1.0 / 64,
                                   bias=eps[:, 0:1]).then_inc(q_root, 1)

                def chunk(c, j, i):
                    if j >= 1:
                        fin(c - 1, j - 1)
                    act.wait_ge(bank_free, BANKS + st.chunk0 + c + 1)
                    if not (isinstance(c, int) and c >= 13):
                        if not isinstance(c, int) or c >= 2:
                            act.wait_ge(q_sum, c - 1)
                        act.activation(sq[:, j % 2, :], row(qk, c),
                                       ACT.Square).then_inc(q_sq, 1)
                    next_half(st, j, i)
                    if j == 3 or (isinstance(c, int) and c == 17):
                        fin(c, j)
                each(act, 18, chunk, peel=4, tail=6)
                vt[0] += 5
                act.wait_ge(rel_out, 16)
                act.wait_ge(sink_in, 16)
                for h in range(4):
                    load_rel(h, None)
                attention(*UNITS["attn"])
                residual(ST["attn_out"], GAIN[nxt[s]])

            def ffn(si, so, s, conv):
                norm_root()
                f0 = ffns[0]
                ffns[0] += KF
                with act.Fori(0, KF // 2) as i:
                    for jj in range(2):
                        p = i * 2 + jj
                        act.wait_ge(bank_free, BANKS + ST[si].chunk0 + 2 * p + 1)
                        next_half(ST[si], 2 * jj, i)
                        if conv:
                            act.activation(f_y[:], f_g[:, 2:S + 2], ACT.Identity, bias=col(conv[1], p),
                                           scale=col(conv[0], 3 * p + 2)).then_inc(f_tap, 1)
                            act.wait_ge(f_conv, conv[2] * 2 * KF + 2 * p + 2)
                            act.activation(f_y[:], f_y[:], ACT.Silu).then_inc(f_silu, 1)
                        else:
                            act.activation(f_y[:], f_g[:, 2:S + 2], ACT.Silu).then_inc(f_silu, 1)
                        act.wait_ge(f_prod, f0 + p + 1)
                        act.activation(row(hh, p), f_h[:], ACT.Copy)\
                            .then_inc(f_hi, 1)
                        next_half(ST[si], 2 * jj + 1, i)
                residual(ST[so], GAIN[nxt[s]])

            act.dma_start(cols[:, 0:KD], A["cols"][:, 0:KD]).then_inc(const_first, 16)
            for c in range(KD):
                act.dma_start(xt[:, c, :], A["xt"][c]).then_inc(x_in[c], 16)
            act.dma_start(cols[:, KD:], A["cols"][:, KD:]).then_inc(const_in, 16)
            if set(stages) & {"attn", "diff", "ssm"}:
                act.dma_start(cst[:], A["cst"]).then_inc(cst_in, 16)
            if "attn" in stages:
                act.dma_start(rel_row[:, 383:767], A["rel_rev"][:, 0:384]).then_inc(rel_in, 16)
                act.dma_start(sink_c[:], A["sinks"].rearrange("(a n) -> a n", a=1).broadcast_to([P, 8]))\
                    .then_inc(sink_in, 16)
            act.wait_ge(const_first, 16)
            half(0, 0, 1)
            each(act, KD, prepare_x(lambda c: act.wait_ge(x_in[c], 16), 0, GAIN[stages[0]]), peel=KD)
            for t in range(1, min(SLOTS, SLABS)):
                half(t, t, 1)
            act.wait_ge(const_in, 16)
            k = 0
            for s in stages:
                if s == "attn":
                    attn(s)
                elif s.startswith("mem"):
                    mem(int(s[3]), s)
                elif s == "diff":
                    diff(s)
                elif s == "conf":
                    conf(s)
                elif s == "ssm":
                    ssm(s)
                elif s.startswith("ffn"):
                    ffn("ffn_in" + s[3], "ffn_out" + s[3], s, ("ffn_w" + s[3], "ffn_b" + s[3], k))
                    k += 1
                elif s.startswith("glu"):
                    ffn("glu_in" + s[3], "glu_out" + s[3], s, None)
                elif s == "final":
                    norm_root()
                    for c in range(KD):
                        act.wait_ge(out_ready, c + 1)
                        act.dma_start(out[c], xt[:, c, :]).then_inc(out_done, 16)
                    act.wait_ge(out_done, 16 * KD)


def pack(w):
    k, n = w.shape
    return np.ascontiguousarray(w.reshape(k // P, P, n // P, P).transpose(2, 1, 0, 3)).reshape(n // P, P, k)


def fcol(v):
    return np.ascontiguousarray(np.asarray(v).reshape(-1, P).T)


def interleave(w, half):
    k = w.shape[0]
    return np.ascontiguousarray(w.reshape(k, 2, half // P, P).transpose(0, 2, 1, 3)).reshape(k, 2 * half)


EXTRA = {"ssm": ("cst",), "attn": ("cst", "rel_rev", "sinks"), "conf": ("memt",), "diff": ("memt", "cst", "pos", "freq", "rot", "lam")}


def constants():
    p, m = np.arange(P)[:, None], np.arange(P)[None, :]
    chunk = np.where((p < 64) & (m >= 64), MASKED, 0.0)
    causal = np.where(m > p, MASKED, 0.0)
    decay = np.where(m < p, MASKED, 0.0)
    heads = (p // 64 == m // 64) * 1.0
    m = np.arange(256)[None, :]
    gone = ((p < 64) & (m >= 192)) | ((p >= 64) & (m < 64))
    alibi = [np.where(gone, MASKED, -8.0 * 2.0 ** -(h + 1) * np.abs(p - m + P)) for h in range(8)]
    return np.concatenate([chunk, causal, decay, heads] + alibi, 1).astype(np.float32)


def rotary():
    freq = np.zeros((P, 1), np.float32)
    rot = np.zeros((P, P), np.float32)
    for base in (0, 64):
        for i in range(8):
            freq[base + i] = freq[base + 8 + i] = 500000.0 ** (-i / 8)
            rot[base + 8 + i, base + i] = -1.0
            rot[base + i, base + 8 + i] = 1.0
    return freq, rot


def attn_in_cols(w):
    qa, ka, va, qb, kb, vb = np.split(w, [512, 1024, 1536, 2048, 2176], axis=1)
    qb = qb.reshape(-1, 2, 4, 64).transpose(0, 2, 1, 3).reshape(-1, 512)
    return np.concatenate([qa, ka, qb, kb, vb, va], 1)


def layout(I):
    A = {}
    A["cst"] = constants()
    A["rel_rev"] = np.ascontiguousarray(I["relpos_table"][0][:, ::-1])
    A["sinks"] = np.ascontiguousarray(I["sinks"][0])
    A["w_attn_in"] = pack(attn_in_cols(I["attn_w_in"][0]))
    wo = I["attn_w_out"][0]
    A["w_attn_out"] = pack(np.concatenate(
        [wo[:512], wo[512:].reshape(2, 4, 64, D).transpose(1, 0, 2, 3).reshape(512, D)], 0))
    A["xt"] = np.ascontiguousarray(np.asarray(I["x"])[0].T).reshape(KD, P, S)
    A["memt"] = np.ascontiguousarray(np.asarray(I["mem_2"])[0].T.reshape(KD, P, M).transpose(1, 0, 2))
    for l in range(2):
        A[f"w_mem_kv{l}"] = pack(np.concatenate([I["mem_w_k_2"][l], I["mem_w_v_2"][l]], 1))
        A[f"w_mem_q{l}"] = pack(I["mem_w_q_2"][l])
        A[f"w_mem_out{l}"] = pack(I["mem_w_o_2"][l])
    A["w_diff_kv"] = pack(np.concatenate([I["w_k_shared_2"], I["w_v_shared_2"]], 1))
    A["w_diff_q"] = pack(I["diff_w_q_2"][0])
    A["w_diff_out"] = pack(I["diff_w_o_2"][0])
    A["pos"] = np.ascontiguousarray(I["positions_2"])
    A["lam"] = np.stack([I["diff_lambda_q1_2"][0], I["diff_lambda_k1_2"][0], I["diff_lambda_q2_2"][0],
                         I["diff_lambda_k2_2"][0]]).reshape(1, 256)
    A["freq"], A["rot"] = rotary()
    A["w_pw1"] = pack(interleave(I["conv_w_pw1_2"][0], D))
    A["w_pw2"] = pack(I["conv_w_pw2_2"][0])
    z, xs, bc, dt = np.split(I["ssm_w_in"][0], [DIN, 2 * DIN, 2 * DIN + 2 * NGRP * NSTATE], axis=1)
    A["w_ssm_in"] = pack(np.concatenate([dt, np.zeros((D, P - SSMH), np.float32), bc, xs, z], 1))
    A["w_ssm_out"] = pack(I["ssm_w_out"][0])
    c = {}
    turned = lambda a: np.concatenate([a[..., DIN:], a[..., :DIN]], -1)
    c["ssm_cw"] = np.ascontiguousarray(turned(I["ssm_conv_w"][0]).reshape(4, 24, P).transpose(2, 1, 0)).reshape(P, -1)
    c["ssm_cb"] = fcol(turned(I["ssm_conv_b"][0]))
    c["ssm_d"] = fcol(np.repeat(I["ssm_d"][0], 64))
    c["ssm_norm"] = fcol(I["ssm_norm"][0])
    on_heads = lambda v: np.concatenate([v, np.zeros(P - SSMH, np.float32)])[:, None]
    c["ssm_dtb"] = on_heads(I["ssm_dt_bias"][0])
    c["ssm_alog"] = on_heads(I["ssm_a_log"][0])
    c["pw1_b"] = fcol(I["conv_b_pw1_2"][0].reshape(2, KD, P).transpose(1, 0, 2).reshape(-1))
    c["dw_w"] = np.ascontiguousarray(I["conv_w_dw_2"][0].reshape(CONVW, KD, P).transpose(2, 1, 0)).reshape(P, -1)
    c["dw_b"] = fcol(I["conv_b_dw_2"][0])
    c["ln_g"] = fcol(I["conv_ln_g_2"][0])
    c["ln_b"] = fcol(I["conv_ln_b_2"][0])
    c["pw2_b"] = fcol(I["conv_b_pw2_2"][0])
    c["subln"] = fcol(I["diff_subln_g_2"][0])
    pair = lambda v: np.concatenate([v, v])[:, None]
    c["g_qk"] = np.concatenate([pair(I["q_norm_a"][0])] * 4 + [pair(I["k_norm_a"][0])] * 4
                               + [pair(I["q_norm_b"][0])] * 4 + [pair(I["k_norm_b"][0])], 1)
    for l in range(2):
        c[f"norm_mix{l}"] = fcol(I["norm_mix"][l])
        c[f"norm_ffn{l}"] = fcol(I["norm_ffn"][l])
        A[f"w_ffn_in{l}"] = pack(interleave(I["ffn_w_in"][l], DFF))
        A[f"w_ffn_out{l}"] = pack(I["ffn_w_out"][l])
        c[f"ffn_w{l}"] = np.ascontiguousarray(I["ffn_conv_w"][l].reshape(3, KF, P).transpose(2, 1, 0)).reshape(P, -1)
        c[f"ffn_b{l}"] = fcol(I["ffn_conv_b"][l])
        c[f"norm_mix2_{l}"] = fcol(I["norm_mix_2"][l])
        c[f"norm_mem2_{l}"] = fcol(I["norm_mem_2"][l])
        c[f"norm_ffn2_{l}"] = fcol(I["norm_ffn_2"][l])
        A[f"w_glu_in{l}"] = pack(interleave(np.concatenate([I["ffn_w_gate_2"][l], I["ffn_w_up_2"][l]], 1), DFF))
        A[f"w_glu_out{l}"] = pack(I["ffn_w_down_2"][l])
    c["norm_final"] = fcol(I["norm_final_2"])
    c["kv_norm"] = fcol(I["kv_norm_2"])
    full = np.zeros((P, NCOL), np.float32)
    for name, n in COLUMNS:
        if name in c:
            full[:, COL[name]:COL[name] + n] = c[name]
    A["cols"] = full
    return A


def kernel(**inputs):
    import concourse.bacc as bacc
    from concourse.bass_utils import run_bass_kernel_spmd

    A = layout({name: np.asarray(value) for name, value in inputs.items()})
    nc = bacc.Bacc("TRN2", target_bir_lowering=False, num_devices=1)
    args = {name: nc.dram_tensor(name, a.shape, mybir.dt.from_np(a.dtype), kind="ExternalInput").ap()
            for name, a in A.items()}
    out = nc.dram_tensor("out", (KD, P, S), F32, kind="ExternalOutput").ap()
    build(nc, args, out)
    result = run_bass_kernel_spmd(nc, [A], core_ids=[0])
    return np.ascontiguousarray(result.results[0]["out"].reshape(D, S).T)[None]
```
